# Optimizing a Trainium2 kernel written in Bass

```python
import jax, jax.numpy as jnp
from jax import lax
import numpy as np

D_MODEL = 1024
BATCH = 1
SEQ = 512
DEPTH = 1
DEC_BATCH = 8
DEC_SEQ = 16
PAST_LEN = 512

CHUNK = 64
N_MEM = 256
EPS = 1e-6
GDN_HEADS = 4
GDN_DK = 128
GDN_DV = 128
GDN_CONV = 4
GDN_QK = GDN_HEADS * GDN_DK
GDN_V = GDN_HEADS * GDN_DV
GDN_CONV_DIM = 2 * GDN_QK + GDN_V
SC_DIM = 256
SC_GROUPS = 4
SC_CONV = 3
SB_HEADS = 4
SB_DH = 64
SB_W = SB_HEADS * SB_DH
SB_BLOCK = 128
D_MIX = GDN_V + SC_DIM + SB_W
IN_SIZES = (GDN_QK, GDN_QK, GDN_V, GDN_V, GDN_HEADS, GDN_HEADS,
            SC_DIM, SC_DIM, SC_DIM, SB_W, SB_W, SB_W)
D_IN = 2 * GDN_QK + 2 * GDN_V + 2 * GDN_HEADS + 3 * SC_DIM + 3 * SB_W
MEM_HEADS = 4
MEM_DH = 128
MEM_W = MEM_HEADS * MEM_DH
D_FF = 2816
FFN_CONV = 3

kernel_name = "hybrid_streaming_encoder_step"

F32 = jnp.float32

def rmsnorm(x, g):
    xf = x.astype(F32)
    y = xf * lax.rsqrt(jnp.mean(xf * xf, axis=-1, keepdims=True) + EPS)
    return (y * g.astype(F32)).astype(x.dtype)

def group_rmsnorm(y, n_groups, g):
    B, T, C = y.shape
    yf = y.astype(F32).reshape(B, T, n_groups, C // n_groups)
    yf = yf * lax.rsqrt(jnp.mean(yf * yf, axis=-1, keepdims=True) + EPS)
    return yf.reshape(B, T, C) * g.astype(F32)

def l2norm(x):
    return x * lax.rsqrt(jnp.sum(x * x, axis=-1, keepdims=True) + EPS)

def causal_dwconv(x, buf, w):
    W = w.shape[0]
    T = x.shape[1]
    xp = jnp.concatenate([buf.astype(x.dtype), x], axis=1)
    y = xp[:, 0:T] * w[0]
    for i in range(1, W):
        y = y + xp[:, i:i + T] * w[i]
    return y, xp[:, T:]

def split_cols(p):
    out, start = [], 0
    for s in IN_SIZES:
        out.append(p[..., start:start + s])
        start += s
    return out

def to_heads(a, d):
    B, T, _ = a.shape
    return a.reshape(B, T, -1, d).transpose(0, 2, 1, 3)

def gdn_chunk(S, q, k, v, g, beta):
    T = q.shape[2]
    gc = jnp.cumsum(g, axis=-1)
    idx = jnp.arange(T)
    causal = idx[:, None] >= idx[None, :]
    strict = idx[:, None] > idx[None, :]
    diff = gc[..., :, None] - gc[..., None, :]
    decay = jnp.exp(jnp.where(causal, diff, -jnp.inf))
    kk = jnp.einsum('bhtd,bhsd->bhts', k, k)
    L = jnp.where(strict, beta[..., None] * kk * decay, 0.0)
    A = L + jnp.eye(T, dtype=L.dtype)
    rhs = jnp.concatenate([v * beta[..., None],
                           k * (beta * jnp.exp(gc))[..., None]], axis=-1)
    sol = lax.linalg.triangular_solve(A, rhs, left_side=True, lower=True,
                                      unit_diagonal=True)
    u, w = sol[..., :GDN_DV], sol[..., GDN_DV:]
    v_new = u - jnp.einsum('bhtk,bhkv->bhtv', w, S)
    qk = jnp.einsum('bhtd,bhsd->bhts', q, k) * decay
    o = (jnp.einsum('bhtk,bhkv->bhtv', q * jnp.exp(gc)[..., None], S)
         + jnp.einsum('bhts,bhsv->bhtv', qk, v_new))
    g_last = gc[..., -1]
    S_new = (S * jnp.exp(g_last)[..., None, None]
             + jnp.einsum('bhtk,bhtv->bhkv',
                          k * jnp.exp(g_last[..., None] - gc)[..., None], v_new))
    return S_new, o

def gdn_prompt(q, k, v, g, beta):
    B, H, T, _ = q.shape
    nc = T // CHUNK

    def split(a):
        return jnp.moveaxis(a.reshape(a.shape[:2] + (nc, CHUNK) + a.shape[3:]), 2, 0)

    S0 = jnp.zeros((B, H, GDN_DK, GDN_DV), F32)
    S, o = lax.scan(lambda S, xs: gdn_chunk(S, *xs), S0,
                    (split(q), split(k), split(v), split(g), split(beta)))
    o = jnp.moveaxis(o, 0, 2).reshape(B, H, T, GDN_DV)
    return o, S

def stick_breaking(q, k, v, q_pos, k_pos):
    z = jnp.einsum('bhtd,bhsd->bhts', q.astype(F32), k.astype(F32)) * (SB_DH ** -0.5)
    strict = k_pos[None, :] < q_pos[:, None]
    log_1mb = jnp.where(strict, jax.nn.log_sigmoid(-z), 0.0)
    rc = lax.cumsum(log_1mb, axis=3, reverse=True) - log_1mb
    logA = jnp.where(strict, jax.nn.log_sigmoid(z) + rc, -jnp.inf)
    return jnp.einsum('bhts,bhsd->bhtd', jnp.exp(logA), v.astype(F32))

def sb_prompt(q, k, v):
    B, H, T, D = q.shape
    nb = T // SB_BLOCK
    qb = jnp.moveaxis(q.reshape(B, H, nb, SB_BLOCK, D), 2, 0)
    pos_b = jnp.arange(T, dtype=jnp.int32).reshape(nb, SB_BLOCK)
    k_pos = jnp.arange(T, dtype=jnp.int32)
    o = lax.map(lambda xs: stick_breaking(xs[0], k, v, xs[1], k_pos), (qb, pos_b))
    return jnp.moveaxis(o, 0, 2).reshape(B, H, T, D)

def memory_kv(mem, mem_in_norm_g, w_mk, w_mv, mk_norm_g):
    B, N, _ = mem.shape
    m = rmsnorm(mem, mem_in_norm_g)
    k = rmsnorm((m @ w_mk).reshape(B, N, MEM_HEADS, MEM_DH), mk_norm_g)
    v = (m @ w_mv).reshape(B, N, MEM_HEADS, MEM_DH)
    return k, v

def hybrid_layer(x, mem_k, mem_v, gdn_S, gdn_buf, sc_buf, sb_past_k, sb_past_v, ffn_buf, lw):
    (norm_mix_g, w_in, gdn_conv_w, gdn_A_log, gdn_dt_bias, gdn_norm_g,
     sc_conv_w, sc_norm_g, sb_norm_g, w_mix_out,
     norm_mem_g, w_mq, mq_norm_g, w_mo,
     norm_ffn_g, w_gate, w_up, ffn_conv_w, w_down) = lw
    B, T, _ = x.shape
    dt = x.dtype

    h = rmsnorm(x, norm_mix_g)
    gq, gk, gv, gz, gb, ga, sB, sC, sx, cq, ck, cv = split_cols(h @ w_in)

    qkv, gdn_buf_new = causal_dwconv(jnp.concatenate([gq, gk, gv], axis=-1), gdn_buf, gdn_conv_w)
    qkv = jax.nn.silu(qkv.astype(F32))
    q = l2norm(to_heads(qkv[..., :GDN_QK], GDN_DK)) * (GDN_DK ** -0.5)
    k = l2norm(to_heads(qkv[..., GDN_QK:2 * GDN_QK], GDN_DK))
    v = to_heads(qkv[..., 2 * GDN_QK:], GDN_DV)
    beta = jax.nn.sigmoid(gb.astype(F32)).transpose(0, 2, 1)
    g = (-jnp.exp(gdn_A_log.astype(F32))
         * jax.nn.softplus(ga.astype(F32) + gdn_dt_bias.astype(F32))).transpose(0, 2, 1)
    if gdn_S is None:
        o_a, S_new = gdn_prompt(q, k, v, g, beta)
    else:
        S_new, o_a = gdn_chunk(gdn_S.astype(F32), q, k, v, g, beta)
    o_a = o_a.transpose(0, 2, 1, 3)
    zh = gz.reshape(B, T, GDN_HEADS, GDN_DV).astype(F32)
    y_a = (rmsnorm(o_a, gdn_norm_g) * jax.nn.silu(zh)).reshape(B, T, GDN_V).astype(dt)

    u, sc_buf_new = causal_dwconv(sC * sx, sc_buf, sc_conv_w)
    y_b = group_rmsnorm(sB * u, SC_GROUPS, sc_norm_g).astype(dt)

    qc, kc, vc = to_heads(cq, SB_DH), to_heads(ck, SB_DH), to_heads(cv, SB_DH)
    if sb_past_k is None:
        o_c = sb_prompt(qc, kc, vc)
    else:
        P = sb_past_k.shape[1]
        k_all = jnp.concatenate([sb_past_k.astype(dt).transpose(0, 2, 1, 3), kc], axis=2)
        v_all = jnp.concatenate([sb_past_v.astype(dt).transpose(0, 2, 1, 3), vc], axis=2)
        q_pos = P + jnp.arange(T, dtype=jnp.int32)
        k_pos = jnp.arange(P + T, dtype=jnp.int32)
        o_c = stick_breaking(qc, k_all, v_all, q_pos, k_pos)
    y_c = group_rmsnorm(o_c.transpose(0, 2, 1, 3).reshape(B, T, SB_W), SB_HEADS, sb_norm_g).astype(dt)
    sb_k_new = ck.reshape(B, T, SB_HEADS, SB_DH)
    sb_v_new = cv.reshape(B, T, SB_HEADS, SB_DH)

    x = x + jnp.concatenate([y_a, y_b, y_c], axis=-1) @ w_mix_out

    h = rmsnorm(x, norm_mem_g)
    qm = rmsnorm((h @ w_mq).reshape(B, T, MEM_HEADS, MEM_DH), mq_norm_g)
    s = jnp.einsum('bthd,bnhd->bhtn', qm.astype(F32), mem_k.astype(F32)) * (MEM_DH ** -0.5)
    p = jax.nn.softmax(s, axis=-1)
    om = jnp.einsum('bhtn,bnhd->bthd', p, mem_v.astype(F32)).reshape(B, T, MEM_W).astype(dt)
    x = x + om @ w_mo

    h = rmsnorm(x, norm_ffn_g)
    gt, ffn_buf_new = causal_dwconv(h @ w_gate, ffn_buf, ffn_conv_w)
    x = x + (jax.nn.silu(gt) * (h @ w_up)) @ w_down

    return x, S_new, gdn_buf_new, sc_buf_new, sb_k_new, sb_v_new, ffn_buf_new

def setup_inputs(seed: int = 0) -> dict:
    key = jax.random.key(seed)
    ks = iter(jax.random.split(key, 48))

    def nrm(shape, scale=1.0):
        return jax.random.normal(next(ks), shape, F32) * scale

    def gain(shape):
        return 1.0 + 0.02 * jax.random.normal(next(ks), shape, F32)

    dt_init = jax.random.uniform(next(ks), (DEPTH, GDN_HEADS), F32, 0.001, 0.1)
    return {
        "x_prompt": nrm((BATCH, SEQ, D_MODEL)),
        "x_sample": nrm((DEC_BATCH, DEC_SEQ, D_MODEL)),
        "mem_prompt": nrm((BATCH, N_MEM, D_MODEL)),
        "state_gdn": nrm((DEPTH, DEC_BATCH, GDN_HEADS, GDN_DK, GDN_DV), 0.05),
        "cache_gdn_conv": nrm((DEPTH, DEC_BATCH, GDN_CONV - 1, GDN_CONV_DIM)),
        "cache_sc_conv": nrm((DEPTH, DEC_BATCH, SC_CONV - 1, SC_DIM)),
        "cache_sb_k": nrm((DEPTH, DEC_BATCH, PAST_LEN, SB_HEADS, SB_DH)),
        "cache_sb_v": nrm((DEPTH, DEC_BATCH, PAST_LEN, SB_HEADS, SB_DH)),
        "cache_mem_k": nrm((DEPTH, DEC_BATCH, N_MEM, MEM_HEADS, MEM_DH)),
        "cache_mem_v": nrm((DEPTH, DEC_BATCH, N_MEM, MEM_HEADS, MEM_DH)),
        "cache_ffn_conv": nrm((DEPTH, DEC_BATCH, FFN_CONV - 1, D_FF)),
        "norm_mix_g": gain((DEPTH, D_MODEL)),
        "w_in": nrm((DEPTH, D_MODEL, D_IN), D_MODEL ** -0.5),
        "gdn_conv_w": nrm((DEPTH, GDN_CONV, GDN_CONV_DIM), GDN_CONV ** -0.5),
        "gdn_A_log": jnp.log(jax.random.uniform(next(ks), (DEPTH, GDN_HEADS), F32, 1.0, 16.0)),
        "gdn_dt_bias": jnp.log(jnp.expm1(dt_init)),
        "gdn_norm_g": gain((DEPTH, GDN_DV)),
        "sc_conv_w": nrm((DEPTH, SC_CONV, SC_DIM), SC_CONV ** -0.5),
        "sc_norm_g": gain((DEPTH, SC_DIM)),
        "sb_norm_g": gain((DEPTH, SB_W)),
        "w_mix_out": nrm((DEPTH, D_MIX, D_MODEL), 0.5 * D_MIX ** -0.5),
        "norm_mem_g": gain((DEPTH, D_MODEL)),
        "mem_in_norm_g": gain((DEPTH, D_MODEL)),
        "w_mq": nrm((DEPTH, D_MODEL, MEM_W), D_MODEL ** -0.5),
        "w_mk": nrm((DEPTH, D_MODEL, MEM_W), D_MODEL ** -0.5),
        "w_mv": nrm((DEPTH, D_MODEL, MEM_W), D_MODEL ** -0.5),
        "mq_norm_g": gain((DEPTH, MEM_DH)),
        "mk_norm_g": gain((DEPTH, MEM_DH)),
        "w_mo": nrm((DEPTH, MEM_W, D_MODEL), 0.5 * MEM_W ** -0.5),
        "norm_ffn_g": gain((DEPTH, D_MODEL)),
        "w_gate": nrm((DEPTH, D_MODEL, D_FF), D_MODEL ** -0.5),
        "w_up": nrm((DEPTH, D_MODEL, D_FF), D_MODEL ** -0.5),
        "ffn_conv_w": nrm((DEPTH, FFN_CONV, D_FF), FFN_CONV ** -0.5),
        "w_down": nrm((DEPTH, D_FF, D_MODEL), 0.5 * D_FF ** -0.5),
    }

def reference(x_prompt, x_sample, mem_prompt, state_gdn, cache_gdn_conv, cache_sc_conv,
              cache_sb_k, cache_sb_v, cache_mem_k, cache_mem_v, cache_ffn_conv,
              norm_mix_g, w_in, gdn_conv_w, gdn_A_log, gdn_dt_bias, gdn_norm_g,
              sc_conv_w, sc_norm_g, sb_norm_g, w_mix_out,
              norm_mem_g, mem_in_norm_g, w_mq, w_mk, w_mv, mq_norm_g, mk_norm_g, w_mo,
              norm_ffn_g, w_gate, w_up, ffn_conv_w, w_down):
    xp, xs = x_prompt, x_sample
    Bp = xp.shape[0]
    P_S, P_GC, P_SC, P_K, P_V, P_MK, P_MV, P_FC = [], [], [], [], [], [], [], []
    S_S, S_GC, S_SC, S_K, S_V, S_FC = [], [], [], [], [], []
    for l in range(DEPTH):
        lw = (norm_mix_g[l], w_in[l], gdn_conv_w[l], gdn_A_log[l], gdn_dt_bias[l], gdn_norm_g[l],
              sc_conv_w[l], sc_norm_g[l], sb_norm_g[l], w_mix_out[l],
              norm_mem_g[l], w_mq[l], mq_norm_g[l], w_mo[l],
              norm_ffn_g[l], w_gate[l], w_up[l], ffn_conv_w[l], w_down[l])
        mk, mv = memory_kv(mem_prompt, mem_in_norm_g[l], w_mk[l], w_mv[l], mk_norm_g[l])
        xp, S_n, gc_n, sc_n, k_n, v_n, fc_n = hybrid_layer(
            xp, mk, mv, None,
            jnp.zeros((Bp, GDN_CONV - 1, GDN_CONV_DIM), xp.dtype),
            jnp.zeros((Bp, SC_CONV - 1, SC_DIM), xp.dtype),
            None, None,
            jnp.zeros((Bp, FFN_CONV - 1, D_FF), xp.dtype), lw)
        P_S.append(S_n); P_GC.append(gc_n); P_SC.append(sc_n); P_K.append(k_n)
        P_V.append(v_n); P_MK.append(mk); P_MV.append(mv); P_FC.append(fc_n)
        xs, S_n, gc_n, sc_n, k_n, v_n, fc_n = hybrid_layer(
            xs, cache_mem_k[l], cache_mem_v[l], state_gdn[l], cache_gdn_conv[l],
            cache_sc_conv[l], cache_sb_k[l], cache_sb_v[l], cache_ffn_conv[l], lw)
        S_S.append(S_n); S_GC.append(gc_n); S_SC.append(sc_n)
        S_K.append(k_n); S_V.append(v_n); S_FC.append(fc_n)
    return (xp, xs,
            jnp.stack(P_S), jnp.stack(P_GC), jnp.stack(P_SC), jnp.stack(P_K), jnp.stack(P_V),
            jnp.stack(P_MK), jnp.stack(P_MV), jnp.stack(P_FC),
            jnp.stack(S_S), jnp.stack(S_GC), jnp.stack(S_SC), jnp.stack(S_K), jnp.stack(S_V),
            jnp.stack(S_FC))


_drawn_inputs = setup_inputs


def setup_inputs(seed=0):
    import zlib

    import numpy as np

    out = dict(_drawn_inputs(seed))
    spreads = {}
    factors = {'gdn_norm_g': 8.0,
     'sc_norm_g': 8.0,
     'sb_norm_g': 8.0,
     'norm_mem_g': 8.0,
     'mem_in_norm_g': 2.812,
     'mq_norm_g': 8.0,
     'mk_norm_g': 3.016,
     'norm_ffn_g': 8.554}
    for name, (base, spread) in spreads.items():
        noise = np.random.default_rng([zlib.crc32(name.encode()), seed]).standard_normal(out[name].shape)
        drawn = base * np.exp(spread * noise) if base else spread * noise
        out[name] = __import__('jax').numpy.asarray(drawn.astype(out[name].dtype))
    for name, factor in factors.items():
        out[name] = (out[name] * factor).astype(out[name].dtype)
    return out
```

```python
import concourse.bass as bass
from concourse import mybir
from contextlib import ExitStack

F32 = mybir.dt.float32
F32R = mybir.dt.float32r
ALU = mybir.AluOpType
ACT = mybir.ActivationFunctionType
AX = mybir.AxisListType

P = 128
D_MODEL, SEQ, DEC_BATCH, DEC_SEQ, PAST_LEN = 1024, 512, 8, 16, 512
KD = D_MODEL // P
TOK = SEQ + DEC_BATCH * DEC_SEQ
PT = SEQ // P
NT = TOK // P
HALF = TOK // 2
N_MEM, EPS = 256, 1e-6
HEADS, DK = 4, 128
GDN_DIM = 3 * HEADS * DK
SC_DIM, SB_W, SB_DH = 256, 256, 64
D_IN = 3592
D_FF = 2816
FT = D_FF // P
GAB = 2048
SCOL = GAB + 2 * HEADS
CKCOL = SCOL + 3 * SC_DIM + SB_W
PAD = 3
NEG = -1.0e30
RING = 6
BLK = 2048
LEVELS = 7
SAMPLE_LEVELS = 4

ARENA = 16512
R0 = ARENA
R1 = R0 + NT * D_MODEL * 4
R2 = R1 + 2 * KD * TOK * 4
R3 = R2 + 6 * BLK * 4
R5 = R3 + FT * TOK * 4


def hybrid_step(nc, A, O):
    ctx = ExitStack()
    with ctx:
        at_r5 = [R5]

        def at(name, shape, offset, dt=F32):
            return nc.alloc_sbuf_tensor_at(name, shape, dt, offset=offset)

        def keep(name, shape, dt=F32):
            n = 4
            for s in shape[1:]:
                n *= s
            t = at(name, shape, at_r5[0], dt)
            at_r5[0] += (n + 31) // 32 * 32
            return t

        def sem(name):
            return ctx.enter_context(nc.semaphore(name))

        def spread(ap, axis, shape):
            return ap.unsqueeze(axis).to_broadcast(shape)

        xres = at("xres", [P, NT, D_MODEL], R0)
        mhi = at("mhi", [P, KD, N_MEM], R0, F32R)
        mlo = at("mlo", [P, KD, N_MEM], R0 + KD * N_MEM * 4, F32R)
        scr = [at(f"scr{n}", [P, HEADS, P], R0 + 2048 * n) for n in range(10)]
        att_a = [at(f"att_a{n}", [P, 640], R0 + 7712 * n) for n in range(2)]
        att_m = [at(f"att_m{n}", [P, 648], R0 + 7712 * n + 2560) for n in range(2)]
        att_t = [at(f"att_t{n}", [P, 640], R0 + 7712 * n + 5152) for n in range(2)]
        hhi = at("hhi", [P, KD, TOK], R1, F32R)
        hlo = at("hlo", [P, KD, TOK], R1 + KD * TOK * 4, F32R)
        junk_mk = at("junk_mk", [P, HEADS, P], R1 + 34816)
        kraw = [at(f"kraw{n}", [P, 4, 256], R1 + 4096 * n) for n in range(4)]
        vraw = [at(f"vraw{n}", [P, 4, 256], R1 + 16384 + 4096 * n) for n in range(4)]
        kTs = [at(f"kTs{n}", [P, 2, 512], R1 + 32768 + 4096 * n) for n in range(2)]
        XT = at("XT", [P, NT, HEADS, P], R1)
        qkD = at("qkD", [P, NT, HEADS, P], R1 + 10240)
        LT = at("LT", [P, NT, HEADS, P], R1 + 20480)
        XY = at("XY", [P, NT, HEADS, P], R1 + 30720)
        stS = at("stS", [P, DEC_BATCH, HEADS, P], R1 + 20480)
        stP = at("stP", [P, HEADS, P], R1 + 20480 + 16384)
        mkraw = [at(f"mkraw{n}", [P, 2, 512], R1 + 4096 * n) for n in range(DEC_BATCH)]
        kmT = [at(f"kmT{n}", [P, HEADS, N_MEM], R1 + 4096 * (DEC_BATCH + n)) for n in range(2)]
        mkout = at("mkout", [P, 2, 512], R1 + 36864)
        vmask = [at(f"vmask{n}", [P, DEC_BATCH, P], R0 + 4096 * n) for n in range(2)]
        sqG = [at(f"sqG{n}", [P, TOK], R0 + 2560 * n) for n in range(2)]
        rG = [at(f"rG{n}", [P, TOK], R0 + 5120 + 2560 * n) for n in range(2)]
        sqA = [at(f"sqA{n}", [P, TOK], R5 + 2560 * n) for n in range(2)]
        rA = [at(f"rA{n}", [P, TOK], R5 + 5120 + 2560 * n) for n in range(2)]
        gT = at("gT", [8, TOK], R5 + 5120)
        sqM = [at(f"sqM{n}", [P, TOK], R3 + 30720 + 2560 * n) for n in range(2)]
        rM = [at(f"rM{n}", [P, TOK], R3 + 35840 + 2560 * n) for n in range(2)]
        wraw = [at(f"wraw{n}", [P, BLK], R2 + BLK * 4 * n) for n in range(2)]
        whi = [at(f"whi{n}", [P, BLK], R2 + BLK * 4 * (2 + n), F32R) for n in range(2)]
        wlo = [at(f"wlo{n}", [P, BLK], R2 + BLK * 4 * (4 + n), F32R) for n in range(2)]
        qkvz = at("qkvz", [P, 16, TOK], R3)
        cq = at("cq", [P, 2, TOK], R3 + 16 * TOK * 4)
        yb = at("yb", [P, 2, TOK], R3 + 18 * TOK * 4)
        kT = at("kT", [P, 2, TOK], R3 + 20 * TOK * 4)
        scC = at("scC", [P, 2, TOK], R3 + 20 * TOK * 4)
        xin = [at(f"xin{n}", [P, D_MODEL], R3 + 4096 * n) for n in range(2)]
        xn = [at(f"xn{n}", [P, D_MODEL], R3 + 8192 + 4096 * n) for n in range(2)]
        junk = at("junk", [P, D_MODEL], R3 + 16384)
        gmix = at("gmix", [P, D_MODEL], R3 + 20480)
        gmin = at("gmin", [P, D_MODEL], R3 + 24576)
        crow = at("crow", [24, GDN_DIM], R3 + 28672)
        scrow = at("scrow", [16, SC_DIM], R3 + 28672 + 6144)
        qm = at("qm", [P, HEADS, TOK], R3)
        omhi = at("omhi", [P, HEADS, TOK], R3 + 10240, F32R)
        omlo = at("omlo", [P, HEADS, TOK], R3 + 20480, F32R)
        gmem = at("gmem", [P, D_MODEL], R3 + 30720)
        xn2 = [at(f"xn2{n}", [P, D_MODEL], R3 + 34816 + 4096 * n) for n in range(2)]
        junk2 = at("junk2", [P, D_MODEL], R3 + 43008)
        gffn = at("gffn", [P, D_MODEL], R3 + 47104)
        probs = [at(f"probs{n}", [P, HEADS, N_MEM], R3 + 30720 + 4096 * n) for n in range(2)]
        probT = [at(f"probT{n}", [P, HEADS, 2, P], R3 + 38912 + 4096 * n) for n in range(2)]
        stsb = at("stsb", [P, 2, HEADS, P], R3 + 51200)
        act = at("act", [P, FT, TOK], R3)
        ckv = keep("ckv", [P, NT, 512])
        yc = keep("yc", [P, 2, TOK])
        memkT = keep("memkT", [P, HEADS, N_MEM])
        memv = keep("memv", [P, 2, 512])
        cb = [keep(f"cb{n}", [P, 672]) for n in range(2)]
        xn3 = [at(f"xn3{n}", [P, D_MODEL], at_r5[0] - 2 * 2688 - 4096 * (2 - n)) for n in range(2)]
        junk3 = at("junk3", [P, D_MODEL], at_r5[0] - 2 * 2688)
        ident = keep("ident", [P, P])
        ones = keep("ones", [P, P])
        uptri = keep("uptri", [P, P])
        up16 = keep("up16", [P, P])
        same16 = keep("same16", [P, P])
        same64 = keep("same64", [P, P])
        lmask = keep("lmask", [P, LEVELS, P])
        negm = keep("negm", [P, P])
        newm = keep("newm", [P, 224])
        newi = keep("newi", [P, 224])
        own8 = keep("own8", [P, DEC_BATCH])
        w8raw = keep("w8raw", [P, KD, 8])
        w8hi = keep("w8hi", [P, KD, 8], F32R)
        w8lo = keep("w8lo", [P, KD, 8], F32R)
        gmk = keep("gmk", [P, DK])
        gcw = keep("gcw", [P, 12, 4])
        scw = keep("scw", [P, 2, 3])
        gout = keep("gout", [P, 8])
        gmq = keep("gmq", [P, 1])
        epsc = keep("epsc", [P, 1])
        lnsc = keep("lnsc", [P, 1])
        dtb = keep("dtb", [P, HEADS])
        nA = keep("nA", [P, HEADS])
        stat = keep("stat", [P, 3, 40])
        mstat = keep("mstat", [P, 4, NT, HEADS])
        gba = keep("gba", [P, NT, 8])
        beta = keep("beta", [P, NT, HEADS])
        gdec = keep("gdec", [P, NT, HEADS])
        gtmp = keep("gtmp", [P, 4, NT, HEADS])
        gcs = keep("gcs", [P, NT, 3, HEADS])
        kdec = keep("kdec", [P, NT, HEADS])
        bege = keep("bege", [P, NT, HEADS])
        etot = keep("etot", [P, NT, HEADS])
        etotS = keep("etotS", [P, HEADS, DEC_BATCH])
        cacheT = keep("cacheT", [P, 12, 24])
        cacheS = keep("cacheS", [P, 2, 16])
        cst = keep("cst", [P, 12, 27])
        scst = keep("scst", [P, 2, 18])
        qbl = at("qbl", [P, 2, DEC_BATCH, 32], R0 + 15456)
        fcw = at("fcw", [P, FT, 3], R5)
        cacheF = at("cacheF", [P, FT, 16], R5 + 288)
        fcst = at("fcst", [P, FT, 18], R5 + 1696)
        strow = at("strow", [27, GDN_DIM], R1 + 24576)
        scsrow = at("scsrow", [18, SC_DIM], R1 + 24576 + 6144)
        frow = at("frow", [16, D_FF], R5 + 3296)
        fsrow = at("fsrow", [18, D_FF], R5 + 3296)
        assert at_r5[0] <= 229344, at_r5[0]
        assert R5 + 3296 + D_FF * 4 <= R5 + 15360

        bank = [ctx.enter_context(nc.psum_tensor(f"bank{b}", [P, 512], F32)) for b in range(8)]
        bank_full = [sem(f"bank_full{b}") for b in range(8)]
        bank_free = [sem(f"bank_free{b}") for b in range(8)]
        w_loaded = [sem(f"w_loaded{n}") for n in range(2)]
        s = {n: sem(n) for n in (
            "consts", "small_loaded", "x_loaded0", "x_loaded1", "rstd_ready", "xn_ready", "h_hi_ready",
            "w_hi_ready", "w_lo_ready", "w8_ready", "kstep", "conv_done", "silu_done", "sq_ready", "rinv_ready",
            "l2_done", "gates", "gates_act", "rhs_ready", "dif_ready", "dt_ready", "dtu_ready", "small_exp",
            "lt_ready", "xt0_ready", "lm_ready", "kd_ready", "vc_loaded0", "vc_loaded1", "vc_loaded2", "vc_loaded3", "kc_loaded0", "kc_loaded1", "kc_loaded2",
            "kc_loaded3", "A_ready", "q_blocks", "st_loaded", "vm_ready", "sqf_ready", "rf_ready", "y_ready",
            "yhi_ready", "ylo_ready", "xres_loaded", "gm_loaded", "f_loaded", "qsq_ready", "qr_ready", "qm_ready",
            "max_ready", "prob_ready", *[f"mc_loaded{n}" for n in range(DEC_BATCH)], "om_hi", "ffn_conv", "ffn_silu", "ahi_ready",
            "alo_ready", "out_sb", "out_mk", "out_mv", "out_rows", "out_frows", "out_pstate", "out_sstate",
            "out_y", "dve_chain", "act_chain", "pool_chain")}

        def flat(t):
            return t[:, :, :].rearrange("p a b -> p (a b)")

        def quad(b):
            return bank[b][:, :].rearrange("p (a b) -> p a b", a=4)

        def conv_s(t):
            return t[:, PAD + SEQ:PAD + SEQ + DEC_BATCH * (PAD + DEC_SEQ)].rearrange("p (b t) -> p b t", b=DEC_BATCH)

        def tri(i):
            return uptri if i < PT else up16

        def mixed(f):
            return qkvz[:, f, :] if f < 4 else yb[:, f - 4, :] if f < 6 else yc[:, f - 6, :]

        def dest1(n, mem, x):
            return mem[:, :, n * P:(n + 1) * P] if n < 2 else x[:, :, (n - 2) * P:(n - 1) * P]

        def at_banks(n):
            return 1 if SB_ITEMS[n][0] == "p" else 2

        turns = [0] * 8
        use = {}
        ring_at = [0, 0]
        ksteps = [0]
        ends = {}

        def filled(eng, key):
            b, n = use[key]
            eng.wait_ge(bank_full[b], n)
            return b

        def evacuated(eng, key):
            b, n = use[key]
            eng.wait_ge(bank_free[b], n)

        def passed(eng, key):
            kind, what = ends[key]
            if kind == "bank":
                filled(eng, what)
            else:
                eng.wait_ge(s["kstep"], what)

        blocks = []

        def cols(w, c0, n=256):
            blocks.append((w[:, c0:c0 + n].rearrange("(k p) c -> p k c", p=P), KD, n))
            return len(blocks) - 1

        def rows(w, k0, nk, c0):
            blocks.append((w[k0 * P:(k0 + nk) * P, c0:c0 + 512].rearrange("(k p) c -> p k c", p=P), nk, 512))
            return len(blocks) - 1

        B_IN = [cols(A["w_in"], 256 * n) for n in range(8)] + [cols(A["w_in"], SCOL + 256 * n) for n in range(4)]
        B_CK = [rows(A["w_in"], k, 4, CKCOL) for k in (0, 4)]
        B_MK = [rows(A["w_mk"], k, 4, 0) for k in (0, 4)]
        B_MV = [rows(A["w_mv"], k, 4, 0) for k in (0, 4)]
        B_OUT = [[rows(A["w_mix_out"], k, 4, 512 * h) for k in (0, 4)] for h in range(2)]
        B_MQ = [cols(A["w_mq"], 256 * n) for n in range(2)]
        B_MO = [[rows(A["w_mo"], 0, 4, 512 * h)] for h in range(2)]
        B_GU = [(cols(A["w_gate"], 256 * n), cols(A["w_up"], 256 * n)) for n in range(FT // 2)]
        B_DN = [[rows(A["w_down"], k, min(4, FT - k), 512 * h) for k in range(0, FT, 4)] for h in range(2)]
        NB = len(blocks)

        def wv(t, i):
            _, nk, n = blocks[i]
            return t[i % 2][:, 0:nk * n].rearrange("p (k c) -> p k c", k=nk)

        small = [
            (crow[0:24, :], A["cache_gdn_conv"].rearrange("b t c -> (b t) c")),
            (scrow[0:16, :], A["cache_sc_conv"].rearrange("b t c -> (b t) c")),
            (gmin[:, :], A["mem_in_norm_g"].partition_broadcast(P)), (gmix[:, :], A["norm_mix_g"].partition_broadcast(P)),
            (gmk[:, :], A["mk_norm_g"].partition_broadcast(P)), (dtb[:, :], A["gdn_dt_bias"].partition_broadcast(P)),
            (nA[:, :], A["gdn_A_log"].partition_broadcast(P)),
            (w8raw[:, :, :], A["w_in"][:, GAB:GAB + 8].rearrange("(k p) c -> p k c", p=P)),
        ] + [(gout[:, 0:1], A["gdn_norm_g"].unsqueeze(1)), (gmq[:, :], A["mq_norm_g"].unsqueeze(1))]
        small_cols = [(gcw[:, :, k], A["gdn_conv_w"][k, :].rearrange("(j p) -> p j", p=P)) for k in range(4)]
        small_cols += [(scw[:, :, k], A["sc_conv_w"][k, :].rearrange("(j p) -> p j", p=P)) for k in range(3)]
        small_cols += [(gout[:, 4:6], A["sc_norm_g"].rearrange("(j p) -> p j", p=P)),
                       (gout[:, 6:8], A["sb_norm_g"].rearrange("(j p) -> p j", p=P))]
        NI = 20
        SMALL_LOADS = len(small) + len(small_cols)

        SB_ITEMS = [("p", h, i) for h in range(HEADS) for i in range(PT)] + [("s", p, None) for p in range(4)]
        TILES_AT = [list(range(NT)) if l < SAMPLE_LEVELS else list(range(PT)) for l in range(LEVELS)]
        LM_ORDER = [(l, i) for l in range(1, LEVELS) for i in TILES_AT[l]]

        block = ctx.enter_context(nc.Block())

        @block.tensor
        def _(pe):
            T = nc.tensor

            def take(key, long=False):
                if long:
                    b = RING + ring_at[1] % 2
                    ring_at[1] += 1
                else:
                    b = ring_at[0] % RING
                    ring_at[0] += 1
                turns[b] += 1
                use[key] = (b, turns[b])
                if turns[b] > 1:
                    pe.wait_ge(bank_free[b], turns[b] - 1)
                return b

            def done(ins, key):
                ins.then_inc(bank_full[use[key][0]], 1)

            def step(ins, key):
                ins.then_inc(s["kstep"], 1)
                ksteps[0] += 1
                ends[key] = ("k", ksteps[0])

            def across(name, i, hi, lo):
                pe.wait_ge(s["w_lo_ready"], i + 1)
                wh, wl = wv(whi, i), wv(wlo, i)
                for c in range(2):
                    keys = [(name, c, h) for h in range(2)]
                    bs = [take(k) for k in keys]
                    for k in range(KD):
                        for w, parts in ((wh, (hi, lo)), (wl, (hi,))):
                            for h in range(2):
                                for a in parts:
                                    ins = T.matmul(bank[bs[h]][:, 0:HALF], w[:, k, c * P:(c + 1) * P],
                                                   a[:, k, h * HALF:(h + 1) * HALF],
                                                   start=(k == 0 and w is wh and a is hi),
                                                   stop=(k == KD - 1 and w is wl))
                                if k == KD - 1 and w is wl:
                                    done(ins, keys[h])
                ends[i] = ("bank", keys[1])

            def down(name, half, blks, left, tiles, ready=None):
                keys = [(name, half, t) for t in range(tiles)]
                bs = [take(k) for k in keys]
                nk = sum(blocks[i][1] for i in blks)
                k = 0
                for i in blks:
                    pe.wait_ge(s["w_lo_ready"], i + 1)
                    wh, wl = wv(whi, i), wv(wlo, i)
                    for kk in range(blocks[i][1]):
                        if ready:
                            ready(half, k)
                        hi, lo = left(half, k)
                        for t in range(tiles):
                            o = bank[bs[t]][:, :]
                            T.matmul(o, hi[:, t * P:(t + 1) * P], wh[:, kk, :], start=(k == 0), stop=False)
                            T.matmul(o, hi[:, t * P:(t + 1) * P], wl[:, kk, :], start=False, stop=False)
                            ins = T.matmul(o, lo[:, t * P:(t + 1) * P], wh[:, kk, :], start=False, stop=(k == nk - 1))
                            if k == nk - 1:
                                done(ins, keys[t])
                        if k < nk - 1:
                            step(ins, (name, half, k))
                        else:
                            ends[(name, half, k)] = ("bank", keys[-1])
                        k += 1
                    ends[i] = ends[(name, half, k - 1)]

            def rows_tile(name, half, blks, left, t):
                b = take((name, half, t))
                k, tt = 0, slice(t * P, (t + 1) * P)
                nk = sum(blocks[i][1] for i in blks)
                for i in blks:
                    if t == 0:
                        pe.wait_ge(s["w_lo_ready"], i + 1)
                    wh, wl = wv(whi, i), wv(wlo, i)
                    for kk in range(blocks[i][1]):
                        hi, lo = left(half, k)
                        T.matmul(bank[b][:, :], hi[:, tt], wh[:, kk, :], start=(k == 0), stop=False)
                        T.matmul(bank[b][:, :], hi[:, tt], wl[:, kk, :], start=False, stop=False)
                        ins = T.matmul(bank[b][:, :], lo[:, tt], wh[:, kk, :], start=False, stop=(k == nk - 1))
                        k += 1
                done(ins, (name, half, t))
                if t == NT - 1:
                    for i in blks:
                        ends[i] = ("bank", (name, half, t))

            def turn_rows(kind, n, src, ready):
                pe.wait_ge(s["xn_ready"], ready)
                for g in range(2):
                    b = take((kind, n, g))
                    for j in range(4):
                        ins = T.transpose(bank[b][:, j * P:(j + 1) * P], src[:, (4 * g + j) * P:(4 * g + j + 1) * P],
                                          ident[:, :])
                    done(ins, (kind, n, g))

            pe.wait_ge(s["consts"], 1)
            pe.wait_ge(s["small_loaded"], SMALL_LOADS * 16)
            b = take(("cache", 0))
            for j in range(12):
                ins = T.transpose(bank[b][:, 24 * j:24 * j + 24], crow[:, j * P:(j + 1) * P], ident[0:24, 0:24])
            for j in range(2):
                ins = T.transpose(bank[b][:, 288 + 16 * j:304 + 16 * j], scrow[:, j * P:(j + 1) * P], ident[0:16, 0:16])
            done(ins, ("cache", 0))
            for n in range(2 + NT):
                turn_rows("norm1", n, xn[n % 2], n + 1)
            for n in range(2, 2 + NT):
                for g in range(2):
                    evacuated(pe, ("norm1", n, g))

            pe.wait_ge(s["w8_ready"], 2)
            for h in range(2):
                b = take(("gates", h))
                hs = slice(h * HALF, (h + 1) * HALF)
                for k in range(KD):
                    T.matmul(bank[b][0:8, 0:HALF], w8hi[:, k, :], hhi[:, k, hs], start=(k == 0), stop=False)
                    T.matmul(bank[b][0:8, 0:HALF], w8hi[:, k, :], hlo[:, k, hs], start=False, stop=False)
                    ins = T.matmul(bank[b][0:8, 0:HALF], w8lo[:, k, :], hhi[:, k, hs], start=False, stop=(k == KD - 1))
                done(ins, ("gates", h))
            for n in range(8):
                across(("in", n), B_IN[n], hhi, hlo)
                if n == 0:
                    evacuated(pe, ("gates", 0))
                    evacuated(pe, ("gates", 1))
                    b = take(("gates", 2))
                    for t in range(NT):
                        ins = T.transpose(bank[b][:, 8 * t:8 * t + 8], gT[0:8, t * P:(t + 1) * P], ident[0:8, 0:8])
                    done(ins, ("gates", 2))
            for c in range(8):
                pe.wait_ge(s["sq_ready"], c + 1)
                for h in range(2):
                    b = take(("l2", c, h))
                    done(T.matmul(bank[b][:, 0:HALF], ones[:, :], sqA[c % 2][:, h * HALF:(h + 1) * HALF],
                                  start=True, stop=True), ("l2", c, h))
                if c % 2:
                    across(("in", 8 + c // 2), B_IN[8 + c // 2], hhi, hlo)
            down("ck", 0, B_CK, lambda h, k: (hhi[:, k, :], hlo[:, k, :]), NT)
            for t in range(NT):
                evacuated(pe, ("ck", 0, t))
            for hp in range(2):
                for g, ts in enumerate(((0, 1, 2, 3), (4,))):
                    b = take(("kT", hp, g))
                    for j, t in enumerate(ts):
                        ins = T.transpose(bank[b][:, j * P:(j + 1) * P], ckv[:, t, hp * P:(hp + 1) * P], ident[:, :])
                    done(ins, ("kT", hp, g))
            mleft = lambda h, k: (mhi[:, k, :], mlo[:, k, :])
            down("mk", 0, B_MK, mleft, 2)
            pe.wait_ge(s["conv_done"], 14)
            for g in range(3):
                b = take(("strow", g))
                for j in range(4):
                    ins = T.transpose(bank[b][0:27, j * P:(j + 1) * P], cst[:, 4 * g + j, :], ident[:, :])
                done(ins, ("strow", g))
            b = take(("strow", 3))
            for j in range(2):
                ins = T.transpose(bank[b][0:18, j * P:(j + 1) * P], scst[:, j, :], ident[:, :])
            done(ins, ("strow", 3))
            down("mv", 0, B_MV, mleft, 2)
            for t in range(2):
                evacuated(pe, ("mk", 0, t))
                b = take(("memkT", t))
                for h in range(HEADS):
                    ins = T.transpose(bank[b][:, h * P:(h + 1) * P], mkout[:, t, h * P:(h + 1) * P], ident[:, :])
                done(ins, ("memkT", t))

            for hp in range(2):
                for g in range(2):
                    evacuated(pe, ("kT", hp, g))

            def scores(n):
                kind, x, i = SB_ITEMS[n]
                if kind == "p":
                    hp, h2 = divmod(x, 2)
                    r = slice(64 * h2, 64 * h2 + 64)
                    b = take(("z", n, 0))
                    w = (i + 1) * P
                    T.matmul(bank[b][:, 0:w], cq[r, hp, i * P:(i + 1) * P], kT[r, hp, 0:w], start=True, stop=False)
                    done(T.matmul(bank[b][:, i * P:w], ident[:, :], negm[:, :], start=False, stop=True), ("z", n, 0))
                    return
                if x == 0:
                    pe.wait_ge(s["q_blocks"], 1)
                bb = []
                for b2 in range(2):
                    bt = 2 * x + b2
                    pe.wait_ge(s[f"kc_loaded{bt % 4}"], 16 * (bt // 4 + 1))
                    for hp in range(2):
                        b = take(("kc", bt, hp))
                        for j in range(4):
                            ins = T.transpose(bank[b][:, j * P:(j + 1) * P], kraw[bt % 4][:, j, hp * P:(hp + 1) * P],
                                              ident[:, :])
                        done(ins, ("kc", bt, hp))
                zo, zn = take(("z", n, 0)), take(("z", n, 1))
                for b2 in range(2):
                    bt = 2 * x + b2
                    for hp in range(2):
                        g = 2 * b2 + hp
                        r = slice(32 * g, 32 * g + 32)
                        evacuated(pe, ("kc", bt, hp))
                        last = T.matmul(bank[zo][r, :], qbl[:, hp, bt, :], kTs[b2][:, hp, :], start=True, stop=True)
                        if g == 3:
                            done(last, ("z", n, 0))
                        last = T.matmul(bank[zn][r, 0:P], qbl[:, hp, bt, :], kT[:, hp, SEQ:TOK], start=True, stop=True)
                        if g == 3:
                            done(last, ("z", n, 1))

            def turn_probs(n):
                kind, x, i = SB_ITEMS[n]
                pe.wait_ge(s["A_ready"], n + 1)
                nb = i + 1 if kind == "p" else 5
                lo = 640 - nb * P
                for g in range((nb + 3) // 4):
                    b = take(("AT", n, g))
                    for j in range(4 * g, min(nb, 4 * g + 4)):
                        ins = T.transpose(bank[b][:, (j % 4) * P:(j % 4 + 1) * P],
                                          att_a[n % 2][:, lo + j * P:lo + (j + 1) * P], ident[:, :])
                    done(ins, ("AT", n, g))

            oc = {}

            def values(n):
                kind, x, i = SB_ITEMS[n]
                for g in range(1 if kind == "p" else 2):
                    evacuated(pe, ("AT", n, g))
                a = att_t[n % 2]
                if kind == "p":
                    hp, h2 = divmod(x, 2)
                    if h2 == 0 and i == 0:
                        oc[hp] = take(("oc", hp), long=True)
                    for j in range(i + 1):
                        ins = T.matmul(bank[oc[hp]][64 * h2:64 * h2 + 64, i * P:(i + 1) * P],
                                       ckv[:, j, 256 + 64 * x:320 + 64 * x], a[:, j * P:(j + 1) * P],
                                       start=(j == 0), stop=(j == i))
                    if h2 == 1 and i == PT - 1:
                        done(ins, ("oc", hp))
                        ends[("av", n)] = ("bank", ("oc", hp))
                    else:
                        step(ins, ("av", n))
                    return
                if x == 0:
                    oc[2] = take(("oc", 2), long=True)
                for b2 in range(2):
                    bt = 2 * x + b2
                    pe.wait_ge(s[f"vc_loaded{bt % 4}"], 16 * (bt // 4 + 1))
                    for hp in range(2):
                        g = 2 * b2 + hp
                        c0 = (hp * DEC_BATCH + bt) * 32
                        for j in range(5):
                            v = vraw[bt % 4][:, j, hp * P:(hp + 1) * P] if j < 4 \
                                else ckv[:, PT, 256 + hp * P:256 + (hp + 1) * P]
                            ins = T.matmul(bank[oc[2]][:, c0:c0 + 32], v, a[:, j * P + 32 * g:j * P + 32 * g + 32],
                                           start=(j == 0), stop=(j == 4))
                if x == 3 and b2 == 1:
                    done(ins, ("oc", 2))
                    ends[("av", n)] = ("bank", ("oc", 2))
                elif b2 == 1:
                    step(ins, ("av", n))

            scores(0)
            for n in range(NI + 1):
                if n + 1 < NI:
                    scores(n + 1)
                if n < NI:
                    turn_probs(n)
                if n >= 1:
                    values(n - 1)

            pe.wait_ge(s["gates"], 1)
            for i in range(NT):
                tt = slice(i * P, (i + 1) * P)
                b = take(("gcol", i))
                T.matmul(bank[b][:, 0:4], (uptri if i < PT else up16)[:, :], gdec[:, i, :], start=True, stop=True)
                done(T.matmul(bank[b][:, 4:8], (ones if i < PT else same16)[:, :], gdec[:, i, :],
                              start=True, stop=True), ("gcol", i))
                pe.wait_ge(s["rhs_ready"], 2 * i + 1)
                b = take(("grow", i))
                done(T.matmul(bank[b][:, :], ones[:, :], flat(scr[i % 2]), start=True, stop=True), ("grow", i))
                b = take(("kk", i))
                for h in range(HEADS):
                    ins = T.matmul(bank[b][:, h * P:(h + 1) * P], qkvz[:, 4 + h, tt], qkvz[:, 4 + h, tt],
                                   start=True, stop=True)
                done(ins, ("kk", i))
                b = take(("qk", i))
                for h in range(HEADS):
                    ins = T.matmul(bank[b][:, h * P:(h + 1) * P], qkvz[:, 4 + h, tt], qkvz[:, h, tt],
                                   start=True, stop=True)
                done(ins, ("qk", i))
                pe.wait_ge(s["rhs_ready"], 2 * i + 2)
                b = take(("brow", i))
                done(T.matmul(bank[b][:, :], ones[:, :], flat(scr[2 + i % 2]), start=True, stop=True), ("brow", i))

            def turn_x(l, i):
                b = take(("X", l, i))
                for h in range(HEADS):
                    ins = T.transpose(bank[b][:, h * P:(h + 1) * P], XT[:, i, h, :], ident[:, :])
                done(ins, ("X", l, i))

            for i in range(NT):
                pe.wait_ge(s["xt0_ready"], i + 1)
                turn_x(0, i)
            for l in range(1, LEVELS):
                for i in TILES_AT[l]:
                    pe.wait_ge(s["lm_ready"], LM_ORDER.index((l, i)) + 1)
                    evacuated(pe, ("X", l - 1, i))
                    b = take(("Y", l, i))
                    for h in range(HEADS):
                        ins = T.matmul(bank[b][:, h * P:(h + 1) * P], scr[4 + LM_ORDER.index((l, i)) % 2][:, h, :],
                                       XY[:, i, h, :], start=True, stop=True)
                    done(ins, ("Y", l, i))
                for i in TILES_AT[l]:
                    evacuated(pe, ("Y", l, i))
                    b = take(("dX", l, i))
                    for h in range(HEADS):
                        ins = T.matmul(bank[b][:, h * P:(h + 1) * P], XY[:, i, h, :], XT[:, i, h, :],
                                       start=True, stop=True)
                    done(ins, ("dX", l, i))
                if l < LEVELS - 1:
                    for i in TILES_AT[l + 1]:
                        evacuated(pe, ("dX", l, i))
                        turn_x(l, i)

            for i in range(NT):
                tt = slice(i * P, (i + 1) * P)
                evacuated(pe, ("dX", (LEVELS if i < PT else SAMPLE_LEVELS) - 1, i))
                b = take(("Vt", i))
                for h in range(HEADS):
                    ins = T.transpose(bank[b][:, h * P:(h + 1) * P], qkvz[:, 8 + h, tt], ident[:, :])
                done(ins, ("Vt", i))
                b = take(("Kt", i))
                for h in range(HEADS):
                    ins = T.transpose(bank[b][:, h * P:(h + 1) * P], qkvz[:, 4 + h, tt], ident[:, :])
                done(ins, ("Kt", i))
                evacuated(pe, ("Vt", i))
                pe.wait_ge(s["kd_ready"], i + 1)
                b = take(("wT", i))
                for h in range(HEADS):
                    ins = T.matmul(bank[b][:, h * P:(h + 1) * P], scr[2 + i % 2][:, h, :], XT[:, i, h, :],
                                   start=True, stop=True)
                done(ins, ("wT", i))
                evacuated(pe, ("wT", i))
                if i == 0:
                    pass
                elif i < PT:
                    evacuated(pe, ("dS", i - 1))
                else:
                    pe.wait_ge(s["st_loaded"], 16 * DEC_BATCH)
                    b = take(("ws", 0))
                    for h in range(HEADS):
                        for bt in range(DEC_BATCH):
                            c0 = h * P + DEC_SEQ * bt
                            ins = T.matmul(bank[b][:, c0:c0 + DEC_SEQ], stS[:, bt, h, :],
                                           scr[6 + i % 2][:, h, DEC_SEQ * bt:DEC_SEQ * (bt + 1)], start=True, stop=True)
                    done(ins, ("ws", 0))
                    evacuated(pe, ("ws", 0))
                b = take(("vn", i))
                for h in range(HEADS):
                    o = bank[b][:, h * P:(h + 1) * P]
                    ins = T.matmul(o, XT[:, i, h, :], scr[i % 2][:, h, :], start=True, stop=(i == 0))
                    if 0 < i < PT:
                        ins = T.matmul(o, scr[6 + i % 2][:, h, :], stP[:, h, :], start=False, stop=True)
                    if i == PT:
                        ins = T.matmul(o, scr[7][:, h, :], ident[:, :], start=False, stop=True)
                done(ins, ("vn", i))
                evacuated(pe, ("vn", i))
                vn = scr[8 + i % 2]
                b = take(("o", i))
                for h in range(HEADS):
                    o = bank[b][:, h * P:(h + 1) * P]
                    ins = T.matmul(o, vn[:, h, :], qkD[:, i, h, :], start=True, stop=(i == 0))
                    if 0 < i < PT:
                        ins = T.matmul(o, stP[:, h, :], qkvz[:, h, tt], start=False, stop=True)
                    if i == PT:
                        for bt in range(DEC_BATCH):
                            c0 = DEC_SEQ * bt
                            ins = T.matmul(o[:, c0:c0 + DEC_SEQ], stS[:, bt, h, :],
                                           qkvz[:, h, SEQ + c0:SEQ + c0 + DEC_SEQ], start=False,
                                           stop=(bt == DEC_BATCH - 1))
                done(ins, ("o", i))
                if i < PT:
                    evacuated(pe, ("Kt", i))
                    b = take(("dS", i))
                    for h in range(HEADS):
                        ins = T.matmul(bank[b][:, h * P:(h + 1) * P], scr[4 + i % 2][:, h, :], vn[:, h, :],
                                       start=True, stop=True)
                    done(ins, ("dS", i))
            evacuated(pe, ("Kt", PT))
            for h in range(HEADS):
                pe.wait_ge(s["vm_ready"], h + 1)
                for g in range(2):
                    b = take(("dSs", h, g))
                    done(T.matmul(bank[b][:, :], scr[4 + PT % 2][:, h, :], vmask[h % 2][:, 4 * g:4 * g + 4, :],
                                  start=True, stop=True), ("dSs", h, g))

            for f in range(8):
                pe.wait_ge(s["sqf_ready"], f + 1)
                for h in range(2):
                    b = take(("gn", f, h))
                    done(T.matmul(bank[b][:, 0:HALF], (ones if f < 4 else same64)[:, :],
                                  sqG[f % 2][:, h * HALF:(h + 1) * HALF], start=True, stop=True), ("gn", f, h))

            ready_y = lambda h, k: pe.wait_ge(s["ylo_ready"], k + 1)
            left_y = lambda h, k: (hhi[:, k, :], hlo[:, k, :])
            down("out", 0, B_OUT[0], left_y, NT, ready_y)
            for n in range(NT + 1):
                if n < NT:
                    rows_tile("out", 1, B_OUT[1], left_y, n)
                if n >= 1:
                    turn_rows("norm2", n - 1, xn2[(n - 1) % 2], 2 + NT + n)
            for n in range(NT):
                for g in range(2):
                    evacuated(pe, ("norm2", n, g))
            for n in range(2):
                across(("mq", n), B_MQ[n], hhi, hlo)
            for h in range(HEADS):
                pe.wait_ge(s["qsq_ready"], h + 1)
                for g in range(2):
                    b = take(("mqn", h, g))
                    done(T.matmul(bank[b][:, 0:HALF], ones[:, :], sqM[h % 2][:, g * HALF:(g + 1) * HALF],
                                  start=True, stop=True), ("mqn", h, g))
            pe.wait_ge(s["qm_ready"], HEADS)

            def mem_scores(i):
                for g in range(2):
                    b = take(("ms", i, g))
                    for j in range(2):
                        h = 2 * g + j
                        ins = T.matmul(bank[b][:, j * N_MEM:(j + 1) * N_MEM], qm[:, h, i * P:(i + 1) * P], memkT[:, h, :],
                                       start=True, stop=True)
                    done(ins, ("ms", i, g))

            def mem_probs(i):
                pe.wait_ge(s["prob_ready"], i + 1)
                for g in range(2):
                    b = take(("pT", i, g))
                    for j in range(4):
                        h, nb = 2 * g + j // 2, j % 2
                        ins = T.transpose(bank[b][:, j * P:(j + 1) * P], probs[i % 2][:, h, nb * P:(nb + 1) * P],
                                          ident[:, :])
                    done(ins, ("pT", i, g))

            def mem_values(i):
                for g in range(2):
                    evacuated(pe, ("pT", i, g))
                b = take(("om", i))
                for h in range(HEADS):
                    for nb in range(2):
                        ins = T.matmul(bank[b][:, h * P:(h + 1) * P], memv[:, nb, h * P:(h + 1) * P],
                                       probT[i % 2][:, h, nb, :], start=(nb == 0), stop=(nb == 1))
                done(ins, ("om", i))

            sT = [take(("sT", nb), long=True) for nb in range(2)]

            def sample_keys(bt):
                pe.wait_ge(s[f"mc_loaded{bt}"], 16)
                for nb in range(2):
                    b = take(("km", bt, nb))
                    for h in range(HEADS):
                        ins = T.transpose(bank[b][:, h * P:(h + 1) * P], mkraw[bt][:, nb, h * P:(h + 1) * P],
                                          ident[:, :])
                    done(ins, ("km", bt, nb))

            def sample_scores(bt):
                for nb in range(2):
                    evacuated(pe, ("km", bt, nb))
                for nb in range(2):
                    for h in range(HEADS):
                        c0 = h * P + DEC_SEQ * bt
                        ins = T.matmul(bank[sT[nb]][:, c0:c0 + DEC_SEQ], kmT[bt % 2][:, h, nb * P:(nb + 1) * P],
                                       qm[:, h, SEQ + DEC_SEQ * bt:SEQ + DEC_SEQ * (bt + 1)], start=True, stop=True)
                    if bt == DEC_BATCH - 1:
                        done(ins, ("sT", nb))
                if bt < DEC_BATCH - 1:
                    step(ins, ("sT", bt))

            mem_scores(0)
            for i in range(PT):
                if i + 1 < PT:
                    mem_scores(i + 1)
                sample_keys(2 * i)
                mem_probs(i)
                sample_scores(2 * i)
                sample_keys(2 * i + 1)
                if i >= 1:
                    mem_values(i - 1)
                sample_scores(2 * i + 1)
            mem_values(PT - 1)
            for nb in range(2):
                evacuated(pe, ("sT", nb))
            for g in range(2):
                b = take(("ms", PT, g))
                for j in range(2):
                    for nb in range(2):
                        ins = T.transpose(bank[b][:, (2 * j + nb) * P:(2 * j + nb + 1) * P], stsb[:, nb, 2 * g + j, :],
                                          ident[:, :])
                done(ins, ("ms", PT, g))

            def mem_out(n):
                evacuated(pe, ("om", n))
                for half in range(2):
                    rows_tile("mo", half, B_MO[half], lambda h, k: (omhi[:, k, :], omlo[:, k, :]), n)

            def turn_norm3(n):
                turn_rows("norm3", n, xn3[n % 2], 2 + 2 * NT + n + 1)

            mem_out(0)
            mem_out(1)
            mem_probs(PT)
            mem_out(2)
            for g in range(2):
                evacuated(pe, ("pT", PT, g))
            b = take(("om", PT))
            for bt in range(DEC_BATCH):
                pe.wait_ge(s[f"mc_loaded{bt}"], 32)
                for h in range(HEADS):
                    for nb in range(2):
                        c0 = h * P + DEC_SEQ * bt
                        ins = T.matmul(bank[b][:, c0:c0 + DEC_SEQ], mkraw[bt][:, nb, h * P:(h + 1) * P],
                                       probT[PT % 2][:, h, nb, DEC_SEQ * bt:DEC_SEQ * (bt + 1)],
                                       start=(nb == 0), stop=(nb == 1))
            done(ins, ("om", PT))
            turn_norm3(0)
            turn_norm3(1)
            mem_out(3)
            turn_norm3(2)
            mem_out(4)
            turn_norm3(3)
            turn_norm3(4)
            pe.wait_ge(s["f_loaded"], 32)
            b = take(("cacheF", 0))
            for j in range(FT):
                ins = T.transpose(bank[b][:, 16 * j:16 * j + 16], frow[:, j * P:(j + 1) * P], ident[0:16, 0:16])
            done(ins, ("cacheF", 0))
            for n in range(NT):
                for g in range(2):
                    evacuated(pe, ("norm3", n, g))
            for j in range(FT // 2):
                across(("gate", j), B_GU[j][0], hhi, hlo)
                across(("up", j), B_GU[j][1], hhi, hlo)
            def ready_a(h, k):
                pe.wait_ge(s["alo_ready"], FT * h + k + 1)

            def left_a(h, k):
                n = (FT * h + k) % KD
                return hhi[:, n, :], hlo[:, n, :]
            down("dn", 0, B_DN[0], left_a, NT, ready_a)
            pe.wait_ge(s["ffn_conv"], FT)
            for g in range(6):
                b = take(("frow", g))
                for j in range(4 * g, min(FT, 4 * g + 4)):
                    ins = T.transpose(bank[b][0:18, (j % 4) * P:(j % 4 + 1) * P], fcst[:, j, :], ident[:, :])
                done(ins, ("frow", g))
            down("dn", 1, B_DN[1], left_a, NT, ready_a)


        @block.sync
        def _(sp):
            D = sp.dma_start

            def load_w(i):
                if i >= 2:
                    sp.wait_ge(s["w_lo_ready"], i - 1)
                D(wv(wraw, i), blocks[i][0]).then_inc(w_loaded[i % 2], 16)

            def load_rows(n):
                if n >= 2:
                    sp.wait_ge(s["xn_ready"], n - 1)
                src = A["mem_prompt"][n * P:(n + 1) * P, :] if n < 2 else \
                    A["x_prompt"][(n - 2) * P:(n - 1) * P, :] if n < 2 + PT else A["x_sample"]
                D(xin[n % 2][:, :], src).then_inc(s[f"x_loaded{n % 2}"], 16)

            load_rows(0)
            load_rows(1)
            for dst, src in small:
                D(dst, src).then_inc(s["small_loaded"], 16)
            with nc.allow_non_contiguous_dma(reason="a few weights of one element per partition"):
                for dst, src in small_cols:
                    D(dst, src).then_inc(s["small_loaded"], 16)
            for n in range(2, 2 + NT):
                load_rows(n)
            for i in range(B_OUT[1][1] + 1):
                load_w(i)
            for t in range(NT):
                evacuated(sp, ("ck", 0, t))
            for col, name in ((0, "sb_k"), (256, "sb_v")):
                D(O["p_" + name].rearrange("(t p) c -> p t c", p=P), ckv[:, 0:PT, col:col + 256]).then_inc(s["out_sb"], 16)
                D(O["s_" + name], ckv[:, PT, col:col + 256]).then_inc(s["out_sb"], 16)

            def load_k(bt):
                D(kraw[bt % 4][:, :, :], A["cache_sb_k"][bt].rearrange("(j p) c -> p j c", p=P))\
                    .then_inc(s[f"kc_loaded{bt % 4}"], 16)

            def load_v(bt):
                D(vraw[bt % 4][:, :, :], A["cache_sb_v"][bt].rearrange("(j p) c -> p j c", p=P))\
                    .then_inc(s[f"vc_loaded{bt % 4}"], 16)
            for bt in range(4):
                load_k(bt)
            load_v(0)
            load_v(1)
            for g in range(4):
                evacuated(sp, ("strow", g))
            D(O["p_gdn_conv"], strow[0:3, :]).then_inc(s["out_rows"], 16)
            D(O["s_gdn_conv"], strow[3:27, :]).then_inc(s["out_rows"], 16)
            D(O["p_sc_conv"], scsrow[0:2, :]).then_inc(s["out_rows"], 16)
            D(O["s_sc_conv"], scsrow[2:18, :]).then_inc(s["out_rows"], 16)
            for t in range(2):
                evacuated(sp, ("mk", 0, t))
            D(O["p_mem_k"].rearrange("(t p) c -> p t c", p=P), mkout[:, :, :]).then_inc(s["out_mk"], 16)
            for t in range(2):
                evacuated(sp, ("mv", 0, t))
            D(O["p_mem_v"].rearrange("(t p) c -> p t c", p=P), memv[:, :, :]).then_inc(s["out_mv"], 16)
            sp.wait_ge(s["out_rows"], 64)
            load_v(2)
            load_v(3)
            for x in (0, 1):
                for b2 in range(2):
                    filled(sp, ("kc", 2 * x + b2, 1))
                    load_k(4 + 2 * x + b2)
                passed(sp, ("av", 16 + x))
                for b2 in range(2):
                    load_v(4 + 2 * x + b2)
            evacuated(sp, ("dX", LEVELS - 1, PT - 1))
            evacuated(sp, ("dX", SAMPLE_LEVELS - 1, PT))
            for bt in range(DEC_BATCH):
                D(stS[:, bt, :, :], A["state_gdn"][bt].rearrange("h k v -> k h v")).then_inc(s["st_loaded"], 16)
            evacuated(sp, ("dS", PT - 1))
            D(O["p_gdn_state"].rearrange("h k v -> k h v"), stP[:, :, :]).then_inc(s["out_pstate"], 16)
            for h in range(HEADS):
                for g in range(2):
                    evacuated(sp, ("dSs", h, g))
            for bt in range(DEC_BATCH):
                D(O["s_gdn_state"][bt].rearrange("h k v -> k h v"), stS[:, bt, :, :]).then_inc(s["out_sstate"], 16)
            sp.wait_ge(s["ylo_ready"], 8)
            D(xres[:, 0:PT, :], A["x_prompt"].rearrange("(t p) c -> p t c", p=P)).then_inc(s["xres_loaded"], 16)
            D(xres[:, PT, :], A["x_sample"]).then_inc(s["xres_loaded"], 16)
            D(gmem[:, :], A["norm_mem_g"].partition_broadcast(P)).then_inc(s["gm_loaded"], 16)
            D(frow[0:16, :], A["cache_ffn_conv"].rearrange("b t c -> (b t) c")).then_inc(s["f_loaded"], 16)
            with nc.allow_non_contiguous_dma(reason="a few weights of one element per partition"):
                for k in range(3):
                    D(fcw[:, :, k], A["ffn_conv_w"][k, :].rearrange("(j p) -> p j", p=P)).then_inc(s["f_loaded"], 16)
            for i in range(B_OUT[1][1] + 1, B_GU[0][0]):
                load_w(i)

            D(gffn[:, :], A["norm_ffn_g"].partition_broadcast(P)).then_inc(s["gm_loaded"], 16)

            def load_mem(bt, name):
                D(mkraw[bt][:, :, :], A[name][bt].rearrange("(j p) c -> p j c", p=P)).then_inc(s[f"mc_loaded{bt}"], 16)
            filled(sp, (("mq", 1), 1, 1))
            for bt in range(DEC_BATCH):
                load_mem(bt, "cache_mem_k")
            for bt in range(DEC_BATCH):
                filled(sp, ("km", bt, 1))
                load_mem(bt, "cache_mem_v")
            for i in range(B_GU[0][0], B_DN[1][0] + 2):
                load_w(i)
            for g in range(6):
                evacuated(sp, ("frow", g))
            D(O["p_ffn_conv"], fsrow[0:2, :]).then_inc(s["out_frows"], 16)
            D(O["s_ffn_conv"], fsrow[2:18, :]).then_inc(s["out_frows"], 16)
            for i in range(B_DN[1][0] + 2, NB):
                load_w(i)
            for t in range(NT):
                evacuated(sp, ("dn", 0, t))
                evacuated(sp, ("dn", 1, t))
                dst = O["y_prompt"][t * P:(t + 1) * P, :] if t < PT else O["y_sample"]
                D(dst, xres[:, t, :]).then_inc(s["out_y"], 16)
            for name, n in (("out_sb", 4), ("out_mk", 1), ("out_mv", 1), ("out_rows", 4), ("out_frows", 2),
                            ("out_pstate", 1), ("out_sstate", DEC_BATCH), ("out_y", NT)):
                sp.wait_ge(s[name], 16 * n)

        @block.gpsimd
        def _(pool):
            G = nc.gpsimd
            chain = [0]

            def link(ins):
                chain[0] += 1
                ins.then_inc(s["pool_chain"], 1)
                pool.wait_ge(s["pool_chain"], chain[0])

            for t, v in ((ones, 1.0), (ident, 0.0), (negm, NEG), (newm, 0.0), (epsc, EPS), (lnsc, 1.0)):
                G.memset(t[:, :], v)
            G.memset(own8[:, :], 1.0)
            G.memset(same16[:, :], 1.0)
            link(G.memset(same64[:, :], 1.0))
            sel = G.affine_select
            sel(out=ident[:, :], in_=ident[:, :], compare_op=ALU.not_equal, fill=1.0, base=0, pattern=[[-1, P]],
                channel_multiplier=1)
            sel(out=uptri[:, :], in_=ones[:, :], compare_op=ALU.is_ge, fill=0.0, base=0, pattern=[[1, P]],
                channel_multiplier=-1)
            sel(out=negm[:, :], in_=negm[:, :], compare_op=ALU.is_ge, fill=0.0, base=0, pattern=[[1, P]],
                channel_multiplier=-1)
            sel(out=own8[:, :], in_=own8[:, :], compare_op=ALU.is_ge, fill=0.0, base=0, pattern=[[-DEC_SEQ, DEC_BATCH]],
                channel_multiplier=1)
            grid = [[-DEC_SEQ, DEC_BATCH], [0, DEC_SEQ]]
            s16 = same16[:, :].rearrange("p (a b) -> p a b", a=DEC_BATCH)
            link(sel(out=s16, in_=s16, compare_op=ALU.is_ge, fill=0.0, base=0, pattern=grid, channel_multiplier=1))
            link(sel(out=s16, in_=s16, compare_op=ALU.is_ge, fill=0.0, base=DEC_SEQ - 1,
                     pattern=[[DEC_SEQ, DEC_BATCH], [0, DEC_SEQ]], channel_multiplier=-1))
            s64 = same64[:, :].rearrange("p (a b) -> p a b", a=2)
            link(sel(out=s64, in_=s64, compare_op=ALU.is_ge, fill=0.0, base=0, pattern=[[-64, 2], [0, 64]],
                     channel_multiplier=1))
            link(sel(out=s64, in_=s64, compare_op=ALU.is_ge, fill=0.0, base=63, pattern=[[64, 2], [0, 64]],
                     channel_multiplier=-1))
            sel(out=own8[:, :], in_=own8[:, :], compare_op=ALU.is_ge, fill=0.0, base=DEC_SEQ - 1,
                pattern=[[DEC_SEQ, DEC_BATCH]], channel_multiplier=-1)
            G.tensor_copy(lmask[:, 0, :], ident[:, :])
            for l in range(1, LEVELS):
                m = 1 << l
                v = lmask[:, l, :].rearrange("p (a b) -> p a b", b=m)
                u = uptri[:, :].rearrange("p (a b) -> p a b", b=m)
                ins = sel(out=v, in_=u, compare_op=ALU.is_ge, fill=0.0, base=0, pattern=[[-m, P // m], [0, m]],
                          channel_multiplier=1)
            link(ins)
            link(G.tensor_copy(up16[:, :], lmask[:, 4, :]))
            for l in range(LEVELS):
                up = lmask[:, l + 1, :] if l < LEVELS - 1 else uptri[:, :]
                link(G.tensor_tensor(lmask[:, l, :], up, lmask[:, l, :], ALU.subtract))
            link(G.tensor_tensor(newi[:, 0:P], same16[:, :], up16[:, :], ALU.subtract))
            for q in range(1, 8):
                link(G.tensor_tensor(newi[:, 0:16], newi[:, 0:16], newi[:, 16 * q:16 * q + 16], ALU.add))
            link(G.tensor_copy(newm[0:64, 96:112], newi[0:64, 0:16]))
            link(G.tensor_copy(newm[64:P, 112:128], newi[64:P, 0:16]))
            G.tensor_scalar(newi[:, :], newm[:, :], -1.0, 1.0, ALU.mult, ALU.add).then_inc(s["consts"], 1)

            def cut_lo(i):
                pool.wait_ge(s["w_hi_ready"], i + 1)
                G.tensor_tensor(wv(wlo, i), wv(wraw, i), wv(whi, i).bitcast(F32), ALU.subtract)\
                    .then_inc(s["w_lo_ready"], 1)

            cut_lo(0)
            pool.wait_ge(s["w8_ready"], 1)
            G.tensor_tensor(w8lo[:, :, :], w8raw[:, :, :], w8hi[:, :, :].bitcast(F32), ALU.subtract)\
                .then_inc(s["w8_ready"], 1)
            for i in range(1, B_OUT[0][1] + 1):
                cut_lo(i)

            def row_sources(i):
                if i >= 2:
                    filled(pool, ("brow", i - 2))
                G.tensor_tensor(scr[i % 2][:, :, :], spread(tri(i)[:, :], 1, [P, HEADS, P]),
                                spread(gdec[:, i, :], 2, [P, HEADS, P]), ALU.mult).then_inc(s["rhs_ready"], 1)
                G.tensor_tensor(scr[2 + i % 2][:, :, :], spread(ident[:, :], 1, [P, HEADS, P]),
                                spread(beta[:, i, :], 2, [P, HEADS, P]), ALU.mult).then_inc(s["rhs_ready"], 1)

            pool.wait_ge(s["gates"], 1)
            passed(pool, ("av", NI - 1))
            row_sources(0)
            row_sources(1)
            for i in range(NT):
                pool.wait_ge(s["dt_ready"], i + 1)
                if i >= 2:
                    pool.wait_ge(s["lt_ready"], i - 1)
                G.tensor_tensor(scr[8 + i % 2][:, :, :], scr[4 + i % 2][:, :, :],
                                spread(tri(i)[:, :], 1, [P, HEADS, P]), ALU.mult).then_inc(s["dtu_ready"], 1)
                if i + 2 < NT:
                    row_sources(i + 2)
                evacuated(pool, ("brow", i))
                link(G.tensor_tensor(XT[:, i, :, :], LT[:, i, :, :], spread(lmask[:, 0, :], 1, [P, HEADS, P]), ALU.mult))
                G.tensor_tensor(XT[:, i, :, :], spread(ident[:, :], 1, [P, HEADS, P]), XT[:, i, :, :], ALU.subtract)\
                    .then_inc(s["xt0_ready"], 1)
            for n, (l, i) in enumerate(LM_ORDER):
                if n >= 2:
                    filled(pool, ("Y",) + LM_ORDER[n - 2])
                G.tensor_tensor(scr[4 + n % 2][:, :, :], LT[:, i, :, :], spread(lmask[:, l, :], 1, [P, HEADS, P]),
                                ALU.mult).then_inc(s["lm_ready"], 1)
            evacuated(pool, ("vn", PT))
            for h in range(HEADS):
                if h >= 2:
                    filled(pool, ("dSs", h - 2, 1))
                G.tensor_tensor(vmask[h % 2][:, :, :], spread(scr[8 + PT % 2][:, h, :], 1, [P, DEC_BATCH, P]),
                                spread(own8[:, :], 2, [P, DEC_BATCH, P]), ALU.mult).then_inc(s["vm_ready"], 1)
            for f in range(8):
                pool.wait_ge(s["yhi_ready"], f + 1)
                G.tensor_tensor(hlo[:, f, :], mixed(f), hhi[:, f, :].bitcast(F32), ALU.subtract)\
                    .then_inc(s["ylo_ready"], 1)
            for i in range(B_OUT[0][1] + 1, NB):
                cut_lo(i)

        @block.scalar
        def _(act_e):
            V = nc.scalar.activation
            e = act_e
            chain = [0]

            def link(ins):
                chain[0] += 1
                ins.then_inc(s["act_chain"], 1)
                e.wait_ge(s["act_chain"], chain[0])

            def cut_hi(i):
                e.wait_ge(w_loaded[i % 2], 16 * (i // 2 + 1))
                if i >= 2:
                    passed(e, i - 2)
                V(wv(whi, i), wv(wraw, i), ACT.Copy).then_inc(s["w_hi_ready"], 1)

            def rstd(col, n=1, width=D_MODEL):
                link(V(stat[:, 1, col:col + n], stat[:, 0, col:col + n], ACT.Ln, bias=epsc[:, :], scale=1.0 / width))
                V(stat[:, 2, col:col + n], stat[:, 1, col:col + n], ACT.Exp, scale=-0.5).then_inc(s["rstd_ready"], 1)

            def hi_part(kind, n, dst):
                for g in range(2):
                    b = filled(e, (kind, n, g))
                    V(dst[:, 4 * g:4 * g + 4], quad(b), ACT.Copy).then_inc(s["h_hi_ready"], 1)

            LN_EXP = "natural_log_exp_and_others"
            e.preload_act_table_set(LN_EXP)
            e.wait_ge(s["consts"], 1)
            for n in range(2 + NT):
                e.wait_ge(s[f"x_loaded{n % 2}"], 16 * (n // 2 + 1))
                link(V(junk[:, :], xin[n % 2][:, :], ACT.Square, accum_out=stat[:, 0, n:n + 1]))
                rstd(n)
                if n >= 1:
                    hi_part("norm1", n - 1, dest1(n - 1, mhi, hhi))
                if n == 4:
                    cut_hi(0)
                    e.wait_ge(s["small_loaded"], 16 * SMALL_LOADS)
                    V(w8hi[:, :, :], w8raw[:, :, :], ACT.Copy).then_inc(s["w8_ready"], 1)
            hi_part("norm1", NT + 1, dest1(NT + 1, mhi, hhi))
            cut_hi(1)

            def silu(ct):
                e.wait_ge(s["conv_done"], ct + 1)
                V(qkvz[:, ct, :], qkvz[:, ct, :], ACT.Silu).then_inc(s["silu_done"], 1)

            def to_conv(ct, keys):
                t = cb[ct % 2]
                A0, B0 = filled(e, keys[0]), None
                V(t[:, PAD:PAD + HALF], bank[A0][:, 0:HALF], ACT.Copy).then_inc(bank_free[A0], 1)
                B0 = filled(e, keys[1])
                V(t[:, PAD + HALF:PAD + SEQ], bank[B0][:, 0:SEQ - HALF], ACT.Copy)
                V(conv_s(t)[:, :, PAD:], bank[B0][:, SEQ - HALF:HALF].rearrange("p (b t) -> p b t", b=DEC_BATCH),
                  ACT.Copy).then_inc(bank_free[B0], 1)

            def l2(c):
                for h in range(2):
                    b = filled(e, ("l2", c, h))
                    if c >= 2 and h == 0:
                        e.wait_ge(s["l2_done"], c - 1)
                    ins = V(rA[c % 2][:, h * HALF:(h + 1) * HALF], bank[b][:, 0:HALF], ACT.Ln, bias=epsc[:, :])
                    ins.then_inc(bank_free[b], 1)
                evacuated(e, ("l2", c, 1))
                V(rA[c % 2][:, :], rA[c % 2][:, :], ACT.Exp, scale=-0.5).then_inc(s["rinv_ready"], 1)

            for n in range(12):
                if n >= 1:
                    cut_hi(n + 1)
                if n == 8:
                    e.preload_act_table_set(LN_EXP)
                if n >= 8:
                    l2(2 * (n - 8))
                    l2(2 * (n - 8) + 1)
                for c in range(2):
                    ct = 2 * n + c
                    keys = [(("in", n), c, h) for h in range(2)]
                    if ct < 12:
                        if ct >= 2:
                            e.wait_ge(s["conv_done"], ct - 1)
                        to_conv(ct, keys)
                        if ct >= 1:
                            silu(ct - 1)
                    elif n not in (10,):
                        if ct == 12:
                            silu(11)
                        dst = qkvz[:, ct, :] if n < 8 else {8: yb, 9: scC, 11: cq}[n][:, c, :]
                        fn = ACT.Silu if n < 8 else ACT.Copy
                        for h in range(2):
                            b = filled(e, keys[h])
                            V(dst[:, h * HALF:(h + 1) * HALF], bank[b][:, 0:HALF], fn).then_inc(bank_free[b], 1)
            evacuated(e, ("gates", 2))
            e.wait_ge(s["gates_act"], 1)
            V(gtmp[:, 0], gba[:, :, 0:4], ACT.Exp, scale=-1.0)
            link(V(gtmp[:, 1], gtmp[:, 3], ACT.Abs))
            link(V(gtmp[:, 1], gtmp[:, 1], ACT.Exp, scale=-1.0))
            V(gtmp[:, 1], gtmp[:, 1], ACT.Ln, bias=ones[:, 0:1])
            V(nA[:, :], nA[:, :], ACT.Exp).then_inc(s["gates_act"], 1)
            cut_hi(13)
            for t in range(NT):
                if t == 0:
                    e.wait_ge(s["l2_done"], 8)
                b = filled(e, ("ck", 0, t))
                V(ckv[:, t, :], bank[b][:, :], ACT.Copy).then_inc(bank_free[b], 1)
            cut_hi(14)
            cut_hi(15)
            e.wait_ge(s["conv_done"], 14)
            for hp in range(2):
                for g, (c0, w) in enumerate(((0, SEQ), (SEQ, P))):
                    b = filled(e, ("kT", hp, g))
                    V(kT[:, hp, c0:c0 + w], bank[b][:, 0:w], ACT.Copy).then_inc(bank_free[b], 1)
            cut_hi(16)
            for t in range(2):
                b = filled(e, ("mk", 0, t))
                for h in range(HEADS):
                    ins = V(junk_mk[:, h, :], bank[b][:, h * P:(h + 1) * P], ACT.Square,
                            accum_out=stat[:, 0, 17 + 4 * t + h:18 + 4 * t + h])
                link(ins)
                rstd(17 + 4 * t, HEADS, DK)
            cut_hi(17)
            for t in range(2):
                b = filled(e, ("mv", 0, t))
                V(memv[:, t, :], bank[b][:, :], ACT.Copy).then_inc(bank_free[b], 1)
            cut_hi(18)
            cut_hi(19)
            for t in range(2):
                b = filled(e, ("memkT", t))
                V(memkT[:, :, t * P:(t + 1) * P], quad(b), ACT.Copy).then_inc(bank_free[b], 1)

            filled(e, ("mv", 0, 1))
            scale = SB_DH ** -0.5

            def sb_in(n):
                kind, x, i = SB_ITEMS[n]
                if kind == "s":
                    for b2 in range(2):
                        bt = 2 * x + b2
                        for hp in range(2):
                            if hp == 0 and b2 == 0:
                                if x == 0:
                                    e.wait_ge(s["out_mk"], 16)
                                else:
                                    filled(e, ("z", n - 1, 1))
                            b = filled(e, ("kc", bt, hp))
                            V(kTs[b2][:, hp, :], bank[b][:, :], ACT.Copy).then_inc(bank_free[b], 1)
                w = (i + 1) * P if kind == "p" else 640
                if n >= 2:
                    filled(e, ("AT", n - 2, at_banks(n - 2) - 1))
                for g, (c0, c1) in enumerate(((640 - w, 640),) if kind == "p" else ((0, 512), (512, 640))):
                    b = filled(e, ("z", n, g))
                    z = bank[b][:, 0:c1 - c0]
                    V(att_a[n % 2][:, c0:c1], z, ACT.Sigmoid, scale=scale)
                    V(att_m[n % 2][:, c0:c1], z, ACT.Sigmoid, scale=-scale).then_inc(bank_free[b], 1)

            def sb_turned(n):
                if n >= 2:
                    passed(e, ("av", n - 2))
                nb = SB_ITEMS[n][2] + 1 if SB_ITEMS[n][0] == "p" else 5
                for g in range(at_banks(n)):
                    b = filled(e, ("AT", n, g))
                    w = min(4, nb - 4 * g) * P
                    V(att_t[n % 2][:, 512 * g:512 * g + w], bank[b][:, 0:w], ACT.Copy).then_inc(bank_free[b], 1)

            sb_in(0)
            for n in range(NI):
                if n + 1 < NI:
                    sb_in(n + 1)
                sb_turned(n)
                if n in (8, 16):
                    hp = n // 8 - 1
                    b = filled(e, ("oc", hp))
                    V(yc[:, hp, 0:SEQ], bank[b][:, :], ACT.Copy).then_inc(bank_free[b], 1)
            b = filled(e, ("oc", 2))
            for h2 in range(2):
                r = slice(64 * h2, 64 * h2 + 64)
                for hp in range(2):
                    src = bank[b][r, 256 * hp:256 * hp + 256].rearrange("p (b q t) -> p b q t", b=DEC_BATCH, q=2)[:, :, h2, :]
                    ins = V(yc[r, hp, SEQ:TOK].rearrange("p (b t) -> p b t", b=DEC_BATCH), src, ACT.Copy)
            ins.then_inc(bank_free[b], 1)

            e.preload_act_table_set(LN_EXP)
            for i in range(NT):
                e.wait_ge(s["dif_ready"], 2 * i + 1)
                V(kdec[:, i, :], gcs[:, i, 2, :], ACT.Exp)
                V(bege[:, i, :], gcs[:, i, 0, :], ACT.Exp).then_inc(s["small_exp"], 1)
                e.wait_ge(s["dif_ready"], 2 * i + 2)
                V(scr[4 + i % 2][:, :, :], scr[4 + i % 2][:, :, :], ACT.Exp).then_inc(s["dt_ready"], 1)
                if i >= 2:
                    e.wait_ge(s["lt_ready"], i - 1)
                b = filled(e, ("grow", i))
                V(scr[6 + i % 2][:, :, :], quad(b), ACT.Exp).then_inc(bank_free[b], 1)

            def to_x(l, i):
                b = filled(e, ("X", l, i))
                V(XY[:, i, :, :], quad(b), ACT.Copy).then_inc(bank_free[b], 1)

            for i in range(NT):
                to_x(0, i)
            for l in range(1, LEVELS):
                for i in TILES_AT[l]:
                    b = filled(e, ("Y", l, i))
                    V(XY[:, i, :, :], quad(b), ACT.Copy).then_inc(bank_free[b], 1)
                if l < LEVELS - 1:
                    for i in TILES_AT[l + 1]:
                        to_x(l, i)
            for i in range(NT):
                b = filled(e, ("wT", i))
                V(scr[6 + i % 2][:, :, :], quad(b), ACT.Copy, scale=-1.0).then_inc(bank_free[b], 1)
                if i == PT:
                    b = filled(e, ("ws", 0))
                    V(scr[7][:, :, :], quad(b), ACT.Copy).then_inc(bank_free[b], 1)
                b = filled(e, ("vn", i))
                if i >= 2:
                    filled(e, ("dS", i - 2))
                V(scr[8 + i % 2][:, :, :], quad(b), ACT.Copy).then_inc(bank_free[b], 1)
                b = filled(e, ("o", i))
                V(qkvz[:, 0:HEADS, i * P:(i + 1) * P], quad(b), ACT.Copy).then_inc(bank_free[b], 1)

            for f in range(8):
                if f >= 2:
                    e.wait_ge(s["y_ready"], f - 1)
                for h in range(2):
                    b = filled(e, ("gn", f, h))
                    V(rG[f % 2][:, h * HALF:(h + 1) * HALF], bank[b][:, 0:HALF], ACT.Ln, bias=epsc[:, :],
                      scale=1.0 / (DK if f < 4 else SB_DH)).then_inc(bank_free[b], 1)
                evacuated(e, ("gn", f, 1))
                V(rG[f % 2][:, :], rG[f % 2][:, :], ACT.Exp, scale=-0.5).then_inc(s["rf_ready"], 1)
                if f == 0:
                    e.wait_ge(s["out_pstate"], 16)
                    e.wait_ge(s["out_sstate"], 16 * DEC_BATCH)
                if f >= 1:
                    e.wait_ge(s["y_ready"], f)
                    V(hhi[:, f - 1, :], mixed(f - 1), ACT.Copy).then_inc(s["yhi_ready"], 1)
            e.wait_ge(s["y_ready"], 8)
            V(hhi[:, 7, :], mixed(7), ACT.Copy).then_inc(s["yhi_ready"], 1)


            def square_rows(n, base, name, junk):
                for half in range(2):
                    evacuated(e, (name, half, n))
                link(V(junk[:, :], xres[:, n, :], ACT.Square, accum_out=stat[:, 0, base + n:base + n + 1]))
                rstd(base + n)

            def norm_hi(kind, n):
                hi_part(kind, n, hhi[:, :, n * P:(n + 1) * P])

            cut_hi(20)
            cut_hi(21)
            for n in range(NT):
                square_rows(n, 7, "out", junk2)
                if n >= 1:
                    norm_hi("norm2", n - 1)
            norm_hi("norm2", PT)
            cut_hi(22)
            cut_hi(23)
            for n in range(2):
                for c in range(2):
                    for h in range(2):
                        b = filled(e, (("mq", n), c, h))
                        V(qm[:, 2 * n + c, h * HALF:(h + 1) * HALF], bank[b][:, 0:HALF], ACT.Copy)\
                            .then_inc(bank_free[b], 1)
            for h in range(HEADS):
                if h >= 2:
                    e.wait_ge(s["qm_ready"], h - 1)
                for g in range(2):
                    b = filled(e, ("mqn", h, g))
                    V(rM[h % 2][:, g * HALF:(g + 1) * HALF], bank[b][:, 0:HALF], ACT.Ln, bias=epsc[:, :], scale=1.0 / DK)\
                        .then_inc(bank_free[b], 1)
                evacuated(e, ("mqn", h, 1))
                V(rM[h % 2][:, :], rM[h % 2][:, :], ACT.Exp, scale=-0.5).then_inc(s["qr_ready"], 1)
            cut_hi(24)
            cut_hi(25)

            mscale = DK ** -0.5

            def soft(i):
                e.wait_ge(s["max_ready"], i + 1)
                if i >= 2:
                    filled(e, ("pT", i - 2, 1))
                for h in range(HEADS):
                    b = filled(e, ("ms", i, h // 2)) if h % 2 == 0 else b
                    ins = V(probs[i % 2][:, h, :], bank[b][:, (h % 2) * N_MEM:(h % 2 + 1) * N_MEM], ACT.Exp,
                            bias=mstat[:, 1, i, h:h + 1], scale=mscale, accum_out=mstat[:, 2, i, h:h + 1])
                    if h % 2:
                        ins.then_inc(bank_free[b], 1)

            def prob_turned(i):
                if i >= 2:
                    filled(e, ("om", i - 2))
                for g in range(2):
                    b = filled(e, ("pT", i, g))
                    V(probT[i % 2][:, 2 * g:2 * g + 2, :, :].rearrange("p h n t -> p (h n t)"), bank[b][:, :], ACT.Copy)\
                        .then_inc(bank_free[b], 1)

            def om_part(i):
                b = filled(e, ("om", i))
                V(omhi[:, :, i * P:(i + 1) * P], quad(b), ACT.Copy).then_inc(s["om_hi"], 1)

            def sample_keys(bt):
                if bt >= 2:
                    passed(e, ("sT", bt - 2))
                b = filled(e, ("km", bt, 0))
                V(kmT[bt % 2][:, :, 0:P], quad(b), ACT.Copy).then_inc(bank_free[b], 1)

            soft(0)
            for i in range(PT):
                if i + 1 < PT:
                    soft(i + 1)
                sample_keys(2 * i)
                prob_turned(i)
                sample_keys(2 * i + 1)
                if i >= 1:
                    om_part(i - 1)
            om_part(PT - 1)
            b = filled(e, ("sT", 0))
            V(stsb[:, 0, :, :], quad(b), ACT.Copy).then_inc(bank_free[b], 1)
            soft(PT)
            square_rows(0, 12, "mo", junk3)
            prob_turned(PT)
            square_rows(1, 12, "mo", junk3)
            om_part(PT)
            norm_hi("norm3", 0)
            norm_hi("norm3", 1)
            square_rows(2, 12, "mo", junk3)
            square_rows(3, 12, "mo", junk3)
            norm_hi("norm3", 2)
            square_rows(4, 12, "mo", junk3)
            cut_hi(26)
            norm_hi("norm3", 3)
            norm_hi("norm3", 4)
            cut_hi(27)

            for j in range(FT // 2):
                for c in range(2):
                    ct = 2 * j + c
                    if ct >= 2:
                        e.wait_ge(s["ffn_conv"], ct - 1)
                    to_conv(ct, [(("gate", j), c, h) for h in range(2)])
                cut_hi(28 + 2 * j)
                for c in range(2):
                    ct = 2 * j + c
                    e.wait_ge(s["ffn_conv"], ct + 1)
                    V(act[:, ct, :], act[:, ct, :], ACT.Silu).then_inc(s["ffn_silu"], 1)
                cut_hi(29 + 2 * j)
            nxt = B_DN[0][0] + 2
            for n in range(2 * FT):
                half, k = divmod(n, FT)
                if n >= KD:
                    passed(e, ("dn",) + divmod(n - KD, FT))
                else:
                    filled(e, (("up", FT // 2 - 1), 1, 1))
                evacuated(e, (("up", k // 2), k % 2, 0))
                evacuated(e, (("up", k // 2), k % 2, 1))
                V(hhi[:, n % KD, :], act[:, k, :], ACT.Copy).then_inc(s["ahi_ready"], 1)
                if n % 4 == 3 and n >= KD and nxt < NB:
                    cut_hi(nxt)
                    nxt += 1
            while nxt < NB:
                cut_hi(nxt)
                nxt += 1

        @block.vector
        def _(dve):
            V = nc.vector
            chain = [0]

            def link(ins):
                chain[0] += 1
                ins.then_inc(s["dve_chain"], 1)
                dve.wait_ge(s["dve_chain"], chain[0])

            for t in cb:
                V.memset(t[:, 0:PAD], 0.0)
            b = filled(dve, ("cache", 0))
            V.tensor_copy(flat(cacheT), bank[b][:, 0:288])
            V.tensor_copy(flat(cacheS), bank[b][:, 288:320]).then_inc(bank_free[b], 1)

            def lo_part(kind, n, hi, lo):
                for g in range(2):
                    lo_part.count += 1
                    dve.wait_ge(s["h_hi_ready"], lo_part.count)
                    b, _ = use[(kind, n, g)]
                    V.tensor_tensor(lo[:, 4 * g:4 * g + 4], quad(b), hi[:, 4 * g:4 * g + 4].bitcast(F32), ALU.subtract)\
                        .then_inc(bank_free[b], 1)
            lo_part.count = 0
            dve.wait_ge(s["small_loaded"], 16 * SMALL_LOADS)
            for n in range(2 + NT):
                dve.wait_ge(s["rstd_ready"], n + 1)
                if n >= 2:
                    filled(dve, ("norm1", n - 2, 1))
                V.scalar_tensor_tensor(out=xn[n % 2][:, :], in0=xin[n % 2][:, :], scalar=stat[:, 2, n:n + 1],
                                       in1=(gmin if n < 2 else gmix)[:, :], op0=ALU.mult, op1=ALU.mult)\
                    .then_inc(s["xn_ready"], 1)
                if n >= 1:
                    lo_part("norm1", n - 1, dest1(n - 1, mhi, hhi), dest1(n - 1, mlo, hlo))
            lo_part("norm1", NT + 1, dest1(NT + 1, mhi, hhi), dest1(NT + 1, mlo, hlo))

            def conv(t, out, w, taps, state, npads):
                first = PAD + 1 - taps
                ts, os = conv_s(t), out[:, SEQ:TOK].rearrange("p (b t) -> p b t", b=DEC_BATCH)
                keep_n = taps - 1
                V.tensor_copy(state[:, 0:keep_n], t[:, PAD + SEQ - keep_n:PAD + SEQ])
                V.tensor_copy(state[:, keep_n:].rearrange("p (b t) -> p b t", b=DEC_BATCH),
                              ts[:, :, PAD + DEC_SEQ - keep_n:])
                for k in range(taps):
                    a, bb = t[:, first + k:first + k + SEQ], ts[:, :, first + k:first + k + DEC_SEQ]
                    if k == 0:
                        V.tensor_scalar(out[:, 0:SEQ], a, w[:, 0:1], None, ALU.mult)
                        ins = V.tensor_scalar(os, bb, w[:, 0:1], None, ALU.mult)
                    else:
                        V.scalar_tensor_tensor(out=out[:, 0:SEQ], in0=a, scalar=w[:, k:k + 1], in1=out[:, 0:SEQ],
                                               op0=ALU.mult, op1=ALU.add)
                        ins = V.scalar_tensor_tensor(out=os, in0=bb, scalar=w[:, k:k + 1], in1=os,
                                                     op0=ALU.mult, op1=ALU.add)
                    if k < taps - 1:
                        link(ins)
                return ins

            def pads(t, cache, n):
                link(V.tensor_copy(conv_s(t)[:, :, PAD - n:PAD], cache.rearrange("p (b t) -> p b t", b=DEC_BATCH)))

            for h in range(2):
                b = filled(dve, ("gates", h))
                V.tensor_copy(gT[:, h * HALF:(h + 1) * HALF], bank[b][0:8, 0:HALF]).then_inc(bank_free[b], 1)

            for ct in range(12):
                if ct == 2:
                    b = filled(dve, ("gates", 2))
                    V.tensor_copy(flat(gba), bank[b][:, 0:8 * NT]).then_inc(bank_free[b], 1)
                keys = [(("in", ct // 2), ct % 2, h) for h in range(2)]
                t = cb[ct % 2]
                pads(t, cacheT[:, ct, :], 3)
                evacuated(dve, keys[0])
                evacuated(dve, keys[1])
                conv(t, qkvz[:, ct, :], gcw[:, ct, :], 4, cst[:, ct, :], 3).then_inc(s["conv_done"], 1)

            def square(c):
                dve.wait_ge(s["silu_done"], c + 1)
                if c >= 2:
                    filled(dve, ("l2", c - 2, 1))
                V.tensor_tensor(sqA[c % 2][:, :], qkvz[:, c, :], qkvz[:, c, :], ALU.mult).then_inc(s["sq_ready"], 1)

            def unit(c):
                dve.wait_ge(s["rinv_ready"], c + 1)
                V.scalar_tensor_tensor(out=qkvz[:, c, :], in0=qkvz[:, c, :], scalar=DK ** -0.5 if c < 4 else 1.0,
                                       in1=rA[c % 2][:, :], op0=ALU.mult, op1=ALU.mult).then_inc(s["l2_done"], 1)

            def short_conv(c):
                keys = [(("in", 10), c, h) for h in range(2)]
                t = cb[c]
                pads(t, cacheS[:, c, :], 2)
                for h in range(2):
                    evacuated(dve, (("in", 9), c, h))
                    evacuated(dve, (("in", 8), c, h))
                b = filled(dve, keys[0])
                V.tensor_tensor(t[:, PAD:PAD + HALF], bank[b][:, 0:HALF], scC[:, c, 0:HALF], ALU.mult)\
                    .then_inc(bank_free[b], 1)
                b = filled(dve, keys[1])
                V.tensor_tensor(t[:, PAD + HALF:PAD + SEQ], bank[b][:, 0:SEQ - HALF], scC[:, c, HALF:SEQ], ALU.mult)
                V.tensor_tensor(conv_s(t)[:, :, PAD:], bank[b][:, SEQ - HALF:HALF].rearrange("p (b t) -> p b t", b=DEC_BATCH),
                                scC[:, c, SEQ:TOK].rearrange("p (b t) -> p b t", b=DEC_BATCH), ALU.mult)\
                    .then_inc(bank_free[b], 1)
                evacuated(dve, keys[0])
                evacuated(dve, keys[1])
                link(conv(t, scC[:, c, :], scw[:, c, :], 3, scst[:, c, :], 2))
                V.tensor_tensor(yb[:, c, :], yb[:, c, :], scC[:, c, :], ALU.mult).then_inc(s["conv_done"], 1)
            square(0)
            square(1)
            for c in range(8):
                unit(c)
                if c + 2 < 8:
                    square(c + 2)
                if c == 5:
                    short_conv(0)
                    short_conv(1)
            evacuated(dve, ("gates", 2))
            V.tensor_tensor(gtmp[:, 3], gba[:, :, 4:8], spread(dtb[:, :], 1, [P, NT, HEADS]), ALU.add)\
                .then_inc(s["gates_act"], 1)
            dve.wait_ge(s["gates_act"], 2)
            link(V.tensor_scalar(gtmp[:, 0], gtmp[:, 0], 1.0, None, ALU.add))
            V.reciprocal(beta[:, :, :], gtmp[:, 0])
            link(V.tensor_scalar(gtmp[:, 2], gtmp[:, 3], 0.0, None, ALU.max))
            link(V.tensor_tensor(gtmp[:, 2], gtmp[:, 2], gtmp[:, 1], ALU.add))
            V.scalar_tensor_tensor(out=gdec[:, :, :], in0=gtmp[:, 2], scalar=-1.0, in1=spread(nA[:, :], 1, [P, NT, HEADS]),
                                   op0=ALU.mult, op1=ALU.mult).then_inc(s["gates"], 1)
            for t in range(2):
                dve.wait_ge(s["rstd_ready"], 2 + NT + t + 1)
                b = filled(dve, ("mk", 0, t))
                for h in range(HEADS):
                    ins = V.scalar_tensor_tensor(out=mkout[:, t, h * P:(h + 1) * P], in0=bank[b][:, h * P:(h + 1) * P],
                                                 scalar=stat[:, 2, 17 + 4 * t + h:18 + 4 * t + h], in1=gmk[:, :],
                                                 op0=ALU.mult, op1=ALU.mult)
                ins.then_inc(bank_free[b], 1)
            for g in range(3):
                b = filled(dve, ("strow", g))
                V.tensor_copy(strow[:, g * 512:(g + 1) * 512], bank[b][0:27, :]).then_inc(bank_free[b], 1)
            b = filled(dve, ("strow", 3))
            V.tensor_copy(scsrow[:, :], bank[b][0:18, 0:SC_DIM]).then_inc(bank_free[b], 1)

            filled(dve, ("mv", 0, 1))
            link(V.memset(qbl[:, :, :, :], 0.0))
            for t in att_m:
                V.memset(t[:, 640:641], 1.0)
            for c in range(2):
                for h in range(2):
                    evacuated(dve, (("in", 11), c, h))
            for h2 in range(2):
                r = slice(64 * h2, 64 * h2 + 64)
                ins = V.tensor_copy(qbl[r, :, :, 16 * h2:16 * h2 + 16],
                                    cq[r, :, SEQ:TOK].rearrange("p a (b t) -> p a b t", b=DEC_BATCH))
            ins.then_inc(s["q_blocks"], 1)
            for n in range(NI):
                kind, x, i = SB_ITEMS[n]
                w = (i + 1) * P if kind == "p" else 640
                for g in range(1 if kind == "p" else 2):
                    evacuated(dve, ("z", n, g))
                a, m = att_a[n % 2], att_m[n % 2]
                if kind == "s":
                    c = 96 - 32 * x
                    V.tensor_tensor(a[:, 512:640], a[:, 512:640], newm[:, c:c + P], ALU.mult)
                    link(V.tensor_tensor(m[:, 512:640], m[:, 512:640], newi[:, c:c + P], ALU.max))
                mr = m[:, 640 - w:640][:, ::-1]
                link(V.tensor_tensor_scan(mr, mr, ones[:, 0:1].to_broadcast([P, w]), 1.0, ALU.mult, ALU.mult))
                V.tensor_tensor(a[:, 640 - w:640], a[:, 640 - w:640], m[:, 641 - w:641], ALU.mult)\
                    .then_inc(s["A_ready"], 1)

            passed(dve, ("av", NI - 1))
            for i in range(NT):
                tt = slice(i * P, (i + 1) * P)
                b = filled(dve, ("gcol", i))
                V.tensor_copy(gcs[:, i, 0:2, :].rearrange("p a h -> p (a h)"), bank[b][:, 0:8]).then_inc(bank_free[b], 1)
                evacuated(dve, ("gcol", i))
                V.tensor_tensor(gcs[:, i, 2, :], gcs[:, i, 1, :], gcs[:, i, 0, :], ALU.subtract).then_inc(s["dif_ready"], 1)
                b = filled(dve, ("grow", i))
                if i >= 2:
                    dve.wait_ge(s["dtu_ready"], i - 1)
                for h in range(HEADS):
                    ins = V.tensor_scalar(scr[4 + i % 2][:, h, :], bank[b][:, h * P:(h + 1) * P], gcs[:, i, 0, h:h + 1], 0.0,
                                          ALU.subtract, ALU.min)
                ins.then_inc(s["dif_ready"], 1)
                dve.wait_ge(s["small_exp"], i + 1)
                V.tensor_tensor(bege[:, i, :], bege[:, i, :], beta[:, i, :], ALU.mult)
                dve.wait_ge(s["dtu_ready"], i + 1)
                d = scr[8 + i % 2][:, :, :]
                b = filled(dve, ("qk", i))
                V.tensor_tensor(qkD[:, i, :, :], quad(b), d, ALU.mult).then_inc(bank_free[b], 1)
                b = filled(dve, ("kk", i))
                V.tensor_tensor(LT[:, i, :, :], quad(b), d, ALU.mult).then_inc(bank_free[b], 1)
                evacuated(dve, ("kk", i))
                b = filled(dve, ("brow", i))
                V.tensor_tensor(LT[:, i, :, :], LT[:, i, :, :], quad(b), ALU.mult).then_inc(bank_free[b], 1)
                evacuated(dve, ("grow", i))
                er = scr[6 + i % 2]
                if i < PT:
                    V.tensor_copy(etot[:, i, :], er[:, :, P - 1])
                else:
                    V.tensor_copy(etotS[:, :, :], er[:, :, :].rearrange("p h (b t) -> p h b t", b=DEC_BATCH)[:, :, :, DEC_SEQ - 1])
                V.tensor_tensor(qkvz[:, 0:HEADS, tt], qkvz[:, 0:HEADS, tt], er[:, :, :], ALU.mult).then_inc(s["lt_ready"], 1)
            for l in range(1, LEVELS):
                for i in TILES_AT[l]:
                    b = filled(dve, ("dX", l, i))
                    V.tensor_tensor(XT[:, i, :, :], XT[:, i, :, :], quad(b), ALU.subtract).then_inc(bank_free[b], 1)
            for i in range(NT):
                b = filled(dve, ("Vt", i))
                if i >= 2:
                    filled(dve, ("dS", i - 2))
                V.tensor_tensor(scr[i % 2][:, :, :], quad(b), spread(beta[:, i, :], 2, [P, HEADS, P]), ALU.mult)\
                    .then_inc(bank_free[b], 1)
                b = filled(dve, ("Kt", i))
                V.tensor_tensor(scr[2 + i % 2][:, :, :], quad(b), spread(bege[:, i, :], 2, [P, HEADS, P]), ALU.mult)\
                    .then_inc(s["kd_ready"], 1)
                V.tensor_tensor(scr[4 + i % 2][:, :, :], quad(b), spread(kdec[:, i, :], 2, [P, HEADS, P]), ALU.mult)\
                    .then_inc(bank_free[b], 1)
                if i < PT:
                    b = filled(dve, ("dS", i))
                    if i == 0:
                        V.tensor_copy(stP[:, :, :], quad(b)).then_inc(bank_free[b], 1)
                        evacuated(dve, ("dS", 0))
                    else:
                        for h in range(HEADS):
                            ins = V.scalar_tensor_tensor(out=stP[:, h, :], in0=stP[:, h, :], scalar=etot[:, i, h:h + 1],
                                                         in1=bank[b][:, h * P:(h + 1) * P], op0=ALU.mult, op1=ALU.add)
                        ins.then_inc(bank_free[b], 1)
                        evacuated(dve, ("dS", i))
            for h in range(HEADS):
                for g in range(2):
                    b = filled(dve, ("dSs", h, g))
                    for j in range(4):
                        bt = 4 * g + j
                        ins = V.scalar_tensor_tensor(out=stS[:, bt, h, :], in0=stS[:, bt, h, :], scalar=etotS[:, h, bt:bt + 1],
                                                     in1=bank[b][:, j * P:(j + 1) * P], op0=ALU.mult, op1=ALU.add)
                    ins.then_inc(bank_free[b], 1)

            for i in range(NT):
                evacuated(dve, ("o", i))

            def group_square(f):
                if f == 6:
                    evacuated(dve, ("oc", 0))
                    evacuated(dve, ("oc", 1))
                    evacuated(dve, ("oc", 2))
                if f >= 2:
                    filled(dve, ("gn", f - 2, 1))
                V.tensor_tensor(sqG[f % 2][:, :], mixed(f), mixed(f), ALU.mult).then_inc(s["sqf_ready"], 1)

            group_square(0)
            group_square(1)
            for f in range(8):
                dve.wait_ge(s["rf_ready"], f + 1)
                ins = V.scalar_tensor_tensor(out=mixed(f), in0=mixed(f), scalar=gout[:, 0:1] if f < 4 else gout[:, f:f + 1],
                                             in1=rG[f % 2][:, :], op0=ALU.mult, op1=ALU.mult)
                if f < 4:
                    link(ins)
                    ins = V.tensor_tensor(mixed(f), mixed(f), qkvz[:, 12 + f, :], ALU.mult)
                ins.then_inc(s["y_ready"], 1)
                if f + 2 < 8:
                    group_square(f + 2)

            def add_res(name, half, t):
                b = filled(dve, (name, half, t))
                c = slice(512 * half, 512 * half + 512)
                V.tensor_tensor(xres[:, t, c], xres[:, t, c], bank[b][:, :], ALU.add).then_inc(bank_free[b], 1)

            def scaled_rows(kind, n, base, g, xn):
                evacuated(dve, ({"norm2": "out", "norm3": "mo"}[kind], 1, n))
                dve.wait_ge(s["rstd_ready"], {"norm2": 10, "norm3": 15}[kind] + n)
                if n >= 2:
                    filled(dve, (kind, n - 2, 1))
                V.scalar_tensor_tensor(out=xn[n % 2][:, :], in0=xres[:, n, :], scalar=stat[:, 2, base + n:base + n + 1],
                                       in1=g[:, :], op0=ALU.mult, op1=ALU.mult).then_inc(s["xn_ready"], 1)

            def norm_lo(kind, n):
                c = slice(n * P, (n + 1) * P)
                lo_part(kind, n, hhi[:, :, c], hlo[:, :, c])

            dve.wait_ge(s["xres_loaded"], 32)
            for n in range(NT):
                add_res("out", 0, n)
            dve.wait_ge(s["gm_loaded"], 16)
            for n in range(NT):
                add_res("out", 1, n)
                scaled_rows("norm2", n, 7, gmem, xn2)
                if n >= 1:
                    norm_lo("norm2", n - 1)
            norm_lo("norm2", PT)

            def q_square(h):
                for g in range(2):
                    evacuated(dve, (("mq", h // 2), h % 2, g))
                if h >= 2:
                    filled(dve, ("mqn", h - 2, 1))
                V.tensor_tensor(sqM[h % 2][:, :], qm[:, h, :], qm[:, h, :], ALU.mult).then_inc(s["qsq_ready"], 1)
            q_square(0)
            q_square(1)
            for h in range(HEADS):
                dve.wait_ge(s["qr_ready"], h + 1)
                V.scalar_tensor_tensor(out=qm[:, h, :], in0=qm[:, h, :], scalar=gmq[:, :], in1=rM[h % 2][:, :],
                                       op0=ALU.mult, op1=ALU.mult).then_inc(s["qm_ready"], 1)
                if h + 2 < HEADS:
                    q_square(h + 2)

            mscale = DK ** -0.5

            def soft_max(i):
                for g in range(2):
                    b = filled(dve, ("ms", i, g))
                    ins = V.tensor_reduce(mstat[:, 0, i, 2 * g:2 * g + 2],
                                          bank[b][:, :].rearrange("p (h n) -> p h n", h=2), AX.X, ALU.max)
                link(ins)
                V.tensor_scalar(mstat[:, 1, i, :], mstat[:, 0, i, :], -mscale, None, ALU.mult).then_inc(s["max_ready"], 1)

            def soft_norm(i):
                for g in range(2):
                    evacuated(dve, ("ms", i, g))
                link(V.reciprocal(mstat[:, 3, i, :], mstat[:, 2, i, :]))
                for h in range(HEADS):
                    ins = V.tensor_scalar(probs[i % 2][:, h, :], probs[i % 2][:, h, :], mstat[:, 3, i, h:h + 1], None, ALU.mult)
                ins.then_inc(s["prob_ready"], 1)

            def om_part(i):
                dve.wait_ge(s["om_hi"], i + 1)
                b, _ = use[("om", i)]
                c = slice(i * P, (i + 1) * P)
                V.tensor_tensor(omlo[:, :, c], quad(b), omhi[:, :, c].bitcast(F32), ALU.subtract).then_inc(bank_free[b], 1)

            def sample_keys(bt):
                if bt >= 2:
                    passed(dve, ("sT", bt - 2))
                b = filled(dve, ("km", bt, 1))
                V.tensor_copy(kmT[bt % 2][:, :, P:N_MEM], quad(b)).then_inc(bank_free[b], 1)

            soft_max(0)
            soft_norm(0)
            for i in range(PT):
                if i + 1 < PT:
                    soft_max(i + 1)
                sample_keys(2 * i)
                if i + 1 < PT:
                    soft_norm(i + 1)
                sample_keys(2 * i + 1)
                if i >= 1:
                    om_part(i - 1)
            om_part(PT - 1)
            b = filled(dve, ("sT", 1))
            V.tensor_copy(stsb[:, 1, :, :], quad(b)).then_inc(bank_free[b], 1)
            soft_max(PT)
            soft_norm(PT)

            def add_mem(n):
                add_res("mo", 0, n)
                add_res("mo", 1, n)

            dve.wait_ge(s["gm_loaded"], 32)
            add_mem(0)
            scaled_rows("norm3", 0, 12, gffn, xn3)
            add_mem(1)
            scaled_rows("norm3", 1, 12, gffn, xn3)
            add_mem(2)
            om_part(PT)
            norm_lo("norm3", 0)
            norm_lo("norm3", 1)
            scaled_rows("norm3", 2, 12, gffn, xn3)
            add_mem(3)
            scaled_rows("norm3", 3, 12, gffn, xn3)
            norm_lo("norm3", 2)
            add_mem(4)
            scaled_rows("norm3", 4, 12, gffn, xn3)
            for t in cb:
                ins = V.memset(t[:, 0:PAD], 0.0)
            link(ins)
            norm_lo("norm3", 3)
            norm_lo("norm3", 4)
            dve.wait_ge(s["f_loaded"], 64)
            b = filled(dve, ("cacheF", 0))
            V.tensor_copy(flat(cacheF), bank[b][:, 0:16 * FT]).then_inc(bank_free[b], 1)
            evacuated(dve, ("cacheF", 0))
            for j in range(FT // 2):
                for c in range(2):
                    ct = 2 * j + c
                    t = cb[ct % 2]
                    pads(t, cacheF[:, ct, :], 2)
                    for h in range(2):
                        evacuated(dve, (("gate", j), c, h))
                    conv(t, act[:, ct, :], fcw[:, ct, :], 3, fcst[:, ct, :], 2).then_inc(s["ffn_conv"], 1)
                for c in range(2):
                    ct = 2 * j + c
                    dve.wait_ge(s["ffn_silu"], ct + 1)
                    for h in range(2):
                        b = filled(dve, (("up", j), c, h))
                        hs = slice(h * HALF, (h + 1) * HALF)
                        V.tensor_tensor(act[:, ct, hs], act[:, ct, hs], bank[b][:, 0:HALF], ALU.mult).then_inc(bank_free[b], 1)

            def act_lo(n):
                half, k = divmod(n, FT)
                dve.wait_ge(s["ahi_ready"], n + 1)
                V.tensor_tensor(hlo[:, n % KD, :], act[:, k, :], hhi[:, n % KD, :].bitcast(F32), ALU.subtract)\
                    .then_inc(s["alo_ready"], 1)
            for n in range(FT + 4):
                act_lo(n)
            for n in range(NT):
                add_res("dn", 0, n)
            for g in range(6):
                b = filled(dve, ("frow", g))
                w = min(4, FT - 4 * g) * P
                V.tensor_copy(fsrow[:, 512 * g:512 * g + w], bank[b][0:18, 0:w]).then_inc(bank_free[b], 1)
            for n in range(FT + 4, 2 * FT):
                act_lo(n)
            for n in range(NT):
                add_res("dn", 1, n)


_INS = ["x_prompt", "x_sample", "mem_prompt", "state_gdn", "cache_gdn_conv", "cache_sc_conv", "cache_sb_k", "cache_sb_v",
        "cache_mem_k", "cache_mem_v", "cache_ffn_conv", "norm_mix_g", "w_in", "gdn_conv_w", "gdn_A_log", "gdn_dt_bias",
        "gdn_norm_g", "sc_conv_w", "sc_norm_g", "sb_norm_g", "w_mix_out", "norm_mem_g", "mem_in_norm_g", "w_mq", "w_mk",
        "w_mv", "mq_norm_g", "mk_norm_g", "w_mo", "norm_ffn_g", "w_gate", "w_up", "ffn_conv_w", "w_down"]
_SHAPES = {"x_prompt": (512, 1024), "x_sample": (128, 1024), "mem_prompt": (256, 1024), "state_gdn": (8, 4, 128, 128),
           "cache_gdn_conv": (8, 3, 1536), "cache_sc_conv": (8, 2, 256), "cache_sb_k": (8, 512, 256),
           "cache_sb_v": (8, 512, 256), "cache_mem_k": (8, 256, 512), "cache_mem_v": (8, 256, 512),
           "cache_ffn_conv": (8, 2, 2816)}
_OUTS = [("y_prompt", (512, 1024), (1, 512, 1024)), ("y_sample", (128, 1024), (8, 16, 1024)),
         ("p_gdn_state", (4, 128, 128), (1, 1, 4, 128, 128)), ("p_gdn_conv", (3, 1536), (1, 1, 3, 1536)),
         ("p_sc_conv", (2, 256), (1, 1, 2, 256)), ("p_sb_k", (512, 256), (1, 1, 512, 4, 64)),
         ("p_sb_v", (512, 256), (1, 1, 512, 4, 64)), ("p_mem_k", (256, 512), (1, 1, 256, 4, 128)),
         ("p_mem_v", (256, 512), (1, 1, 256, 4, 128)), ("p_ffn_conv", (2, 2816), (1, 1, 2, 2816)),
         ("s_gdn_state", (8, 4, 128, 128), (1, 8, 4, 128, 128)), ("s_gdn_conv", (24, 1536), (1, 8, 3, 1536)),
         ("s_sc_conv", (16, 256), (1, 8, 2, 256)), ("s_sb_k", (128, 256), (1, 8, 16, 4, 64)),
         ("s_sb_v", (128, 256), (1, 8, 16, 4, 64)), ("s_ffn_conv", (16, 2816), (1, 8, 2, 2816))]


def kernel(**inputs):
    import numpy as _np
    import concourse.bacc as _bacc
    from concourse.bass_utils import run_bass_kernel_spmd as _run

    nc = _bacc.Bacc("TRN2", target_bir_lowering=False, num_devices=1)
    arrays, A, O = {}, {}, {}
    for name in _INS:
        a = _np.ascontiguousarray(inputs[name])
        a = a.reshape(_SHAPES.get(name, a.shape[1:]))
        arrays[f"in_{name}"] = a
        A[name] = nc.dram_tensor(f"in_{name}", a.shape, F32, kind="ExternalInput").ap()
    for name, shape, _ in _OUTS:
        O[name] = nc.dram_tensor(f"out_{name}", shape, F32, kind="ExternalOutput").ap()
    hybrid_step(nc, A, O)
    r = _run(nc, [arrays], core_ids=[0])
    return tuple(r.results[0][f"out_{name}"].reshape(shape) for name, _, shape in _OUTS)
```

```python
import concourse.bass as bass
from concourse import mybir
from contextlib import ExitStack

F32 = mybir.dt.float32
F32R = mybir.dt.float32r
ALU = mybir.AluOpType
ACT = mybir.ActivationFunctionType
AX = mybir.AxisListType

P = 128
D_MODEL, SEQ, DEC_BATCH, DEC_SEQ, PAST_LEN = 1024, 512, 8, 16, 512
KD = D_MODEL // P
TOK = SEQ + DEC_BATCH * DEC_SEQ
PT = SEQ // P
NT = TOK // P
HALF = TOK // 2
N_MEM, EPS = 256, 1e-6
HEADS, DK = 4, 128
GDN_DIM = 3 * HEADS * DK
SC_DIM, SB_W, SB_DH = 256, 256, 64
D_IN = 3592
D_FF = 2816
FT = D_FF // P
GAB = 2048
SCOL = GAB + 2 * HEADS
CKCOL = SCOL + 3 * SC_DIM + SB_W
PAD = 3
NEG = -1.0e30
RING = 6
BLK = 2048
LEVELS = 7
XIN = 4
SAMPLE_LEVELS = 4

ARENA = 16512
R0 = ARENA
R1 = R0 + NT * D_MODEL * 4
R2 = R1 + 2 * KD * TOK * 4
R3 = R2 + 6 * BLK * 4
R5 = R3 + FT * TOK * 4


def hybrid_step(nc, A, O):
    ctx = ExitStack()
    with ctx:
        at_r5 = [R5]

        def at(name, shape, offset, dt=F32):
            return nc.alloc_sbuf_tensor_at(name, shape, dt, offset=offset)

        def keep(name, shape, dt=F32):
            n = 4
            for s in shape[1:]:
                n *= s
            t = at(name, shape, at_r5[0], dt)
            at_r5[0] += (n + 31) // 32 * 32
            return t

        def sem(name):
            return ctx.enter_context(nc.semaphore(name))

        def spread(ap, axis, shape):
            return ap.unsqueeze(axis).to_broadcast(shape)

        xres = at("xres", [P, NT, D_MODEL], R0)
        mhi = at("mhi", [P, KD, N_MEM], R0, F32R)
        mlo = at("mlo", [P, KD, N_MEM], R0 + KD * N_MEM * 4, F32R)
        scr = [at(f"scr{n}", [P, HEADS, P], R0 + 2048 * n) for n in range(10)]
        att_a = [at(f"att_a{n}", [P, 640], R0 + 7712 * n) for n in range(2)]
        att_m = [at(f"att_m{n}", [P, 648], R0 + 7712 * n + 2560) for n in range(2)]
        att_t = [at(f"att_t{n}", [P, 640], R0 + 7712 * n + 5152) for n in range(2)]
        hhi = at("hhi", [P, KD, TOK], R1, F32R)
        hlo = at("hlo", [P, KD, TOK], R1 + KD * TOK * 4, F32R)
        junk_mk = at("junk_mk", [P, HEADS, P], R3 + 51200 + TOK * 4)
        kraw = [at(f"kraw{n}", [P, 4, 256], R1 + 4096 * n) for n in range(4)]
        vraw = [at(f"vraw{n}", [P, 4, 256], R1 + 16384 + 4096 * n) for n in range(4)]
        kTs = [at(f"kTs{n}", [P, 2, 512], R1 + 32768 + 4096 * n) for n in range(2)]
        XT = at("XT", [P, NT, HEADS, P], R1)
        qkD = at("qkD", [P, NT, HEADS, P], R1 + 10240)
        LT = at("LT", [P, NT, HEADS, P], R1 + 20480)
        XY = at("XY", [P, NT, HEADS, P], R1 + 30720)
        stS = at("stS", [P, DEC_BATCH, HEADS, P], R1 + 20480)
        stP = [at(f"stP{n}", [P, HEADS, P], R1 + 20480 + 16384 + 2048 * n) for n in range(2)]
        mkraw = [at(f"mkraw{n}", [P, 2, 512], R1 + 4096 * n) for n in range(DEC_BATCH)]
        kmT = [at(f"kmT{n}", [P, HEADS, N_MEM], R1 + 4096 * (DEC_BATCH + n)) for n in range(2)]
        vmask = [at(f"vmask{n}", [P, DEC_BATCH, P], R0 + 4096 * n) for n in range(2)]
        sqG = [at(f"sqG{n}", [P, TOK], R3 + (16 + n) * TOK * 4) for n in range(2)]
        rG = [at(f"rG{n}", [P, TOK], R3 + (20 + n) * TOK * 4) for n in range(2)]
        mxhi = at("mxhi", [P, KD, TOK], R3 + 4 * TOK * 4, F32R)
        mxlo = at("mxlo", [P, KD, TOK], R1, F32R)
        sqA = [at(f"sqA{n}", [P, TOK], R0 + 2560 * n) for n in range(2)]
        rA = [at(f"rA{n}", [P, TOK], R0 + 5120 + 2560 * n) for n in range(2)]
        gT = at("gT", [8, TOK], R3 + 51200)
        sqM = [at(f"sqM{n}", [P, TOK], R3 + 30720 + 2560 * n) for n in range(2)]
        rM = [at(f"rM{n}", [P, TOK], R3 + 35840 + 2560 * n) for n in range(2)]
        wraw = [at(f"wraw{n}", [P, BLK], R2 + BLK * 4 * n) for n in range(2)]
        whi = [at(f"whi{n}", [P, BLK], R2 + BLK * 4 * (2 + n), F32R) for n in range(2)]
        wlo = [at(f"wlo{n}", [P, BLK], R2 + BLK * 4 * (4 + n), F32R) for n in range(2)]
        qkvz = at("qkvz", [P, 16, TOK], R3)
        cq = at("cq", [P, 2, TOK], R3 + 16 * TOK * 4)
        yb = at("yb", [P, 2, TOK], R3 + 18 * TOK * 4)
        kT = at("kT", [P, 2, TOK], R3 + 20 * TOK * 4)
        xin = [at(f"xin{n}", [P, D_MODEL], R3 + (0, 4096, 40960, 45056)[n]) for n in range(XIN)]
        xn = [at(f"xn{n}", [P, D_MODEL], R3 + 8192 + 4096 * n) for n in range(2)]
        junk = at("junk", [P, D_MODEL], R3 + 16384)
        gmix = at("gmix", [P, D_MODEL], R3 + 20480)
        gmin = at("gmin", [P, D_MODEL], R3 + 24576)
        crow = at("crow", [24, GDN_DIM], R3 + 28672)
        scrow = at("scrow", [16, SC_DIM], R3 + 28672 + 6144)
        qm = at("qm", [P, HEADS, TOK], R3)
        omhi = at("omhi", [P, HEADS, TOK], R3 + 10240, F32R)
        omlo = at("omlo", [P, HEADS, TOK], R3 + 20480, F32R)
        gmem = at("gmem", [P, D_MODEL], R3 + 30720)
        xn2 = [at(f"xn2{n}", [P, D_MODEL], R3 + 34816 + 4096 * n) for n in range(2)]
        junk2 = at("junk2", [P, D_MODEL], R3 + 43008)
        gffn = at("gffn", [P, D_MODEL], R3 + 47104)
        probs = [at(f"probs{n}", [P, HEADS, N_MEM], R3 + 30720 + 4096 * n) for n in range(2)]
        probT = [at(f"probT{n}", [P, HEADS, 2, P], R3 + 38912 + 4096 * n) for n in range(2)]
        stsb = at("stsb", [P, 2, HEADS, P], R3 + 51200)
        act = at("act", [P, FT, TOK], R3)
        ckv = keep("ckv", [P, NT, 512])
        smp_v, smp_kb, smp_kd, smp_w, smp_ws = [at(f"smp{n}", [P, HEADS, P], R5 + 2048 * n) for n in range(5)]
        yc = keep("yc", [P, 2, TOK])
        scC = at("scC", [P, 2, TOK], at_r5[0] - 2 * TOK * 4)
        mkout = at("mkout", [P, 2, 512], at_r5[0] - 2 * TOK * 4)
        memkT = keep("memkT", [P, HEADS, N_MEM])
        memv = keep("memv", [P, 2, 512])
        cb = [keep(f"cb{n}", [P, 672]) for n in range(2)]
        xn3 = [at(f"xn3{n}", [P, D_MODEL], at_r5[0] - 2 * 2688 - 4096 * (2 - n)) for n in range(2)]
        junk3 = at("junk3", [P, D_MODEL], at_r5[0] - 2 * 2688)
        ident = keep("ident", [P, P])
        ones = keep("ones", [P, P])
        uptri = keep("uptri", [P, P])
        up16 = keep("up16", [P, P])
        same16 = keep("same16", [P, P])
        same64 = keep("same64", [P, P])
        lmask = keep("lmask", [P, LEVELS, P])
        negm = keep("negm", [P, P])
        newm = keep("newm", [P, 224])
        newi = keep("newi", [P, 224])
        own8 = keep("own8", [P, DEC_BATCH])
        w8raw = keep("w8raw", [P, KD, 8])
        w8hi = keep("w8hi", [P, KD, 8], F32R)
        w8lo = keep("w8lo", [P, KD, 8], F32R)
        gmk = keep("gmk", [P, DK])
        gcw = keep("gcw", [P, 12, 4])
        scw = keep("scw", [P, 2, 3])
        gout = keep("gout", [P, 8])
        gmq = keep("gmq", [P, 1])
        epsc = keep("epsc", [P, 1])
        dtb = keep("dtb", [P, HEADS])
        nA = keep("nA", [P, HEADS])
        stat = keep("stat", [P, 3, 40])
        mstat = keep("mstat", [P, 4, NT, HEADS])
        gba = keep("gba", [P, NT, 8])
        beta = keep("beta", [P, NT, HEADS])
        gdec = keep("gdec", [P, NT, HEADS])
        gtmp = keep("gtmp", [P, 4, NT, HEADS])
        gcs = keep("gcs", [P, NT, 3, HEADS])
        kdec = keep("kdec", [P, NT, HEADS])
        bege = keep("bege", [P, NT, HEADS])
        etot = keep("etot", [P, NT, HEADS])
        etotS = keep("etotS", [P, HEADS, DEC_BATCH])
        cacheT = keep("cacheT", [P, 12, 24])
        cacheS = keep("cacheS", [P, 2, 16])
        cst = keep("cst", [P, 12, 27])
        scst = keep("scst", [P, 2, 18])
        qbl = at("qbl", [P, 2, DEC_BATCH, 32], R0 + 15456)
        fcw = at("fcw", [P, FT, 3], R5)
        cacheF = at("cacheF", [P, FT, 16], R5 + 288)
        fcst = at("fcst", [P, FT, 18], R5 + 1696)
        strow = at("strow", [27, GDN_DIM], R1 + 24576)
        scsrow = at("scsrow", [18, SC_DIM], R1 + 24576 + 6144)
        frow = at("frow", [16, D_FF], R5 + 3296)
        fsrow = at("fsrow", [18, D_FF], R5 + 3296)
        assert at_r5[0] <= 229344, at_r5[0]
        assert R5 + 3296 + D_FF * 4 <= R5 + 15360

        bank = [ctx.enter_context(nc.psum_tensor(f"bank{b}", [P, 512], F32)) for b in range(8)]
        bank_full = [sem(f"bank_full{b}") for b in range(8)]
        bank_free = [sem(f"bank_free{b}") for b in range(8)]
        w_loaded = [sem(f"w_loaded{n}") for n in range(2)]
        s = {n: sem(n) for n in (
            "eps_ready", "ident_ready", "consts", "small_loaded", "gmin_loaded", "gmix_loaded", *[f"x_loaded{n}" for n in range(XIN)], "rstd_ready", "xn_ready", "h_hi_ready",
            "w_hi_ready", "w_lo_ready", "w8_ready", "kstep", "conv_done", "sig_ready", "silu_done", "sq_ready", "rinv_ready",
            "l2_done", "gates", "gates_act", "rhs_ready", "dif_ready", "dt_ready", "dtu_ready", "small_exp",
            "lt_ready", "xt0_ready", "lm_ready", "kd_ready", "vc_loaded0", "vc_loaded1", "vc_loaded2", "vc_loaded3", "kc_loaded0", "kc_loaded1", "kc_loaded2",
            "kc_loaded3", "A_ready", "q_blocks", "st_loaded", "vm_ready", "sqf_ready", "rf_ready", "y_ready",
            "yhi_ready", "ylo_ready", "xres_loaded", "gm_loaded", "f_loaded", "qsq_ready", "qr_ready", "qm_ready",
            "max_ready", "prob_ready", *[f"mc_loaded{n}" for n in range(DEC_BATCH)], "om_hi", "ffn_conv", "ffn_silu", "ahi_ready",
            "alo_ready", "out_sb", "out_mk", "out_mv", "out_rows", "out_frows", "out_pstate", "out_sstate",
            "out_y", "dve_chain", "act_chain", "pool_chain")}

        def flat(t):
            return t[:, :, :].rearrange("p a b -> p (a b)")

        def quad(b):
            return bank[b][:, :].rearrange("p (a b) -> p a b", a=4)

        def conv_s(t):
            return t[:, PAD + SEQ:PAD + SEQ + DEC_BATCH * (PAD + DEC_SEQ)].rearrange("p (b t) -> p b t", b=DEC_BATCH)

        def tri(i):
            return uptri if i < PT else up16

        def mixed(f):
            return qkvz[:, f, :] if f < 4 else yb[:, f - 4, :] if f < 6 else yc[:, f - 6, :]

        def dest1(n, mem, x):
            return mem[:, :, n * P:(n + 1) * P] if n < 2 else x[:, :, (n - 2) * P:(n - 1) * P]

        def at_banks(n):
            return 1 if SB_ITEMS[n][0] == "p" else 2

        turns = [0] * 8
        use = {}
        ring_at = [0, 0]
        ksteps = [0]
        ends = {}

        def filled(eng, key):
            b, n = use[key]
            eng.wait_ge(bank_full[b], n)
            return b

        def evacuated(eng, key):
            b, n = use[key]
            eng.wait_ge(bank_free[b], n)

        def passed(eng, key):
            kind, what = ends[key]
            if kind == "bank":
                filled(eng, what)
            else:
                eng.wait_ge(s["kstep"], what)

        blocks = []

        def cols(w, c0, n=256):
            blocks.append((w[:, c0:c0 + n].rearrange("(k p) c -> p k c", p=P), KD, n))
            return len(blocks) - 1

        def rows(w, k0, nk, c0):
            blocks.append((w[k0 * P:(k0 + nk) * P, c0:c0 + 512].rearrange("(k p) c -> p k c", p=P), nk, 512))
            return len(blocks) - 1

        B_MK = [rows(A["w_mk"], k, 4, 0) for k in (0, 4)]
        B_MV = [rows(A["w_mv"], k, 4, 0) for k in (0, 4)]
        B_CQ = cols(A["w_in"], SCOL + 3 * SC_DIM)
        B_CK = [rows(A["w_in"], k, 4, CKCOL) for k in (0, 4)]
        B_SB, B_SC, B_SX = [cols(A["w_in"], SCOL + SC_DIM * n) for n in range(3)]
        B_QKV = [cols(A["w_in"], 256 * n) for n in range(6)]
        B_Z = [cols(A["w_in"], 256 * n) for n in (6, 7)]
        B_OUT = [[rows(A["w_mix_out"], k, 4, 512 * h) for k in (4, 0)] for h in range(2)]
        B_MQ = [cols(A["w_mq"], 256 * n) for n in range(2)]
        B_MO = [[rows(A["w_mo"], 0, 4, 512 * h)] for h in range(2)]
        B_GU = [(cols(A["w_gate"], 256 * n), cols(A["w_up"], 256 * n)) for n in range(FT // 2)]
        B_DN = [[rows(A["w_down"], k, min(4, FT - k), 512 * h) for k in range(0, FT, 4)] for h in range(2)]
        NB = len(blocks)

        def wv(t, i):
            _, nk, n = blocks[i]
            return t[i % 2][:, 0:nk * n].rearrange("p (k c) -> p k c", k=nk)

        small = [
            (crow[0:24, :], A["cache_gdn_conv"].rearrange("b t c -> (b t) c")),
            (scrow[0:16, :], A["cache_sc_conv"].rearrange("b t c -> (b t) c")),
            (gmk[:, :], A["mk_norm_g"].partition_broadcast(P)), (dtb[:, :], A["gdn_dt_bias"].partition_broadcast(P)),
            (nA[:, :], A["gdn_A_log"].partition_broadcast(P)),
            (w8raw[:, :, :], A["w_in"][:, GAB:GAB + 8].rearrange("(k p) c -> p k c", p=P)),
        ] + [(gout[:, 0:1], A["gdn_norm_g"].unsqueeze(1)), (gmq[:, :], A["mq_norm_g"].unsqueeze(1))]
        small_cols = [(gcw[:, :, k], A["gdn_conv_w"][k, :].rearrange("(j p) -> p j", p=P)) for k in range(4)]
        small_cols += [(scw[:, :, k], A["sc_conv_w"][k, :].rearrange("(j p) -> p j", p=P)) for k in range(3)]
        small_cols += [(gout[:, 4:6], A["sc_norm_g"].rearrange("(j p) -> p j", p=P)),
                       (gout[:, 6:8], A["sb_norm_g"].rearrange("(j p) -> p j", p=P))]
        NI = 20
        SMALL_LOADS = len(small) + len(small_cols)

        SB_ITEMS = [("p", h, i) for h in range(HEADS) for i in range(PT)] + [("s", p, None) for p in range(4)]
        TILES_AT = [list(range(NT)) if l < SAMPLE_LEVELS else list(range(PT)) for l in range(LEVELS)]
        GN = (4, 5, 6, 7, 0, 1, 2, 3)
        WOVEN = [(name, i, c) for name, i in [("sC", B_SC), ("sx", B_SX)] + [(("qkv", n), b) for n, b in enumerate(B_QKV)]
                 for c in range(2)]
        N_P = len(WOVEN)
        LM_ORDER = [(l, i) for l in range(1, LEVELS) for i in TILES_AT[l]]

        block = ctx.enter_context(nc.Block())

        @block.tensor
        def _(pe):
            T = nc.tensor

            def take(key, long=False):
                if long:
                    b = RING + ring_at[1] % 2
                    ring_at[1] += 1
                else:
                    b = ring_at[0] % RING
                    ring_at[0] += 1
                turns[b] += 1
                use[key] = (b, turns[b])
                if turns[b] > 1:
                    pe.wait_ge(bank_free[b], turns[b] - 1)
                return b

            def done(ins, key):
                ins.then_inc(bank_full[use[key][0]], 1)

            def step(ins, key):
                ins.then_inc(s["kstep"], 1)
                ksteps[0] += 1
                ends[key] = ("k", ksteps[0])

            def across(name, i, hi, lo, cs=(0, 1)):
                pe.wait_ge(s["w_lo_ready"], i + 1)
                wh, wl = wv(whi, i), wv(wlo, i)
                for c in cs:
                    keys = [(name, c, h) for h in range(2)]
                    bs = [take(k) for k in keys]
                    for k in range(KD):
                        for w, parts in ((wh, (hi, lo)), (wl, (hi,))):
                            for h in range(2):
                                for a in parts:
                                    ins = T.matmul(bank[bs[h]][:, 0:HALF], w[:, k, c * P:(c + 1) * P],
                                                   a[:, k, h * HALF:(h + 1) * HALF],
                                                   start=(k == 0 and w is wh and a is hi),
                                                   stop=(k == KD - 1 and w is wl))
                                if k == KD - 1 and w is wl:
                                    done(ins, keys[h])
                ends[i] = ("bank", keys[1])

            def down(name, half, blks, left, tiles, ready=None, behind=lambda i: None):
                keys = [(name, half, t) for t in range(tiles)]
                bs = [take(k) for k in keys]
                nk = sum(blocks[i][1] for i in blks)
                k = 0
                for i in blks:
                    pe.wait_ge(s["w_lo_ready"], i + 1)
                    wh, wl = wv(whi, i), wv(wlo, i)
                    for kk in range(blocks[i][1]):
                        if ready:
                            ready(half, k)
                        hi, lo = left(half, k)
                        for t in range(tiles):
                            o = bank[bs[t]][:, :]
                            T.matmul(o, hi[:, t * P:(t + 1) * P], wh[:, kk, :], start=(k == 0), stop=False)
                            T.matmul(o, hi[:, t * P:(t + 1) * P], wl[:, kk, :], start=False, stop=False)
                            ins = T.matmul(o, lo[:, t * P:(t + 1) * P], wh[:, kk, :], start=False, stop=(k == nk - 1))
                            if k == nk - 1:
                                done(ins, keys[t])
                        if k < nk - 1:
                            step(ins, (name, half, k))
                        else:
                            ends[(name, half, k)] = ("bank", keys[-1])
                        k += 1
                    ends[i] = ends[(name, half, k - 1)]
                    behind(i)

            def rows_tile(name, half, blks, left, t):
                b = take((name, half, t))
                k, tt = 0, slice(t * P, (t + 1) * P)
                nk = sum(blocks[i][1] for i in blks)
                for i in blks:
                    if t == 0:
                        pe.wait_ge(s["w_lo_ready"], i + 1)
                    wh, wl = wv(whi, i), wv(wlo, i)
                    for kk in range(blocks[i][1]):
                        hi, lo = left(half, k)
                        T.matmul(bank[b][:, :], hi[:, tt], wh[:, kk, :], start=(k == 0), stop=False)
                        T.matmul(bank[b][:, :], hi[:, tt], wl[:, kk, :], start=False, stop=False)
                        ins = T.matmul(bank[b][:, :], lo[:, tt], wh[:, kk, :], start=False, stop=(k == nk - 1))
                        k += 1
                done(ins, (name, half, t))
                if t == NT - 1:
                    for i in blks:
                        ends[i] = ("bank", (name, half, t))

            def turn_rows(kind, n, src, ready):
                pe.wait_ge(s["xn_ready"], ready)
                for g in range(2):
                    b = take((kind, n, g))
                    for j in range(4):
                        ins = T.transpose(bank[b][:, j * P:(j + 1) * P], src[:, (4 * g + j) * P:(4 * g + j + 1) * P],
                                          ident[:, :])
                    done(ins, (kind, n, g))

            def scores(n):
                kind, x, i = SB_ITEMS[n]
                if kind == "p":
                    hp, h2 = divmod(x, 2)
                    r = slice(64 * h2, 64 * h2 + 64)
                    b = take(("z", n, 0))
                    w = (i + 1) * P
                    T.matmul(bank[b][:, 0:w], cq[r, hp, i * P:(i + 1) * P], kT[r, hp, 0:w], start=True, stop=False)
                    done(T.matmul(bank[b][:, i * P:w], ident[:, :], negm[:, :], start=False, stop=True), ("z", n, 0))
                    return
                if x == 0:
                    pe.wait_ge(s["q_blocks"], 1)
                bb = []
                for b2 in range(2):
                    bt = 2 * x + b2
                    pe.wait_ge(s[f"kc_loaded{bt % 4}"], 16 * (bt // 4 + 1))
                    for hp in range(2):
                        b = take(("kc", bt, hp))
                        for j in range(4):
                            ins = T.transpose(bank[b][:, j * P:(j + 1) * P], kraw[bt % 4][:, j, hp * P:(hp + 1) * P],
                                              ident[:, :])
                        done(ins, ("kc", bt, hp))
                zo, zn = take(("z", n, 0)), take(("z", n, 1))
                for b2 in range(2):
                    bt = 2 * x + b2
                    for hp in range(2):
                        g = 2 * b2 + hp
                        r = slice(32 * g, 32 * g + 32)
                        evacuated(pe, ("kc", bt, hp))
                        last = T.matmul(bank[zo][r, :], qbl[:, hp, bt, :], kTs[b2][:, hp, :], start=True, stop=True)
                        if g == 3:
                            done(last, ("z", n, 0))
                        last = T.matmul(bank[zn][r, 0:P], qbl[:, hp, bt, :], kT[:, hp, SEQ:TOK], start=True, stop=True)
                        if g == 3:
                            done(last, ("z", n, 1))

            def turn_probs(n):
                kind, x, i = SB_ITEMS[n]
                pe.wait_ge(s["A_ready"], n + 1)
                nb = i + 1 if kind == "p" else 5
                lo = 640 - nb * P
                for g in range((nb + 3) // 4):
                    b = take(("AT", n, g))
                    for j in range(4 * g, min(nb, 4 * g + 4)):
                        ins = T.transpose(bank[b][:, (j % 4) * P:(j % 4 + 1) * P],
                                          att_a[n % 2][:, lo + j * P:lo + (j + 1) * P], ident[:, :])
                    done(ins, ("AT", n, g))

            oc = {}

            def values(n):
                kind, x, i = SB_ITEMS[n]
                for g in range(1 if kind == "p" else 2):
                    evacuated(pe, ("AT", n, g))
                a = att_t[n % 2]
                if kind == "p":
                    hp, h2 = divmod(x, 2)
                    if h2 == 0 and i == 0:
                        oc[hp] = take(("oc", hp), long=True)
                    for j in range(i + 1):
                        ins = T.matmul(bank[oc[hp]][64 * h2:64 * h2 + 64, i * P:(i + 1) * P],
                                       ckv[:, j, 256 + 64 * x:320 + 64 * x], a[:, j * P:(j + 1) * P],
                                       start=(j == 0), stop=(j == i))
                    if h2 == 1 and i == PT - 1:
                        done(ins, ("oc", hp))
                        ends[("av", n)] = ("bank", ("oc", hp))
                    else:
                        step(ins, ("av", n))
                    return
                if x == 0:
                    oc[2] = take(("oc", 2), long=True)
                for b2 in range(2):
                    bt = 2 * x + b2
                    pe.wait_ge(s[f"vc_loaded{bt % 4}"], 16 * (bt // 4 + 1))
                    for hp in range(2):
                        g = 2 * b2 + hp
                        c0 = (hp * DEC_BATCH + bt) * 32
                        for j in range(5):
                            v = vraw[bt % 4][:, j, hp * P:(hp + 1) * P] if j < 4 \
                                else ckv[:, PT, 256 + hp * P:256 + (hp + 1) * P]
                            ins = T.matmul(bank[oc[2]][:, c0:c0 + 32], v, a[:, j * P + 32 * g:j * P + 32 * g + 32],
                                           start=(j == 0), stop=(j == 4))
                if x == 3 and b2 == 1:
                    done(ins, ("oc", 2))
                    ends[("av", n)] = ("bank", ("oc", 2))
                elif b2 == 1:
                    step(ins, ("av", n))

            pe.wait_ge(s["ident_ready"], 1)

            def turn1(n):
                turn_rows("norm1", n, xn[n % 2], n + 1)

            def mleft(h, k):
                return mhi[:, k, :], mlo[:, k, :]

            turn1(0)
            turn1(1)
            for n in range(2):
                for g in range(2):
                    evacuated(pe, ("norm1", n, g))
            down("mk", 0, B_MK, mleft, 2, behind=lambda i: turn1(2 + i))
            down("mv", 0, B_MV, mleft, 2, behind=lambda i: turn1(2 + i))
            turn1(6)
            for t in range(2):
                evacuated(pe, ("mk", 0, t))
                b = take(("memkT", t))
                for h in range(HEADS):
                    ins = T.transpose(bank[b][:, h * P:(h + 1) * P], mkout[:, t, h * P:(h + 1) * P], ident[:, :])
                done(ins, ("memkT", t))
            pe.wait_ge(s["small_loaded"], SMALL_LOADS * 16)
            b = take(("cache", 0))
            for j in range(12):
                ins = T.transpose(bank[b][:, 24 * j:24 * j + 24], crow[:, j * P:(j + 1) * P], ident[0:24, 0:24])
            for j in range(2):
                ins = T.transpose(bank[b][:, 288 + 16 * j:304 + 16 * j], scrow[:, j * P:(j + 1) * P], ident[0:16, 0:16])
            done(ins, ("cache", 0))
            for n in range(2, 2 + NT):
                for g in range(2):
                    evacuated(pe, ("norm1", n, g))
            across(("cq", 0), B_CQ, hhi, hlo)
            pe.wait_ge(s["w8_ready"], 2)
            for h in range(2):
                b = take(("gates", h))
                hs = slice(h * HALF, (h + 1) * HALF)
                for k in range(KD):
                    T.matmul(bank[b][0:8, 0:HALF], w8hi[:, k, :], hhi[:, k, hs], start=(k == 0), stop=False)
                    T.matmul(bank[b][0:8, 0:HALF], w8hi[:, k, :], hlo[:, k, hs], start=False, stop=False)
                    ins = T.matmul(bank[b][0:8, 0:HALF], w8lo[:, k, :], hhi[:, k, hs], start=False, stop=(k == KD - 1))
                done(ins, ("gates", h))
            down("ck", 0, B_CK, lambda h, k: (hhi[:, k, :], hlo[:, k, :]), NT)
            evacuated(pe, ("gates", 0))
            evacuated(pe, ("gates", 1))
            b = take(("gates", 2))
            for t in range(NT):
                ins = T.transpose(bank[b][:, 8 * t:8 * t + 8], gT[0:8, t * P:(t + 1) * P], ident[0:8, 0:8])
            done(ins, ("gates", 2))
            across("sB", B_SB, hhi, hlo)
            for t in range(NT):
                evacuated(pe, ("ck", 0, t))
            for hp in range(2):
                for g, ts in enumerate(((0, 1, 2, 3), (4,))):
                    b = take(("kT", hp, g))
                    for j, t in enumerate(ts):
                        ins = T.transpose(bank[b][:, j * P:(j + 1) * P], ckv[:, t, hp * P:(hp + 1) * P], ident[:, :])
                    done(ins, ("kT", hp, g))
            pe.wait_ge(s["consts"], 1)
            for n, (name, i, c) in enumerate(WOVEN):
                across(name, i, hhi, hlo, (c,))
                if n == 0:
                    for hp in range(2):
                        for g in range(2):
                            evacuated(pe, ("kT", hp, g))
                    scores(0)
                else:
                    turn_probs(n - 1)
                    if n >= 2:
                        values(n - 2)
                    scores(n)

            def squares(c):
                pe.wait_ge(s["sq_ready"], c + 1)
                for h in range(2):
                    b = take(("l2", c, h))
                    done(T.matmul(bank[b][:, 0:HALF], ones[:, :], sqA[c % 2][:, h * HALF:(h + 1) * HALF],
                                  start=True, stop=True), ("l2", c, h))

            for j in range(4):
                across(("z", j // 2), B_Z[j // 2], hhi, hlo, (j % 2,))
                if j == 0:
                    turn_probs(N_P - 1)
                    values(N_P - 2)
                elif j == 1:
                    values(N_P - 1)
                else:
                    squares(2 * j - 4)
                    squares(2 * j - 3)
            pe.wait_ge(s["conv_done"], 14)
            for g in range(3):
                b = take(("strow", g))
                for j in range(4):
                    ins = T.transpose(bank[b][0:27, j * P:(j + 1) * P], cst[:, 4 * g + j, :], ident[:, :])
                done(ins, ("strow", g))
            b = take(("strow", 3))
            for j in range(2):
                ins = T.transpose(bank[b][0:18, j * P:(j + 1) * P], scst[:, j, :], ident[:, :])
            done(ins, ("strow", 3))
            for c in range(4, 8):
                squares(c)
            scores(N_P)
            for n in range(N_P, NI + 1):
                if n + 1 < NI:
                    scores(n + 1)
                if n < NI:
                    turn_probs(n)
                if n >= N_P + 1:
                    values(n - 1)

            pe.wait_ge(s["gates"], 1)
            for i in range(NT):
                tt = slice(i * P, (i + 1) * P)
                b = take(("gcol", i))
                T.matmul(bank[b][:, 0:4], (uptri if i < PT else up16)[:, :], gdec[:, i, :], start=True, stop=True)
                done(T.matmul(bank[b][:, 4:8], (ones if i < PT else same16)[:, :], gdec[:, i, :],
                              start=True, stop=True), ("gcol", i))
                pe.wait_ge(s["rhs_ready"], 2 * i + 1)
                b = take(("grow", i))
                done(T.matmul(bank[b][:, :], ones[:, :], flat(scr[i % 2]), start=True, stop=True), ("grow", i))
                b = take(("kk", i))
                for h in range(HEADS):
                    ins = T.matmul(bank[b][:, h * P:(h + 1) * P], qkvz[:, 4 + h, tt], qkvz[:, 4 + h, tt],
                                   start=True, stop=True)
                done(ins, ("kk", i))
                b = take(("qk", i))
                for h in range(HEADS):
                    ins = T.matmul(bank[b][:, h * P:(h + 1) * P], qkvz[:, 4 + h, tt], qkvz[:, h, tt],
                                   start=True, stop=True)
                done(ins, ("qk", i))
                pe.wait_ge(s["rhs_ready"], 2 * i + 2)
                b = take(("brow", i))
                done(T.matmul(bank[b][:, :], ones[:, :], flat(scr[2 + i % 2]), start=True, stop=True), ("brow", i))

            def turn_x(l, i):
                b = take(("X", l, i))
                for h in range(HEADS):
                    ins = T.transpose(bank[b][:, h * P:(h + 1) * P], XT[:, i, h, :], ident[:, :])
                done(ins, ("X", l, i))

            for i in range(NT):
                pe.wait_ge(s["xt0_ready"], i + 1)
                turn_x(0, i)
            def turn_vk(i):
                tt = slice(i * P, (i + 1) * P)
                for name, f0 in (("Vt", 8), ("Kt", 4)):
                    b = take((name, i))
                    for h in range(HEADS):
                        ins = T.transpose(bank[b][:, h * P:(h + 1) * P], qkvz[:, f0 + h, tt], ident[:, :])
                    done(ins, (name, i))

            for l in range(1, LEVELS):
                if l == LEVELS - 1:
                    turn_vk(PT)
                for i in TILES_AT[l]:
                    pe.wait_ge(s["lm_ready"], LM_ORDER.index((l, i)) + 1)
                    evacuated(pe, ("X", l - 1, i))
                    b = take(("Y", l, i))
                    for h in range(HEADS):
                        ins = T.matmul(bank[b][:, h * P:(h + 1) * P], scr[4 + LM_ORDER.index((l, i)) % 2][:, h, :],
                                       XY[:, i, h, :], start=True, stop=True)
                    done(ins, ("Y", l, i))
                if l == LEVELS - 1:
                    turn_vk(0)
                for i in TILES_AT[l]:
                    evacuated(pe, ("Y", l, i))
                    b = take(("dX", l, i))
                    for h in range(HEADS):
                        ins = T.matmul(bank[b][:, h * P:(h + 1) * P], XY[:, i, h, :], XT[:, i, h, :],
                                       start=True, stop=True)
                    done(ins, ("dX", l, i))
                if l < LEVELS - 1:
                    for i in TILES_AT[l + 1]:
                        evacuated(pe, ("dX", l, i))
                        turn_x(l, i)

            def w_part(i):
                evacuated(pe, ("dX", (LEVELS if i < PT else SAMPLE_LEVELS) - 1, i))
                pe.wait_ge(s["kd_ready"], 1 if i == PT else i + 2)
                b = take(("wT", i))
                kb = smp_kb if i == PT else scr[2 + i % 2]
                for h in range(HEADS):
                    ins = T.matmul(bank[b][:, h * P:(h + 1) * P], kb[:, h, :], XT[:, i, h, :], start=True, stop=True)
                done(ins, ("wT", i))

            def group_sum(n):
                pe.wait_ge(s["sqf_ready"], n + 1)
                for h in range(2):
                    b = take(("gn", n, h))
                    done(T.matmul(bank[b][:, 0:HALF], (ones if GN[n] < 4 else same64)[:, :],
                                  sqG[n % 2][:, h * HALF:(h + 1) * HALF], start=True, stop=True), ("gn", n, h))

            def sample_ws(h):
                if h == 0:
                    pe.wait_ge(s["st_loaded"], 16 * DEC_BATCH)
                    evacuated(pe, ("wT", PT))
                for bt in range(DEC_BATCH):
                    c0 = h * P + DEC_SEQ * bt
                    ins = T.matmul(bank[ws][:, c0:c0 + DEC_SEQ], stS[:, bt, h, :],
                                   smp_w[:, h, DEC_SEQ * bt:DEC_SEQ * (bt + 1)], start=True, stop=True)
                if h == HEADS - 1:
                    done(ins, ("ws", 0))

            def sample_qs(h):
                for bt in range(DEC_BATCH):
                    c0 = h * P + DEC_SEQ * bt
                    ins = T.matmul(bank[qs][:, c0:c0 + DEC_SEQ], stS[:, bt, h, :],
                                   qkvz[:, h, SEQ + DEC_SEQ * bt:SEQ + DEC_SEQ * (bt + 1)], start=True, stop=True)
                if h == HEADS - 1:
                    done(ins, ("qs", 0))

            ws, qs = take(("ws", 0), long=True), take(("qs", 0), long=True)
            w_part(PT)
            w_part(0)
            turn_vk(1)
            for i in range(PT):
                tt = slice(i * P, (i + 1) * P)
                evacuated(pe, ("Vt", i))
                evacuated(pe, ("wT", i))
                if i > 0:
                    evacuated(pe, ("dS", i - 1))
                b = take(("vn", i))
                for h in range(HEADS):
                    o = bank[b][:, h * P:(h + 1) * P]
                    ins = T.matmul(o, XT[:, i, h, :], scr[i % 2][:, h, :], start=True, stop=(i == 0))
                    if i > 0:
                        ins = T.matmul(o, scr[6 + i % 2][:, h, :], stP[(i - 1) % 2][:, h, :], start=False, stop=True)
                done(ins, ("vn", i))
                if i + 1 < PT:
                    w_part(i + 1)
                evacuated(pe, ("vn", i))
                evacuated(pe, ("Kt", i))
                vn = scr[8 + i % 2]
                b = take(("dS", i))
                for h in range(HEADS):
                    ins = T.matmul(bank[b][:, h * P:(h + 1) * P], scr[4 + i % 2][:, h, :], vn[:, h, :],
                                   start=True, stop=True)
                done(ins, ("dS", i))
                b = take(("o", i))
                for h in range(HEADS):
                    o = bank[b][:, h * P:(h + 1) * P]
                    ins = T.matmul(o, vn[:, h, :], qkD[:, i, h, :], start=True, stop=(i == 0))
                    if i > 0:
                        ins = T.matmul(o, stP[(i - 1) % 2][:, h, :], qkvz[:, h, tt], start=False, stop=True)
                done(ins, ("o", i))
                if i + 2 < PT:
                    turn_vk(i + 2)
                group_sum(i)
                if i == 1 or i == 2:
                    sample_ws(2 * i - 2)
                    sample_ws(2 * i - 1)
                if i == 3:
                    sample_qs(0)
                    sample_qs(1)
            evacuated(pe, ("ws", 0))
            evacuated(pe, ("Vt", PT))
            b = take(("vn", PT))
            for h in range(HEADS):
                o = bank[b][:, h * P:(h + 1) * P]
                T.matmul(o, XT[:, PT, h, :], smp_v[:, h, :], start=True, stop=False)
                ins = T.matmul(o, smp_ws[:, h, :], ident[:, :], start=False, stop=True)
            done(ins, ("vn", PT))
            sample_qs(2)
            sample_qs(3)
            evacuated(pe, ("vn", PT))
            b = take(("o", PT))
            for h in range(HEADS):
                ins = T.matmul(bank[b][:, h * P:(h + 1) * P], scr[8][:, h, :], qkD[:, PT, h, :], start=True, stop=True)
            done(ins, ("o", PT))
            evacuated(pe, ("Kt", PT))
            for h in range(HEADS):
                pe.wait_ge(s["vm_ready"], h + 1)
                for g in range(2):
                    b = take(("dSs", h, g))
                    done(T.matmul(bank[b][:, :], smp_kd[:, h, :], vmask[h % 2][:, 4 * g:4 * g + 4, :],
                                  start=True, stop=True), ("dSs", h, g))
                group_sum(4 + h)

            ready_y = lambda h, k: pe.wait_ge(s["ylo_ready"], k + 1)
            left_y = lambda h, k: (mxhi[:, GN[k], :], mxlo[:, GN[k], :])
            down("out", 0, B_OUT[0], left_y, NT, ready_y)
            for n in range(NT + 1):
                if n < NT:
                    rows_tile("out", 1, B_OUT[1], left_y, n)
                if n >= 1:
                    turn_rows("norm2", n - 1, xn2[(n - 1) % 2], 2 + NT + n)
            for n in range(NT):
                for g in range(2):
                    evacuated(pe, ("norm2", n, g))
            for n in range(2):
                across(("mq", n), B_MQ[n], hhi, hlo)
            for h in range(HEADS):
                pe.wait_ge(s["qsq_ready"], h + 1)
                for g in range(2):
                    b = take(("mqn", h, g))
                    done(T.matmul(bank[b][:, 0:HALF], ones[:, :], sqM[h % 2][:, g * HALF:(g + 1) * HALF],
                                  start=True, stop=True), ("mqn", h, g))
            pe.wait_ge(s["qm_ready"], HEADS)

            def mem_scores(i):
                for g in range(2):
                    b = take(("ms", i, g))
                    for j in range(2):
                        h = 2 * g + j
                        ins = T.matmul(bank[b][:, j * N_MEM:(j + 1) * N_MEM], qm[:, h, i * P:(i + 1) * P], memkT[:, h, :],
                                       start=True, stop=True)
                    done(ins, ("ms", i, g))

            def mem_probs(i):
                pe.wait_ge(s["prob_ready"], i + 1)
                for g in range(2):
                    b = take(("pT", i, g))
                    for j in range(4):
                        h, nb = 2 * g + j // 2, j % 2
                        ins = T.transpose(bank[b][:, j * P:(j + 1) * P], probs[i % 2][:, h, nb * P:(nb + 1) * P],
                                          ident[:, :])
                    done(ins, ("pT", i, g))

            def mem_values(i):
                for g in range(2):
                    evacuated(pe, ("pT", i, g))
                b = take(("om", i))
                for h in range(HEADS):
                    for nb in range(2):
                        ins = T.matmul(bank[b][:, h * P:(h + 1) * P], memv[:, nb, h * P:(h + 1) * P],
                                       probT[i % 2][:, h, nb, :], start=(nb == 0), stop=(nb == 1))
                done(ins, ("om", i))

            sT = [take(("sT", nb), long=True) for nb in range(2)]

            def sample_keys(bt):
                pe.wait_ge(s[f"mc_loaded{bt}"], 16)
                for nb in range(2):
                    b = take(("km", bt, nb))
                    for h in range(HEADS):
                        ins = T.transpose(bank[b][:, h * P:(h + 1) * P], mkraw[bt][:, nb, h * P:(h + 1) * P],
                                          ident[:, :])
                    done(ins, ("km", bt, nb))

            def sample_scores(bt):
                for nb in range(2):
                    evacuated(pe, ("km", bt, nb))
                for nb in range(2):
                    for h in range(HEADS):
                        c0 = h * P + DEC_SEQ * bt
                        ins = T.matmul(bank[sT[nb]][:, c0:c0 + DEC_SEQ], kmT[bt % 2][:, h, nb * P:(nb + 1) * P],
                                       qm[:, h, SEQ + DEC_SEQ * bt:SEQ + DEC_SEQ * (bt + 1)], start=True, stop=True)
                    if bt == DEC_BATCH - 1:
                        done(ins, ("sT", nb))
                if bt < DEC_BATCH - 1:
                    step(ins, ("sT", bt))

            mem_scores(0)
            for i in range(PT):
                if i + 1 < PT:
                    mem_scores(i + 1)
                sample_keys(2 * i)
                mem_probs(i)
                sample_scores(2 * i)
                sample_keys(2 * i + 1)
                if i >= 1:
                    mem_values(i - 1)
                sample_scores(2 * i + 1)
            mem_values(PT - 1)
            for nb in range(2):
                evacuated(pe, ("sT", nb))
            for g in range(2):
                b = take(("ms", PT, g))
                for j in range(2):
                    for nb in range(2):
                        ins = T.transpose(bank[b][:, (2 * j + nb) * P:(2 * j + nb + 1) * P], stsb[:, nb, 2 * g + j, :],
                                          ident[:, :])
                done(ins, ("ms", PT, g))

            def mem_out(n):
                evacuated(pe, ("om", n))
                for half in range(2):
                    rows_tile("mo", half, B_MO[half], lambda h, k: (omhi[:, k, :], omlo[:, k, :]), n)

            def turn_norm3(n):
                turn_rows("norm3", n, xn3[n % 2], 2 + 2 * NT + n + 1)

            mem_out(0)
            mem_out(1)
            mem_probs(PT)
            mem_out(2)
            for g in range(2):
                evacuated(pe, ("pT", PT, g))
            b = take(("om", PT))
            for bt in range(DEC_BATCH):
                pe.wait_ge(s[f"mc_loaded{bt}"], 32)
                for h in range(HEADS):
                    for nb in range(2):
                        c0 = h * P + DEC_SEQ * bt
                        ins = T.matmul(bank[b][:, c0:c0 + DEC_SEQ], mkraw[bt][:, nb, h * P:(h + 1) * P],
                                       probT[PT % 2][:, h, nb, DEC_SEQ * bt:DEC_SEQ * (bt + 1)],
                                       start=(nb == 0), stop=(nb == 1))
            done(ins, ("om", PT))
            turn_norm3(0)
            turn_norm3(1)
            mem_out(3)
            turn_norm3(2)
            mem_out(4)
            turn_norm3(3)
            turn_norm3(4)
            pe.wait_ge(s["f_loaded"], 32)
            b = take(("cacheF", 0))
            for j in range(FT):
                ins = T.transpose(bank[b][:, 16 * j:16 * j + 16], frow[:, j * P:(j + 1) * P], ident[0:16, 0:16])
            done(ins, ("cacheF", 0))
            for n in range(NT):
                for g in range(2):
                    evacuated(pe, ("norm3", n, g))
            for j in range(FT // 2):
                across(("gate", j), B_GU[j][0], hhi, hlo)
                across(("up", j), B_GU[j][1], hhi, hlo)
            def ready_a(h, k):
                pe.wait_ge(s["alo_ready"], FT * h + k + 1)

            def left_a(h, k):
                n = (FT * h + k) % KD
                return hhi[:, n, :], hlo[:, n, :]
            down("dn", 0, B_DN[0], left_a, NT, ready_a)
            pe.wait_ge(s["ffn_conv"], FT)
            for g in range(6):
                b = take(("frow", g))
                for j in range(4 * g, min(FT, 4 * g + 4)):
                    ins = T.transpose(bank[b][0:18, (j % 4) * P:(j % 4 + 1) * P], fcst[:, j, :], ident[:, :])
                done(ins, ("frow", g))
            down("dn", 1, B_DN[1], left_a, NT, ready_a)


        @block.sync
        def _(sp):
            D = sp.dma_start

            def load_w(i):
                if i >= 2:
                    sp.wait_ge(s["w_lo_ready"], i - 1)
                D(wv(wraw, i), blocks[i][0]).then_inc(w_loaded[i % 2], 16)

            def load_rows(n):
                if n >= XIN:
                    sp.wait_ge(s["xn_ready"], n - XIN + 1)
                src = A["mem_prompt"][n * P:(n + 1) * P, :] if n < 2 else \
                    A["x_prompt"][(n - 2) * P:(n - 1) * P, :] if n < 2 + PT else A["x_sample"]
                D(xin[n % XIN][:, :], src).then_inc(s[f"x_loaded{n % XIN}"], 16)

            load_rows(0)
            D(gmin[:, :], A["mem_in_norm_g"].partition_broadcast(P)).then_inc(s["gmin_loaded"], 16)
            load_rows(1)
            load_w(0)
            load_rows(2)
            D(gmix[:, :], A["norm_mix_g"].partition_broadcast(P)).then_inc(s["gmix_loaded"], 16)
            load_rows(3)
            load_w(1)
            for n in range(4, 2 + NT):
                load_rows(n)
                if n == 4:
                    for dst, src in small:
                        D(dst, src).then_inc(s["small_loaded"], 16)
            with nc.allow_non_contiguous_dma(reason="a few weights of one element per partition"):
                for dst, src in small_cols:
                    D(dst, src).then_inc(s["small_loaded"], 16)
            for i in range(2, B_OUT[1][0]):
                load_w(i)
                if i == B_CK[0]:
                    for t in range(2):
                        evacuated(sp, ("mk", 0, t))
                    D(O["p_mem_k"].rearrange("(t p) c -> p t c", p=P), mkout[:, :, :]).then_inc(s["out_mk"], 16)
                    for t in range(2):
                        evacuated(sp, ("mv", 0, t))
                    D(O["p_mem_v"].rearrange("(t p) c -> p t c", p=P), memv[:, :, :]).then_inc(s["out_mv"], 16)
                if i == B_QKV[1]:
                    for t in range(NT):
                        evacuated(sp, ("ck", 0, t))
                    for col, name in ((0, "sb_k"), (256, "sb_v")):
                        D(O["p_" + name].rearrange("(t p) c -> p t c", p=P), ckv[:, 0:PT, col:col + 256])\
                            .then_inc(s["out_sb"], 16)
                        D(O["s_" + name], ckv[:, PT, col:col + 256]).then_inc(s["out_sb"], 16)

            def load_k(bt):
                D(kraw[bt % 4][:, :, :], A["cache_sb_k"][bt].rearrange("(j p) c -> p j c", p=P))\
                    .then_inc(s[f"kc_loaded{bt % 4}"], 16)

            def load_v(bt):
                D(vraw[bt % 4][:, :, :], A["cache_sb_v"][bt].rearrange("(j p) c -> p j c", p=P))\
                    .then_inc(s[f"vc_loaded{bt % 4}"], 16)
            for c in range(2):
                for h in range(2):
                    filled(sp, (("z", 1), c, h))
            for bt in range(4):
                load_k(bt)
            load_v(0)
            load_v(1)
            for g in range(4):
                evacuated(sp, ("strow", g))
            D(O["p_gdn_conv"], strow[0:3, :]).then_inc(s["out_rows"], 16)
            D(O["s_gdn_conv"], strow[3:27, :]).then_inc(s["out_rows"], 16)
            D(O["p_sc_conv"], scsrow[0:2, :]).then_inc(s["out_rows"], 16)
            D(O["s_sc_conv"], scsrow[2:18, :]).then_inc(s["out_rows"], 16)
            sp.wait_ge(s["out_rows"], 64)
            load_v(2)
            load_v(3)
            for bt in range(4):
                filled(sp, ("kc", bt, 1))
                load_k(4 + bt)
            for x in (0, 1):
                passed(sp, ("av", N_P + x))
                for b2 in range(2):
                    load_v(4 + 2 * x + b2)
            for i in B_OUT[1]:
                load_w(i)
            evacuated(sp, ("dX", LEVELS - 1, PT - 1))
            evacuated(sp, ("dX", SAMPLE_LEVELS - 1, PT))
            for bt in range(DEC_BATCH):
                D(stS[:, bt, :, :], A["state_gdn"][bt].rearrange("h k v -> k h v")).then_inc(s["st_loaded"], 16)
            evacuated(sp, ("dS", PT - 1))
            D(O["p_gdn_state"].rearrange("h k v -> k h v"), stP[(PT - 1) % 2][:, :, :]).then_inc(s["out_pstate"], 16)
            for h in range(HEADS):
                for g in range(2):
                    evacuated(sp, ("dSs", h, g))
            for bt in range(DEC_BATCH):
                D(O["s_gdn_state"][bt].rearrange("h k v -> k h v"), stS[:, bt, :, :]).then_inc(s["out_sstate"], 16)
            sp.wait_ge(s["ylo_ready"], 8)
            D(xres[:, 0:PT, :], A["x_prompt"].rearrange("(t p) c -> p t c", p=P)).then_inc(s["xres_loaded"], 16)
            D(xres[:, PT, :], A["x_sample"]).then_inc(s["xres_loaded"], 16)
            D(gmem[:, :], A["norm_mem_g"].partition_broadcast(P)).then_inc(s["gm_loaded"], 16)
            D(frow[0:16, :], A["cache_ffn_conv"].rearrange("b t c -> (b t) c")).then_inc(s["f_loaded"], 16)
            with nc.allow_non_contiguous_dma(reason="a few weights of one element per partition"):
                for k in range(3):
                    D(fcw[:, :, k], A["ffn_conv_w"][k, :].rearrange("(j p) -> p j", p=P)).then_inc(s["f_loaded"], 16)
            for i in range(B_OUT[1][1] + 1, B_GU[0][0]):
                load_w(i)

            D(gffn[:, :], A["norm_ffn_g"].partition_broadcast(P)).then_inc(s["gm_loaded"], 16)

            def load_mem(bt, name):
                D(mkraw[bt][:, :, :], A[name][bt].rearrange("(j p) c -> p j c", p=P)).then_inc(s[f"mc_loaded{bt}"], 16)
            filled(sp, (("mq", 1), 1, 1))
            for bt in range(DEC_BATCH):
                load_mem(bt, "cache_mem_k")
            for bt in range(DEC_BATCH):
                filled(sp, ("km", bt, 1))
                load_mem(bt, "cache_mem_v")
            for i in range(B_GU[0][0], B_DN[1][0] + 2):
                load_w(i)
            for g in range(6):
                evacuated(sp, ("frow", g))
            D(O["p_ffn_conv"], fsrow[0:2, :]).then_inc(s["out_frows"], 16)
            D(O["s_ffn_conv"], fsrow[2:18, :]).then_inc(s["out_frows"], 16)
            for i in range(B_DN[1][0] + 2, NB):
                load_w(i)
            for t in range(NT):
                evacuated(sp, ("dn", 0, t))
                evacuated(sp, ("dn", 1, t))
                dst = O["y_prompt"][t * P:(t + 1) * P, :] if t < PT else O["y_sample"]
                D(dst, xres[:, t, :]).then_inc(s["out_y"], 16)
            for name, n in (("out_sb", 4), ("out_mk", 1), ("out_mv", 1), ("out_rows", 4), ("out_frows", 2),
                            ("out_pstate", 1), ("out_sstate", DEC_BATCH), ("out_y", NT)):
                sp.wait_ge(s[name], 16 * n)

        @block.gpsimd
        def _(pool):
            G = nc.gpsimd
            chain = [0]

            def link(ins):
                chain[0] += 1
                ins.then_inc(s["pool_chain"], 1)
                pool.wait_ge(s["pool_chain"], chain[0])

            sel = G.affine_select
            G.memset(epsc[:, :], EPS).then_inc(s["eps_ready"], 1)
            link(G.memset(ident[:, :], 0.0))
            sel(out=ident[:, :], in_=ident[:, :], compare_op=ALU.not_equal, fill=1.0, base=0, pattern=[[-1, P]],
                channel_multiplier=1).then_inc(s["ident_ready"], 1)

            def cut_lo(i):
                pool.wait_ge(s["w_hi_ready"], i + 1)
                G.tensor_tensor(wv(wlo, i), wv(wraw, i), wv(whi, i).bitcast(F32), ALU.subtract)\
                    .then_inc(s["w_lo_ready"], 1)

            for i in range(4):
                cut_lo(i)
            pool.wait_ge(s["w8_ready"], 1)
            G.tensor_tensor(w8lo[:, :, :], w8raw[:, :, :], w8hi[:, :, :].bitcast(F32), ALU.subtract)\
                .then_inc(s["w8_ready"], 1)
            cut_lo(4)
            cut_lo(5)
            for t, v in ((ones, 1.0), (negm, NEG), (newm, 0.0), (own8, 1.0), (same16, 1.0)):
                G.memset(t[:, :], v)
            link(G.memset(same64[:, :], 1.0))
            sel(out=uptri[:, :], in_=ones[:, :], compare_op=ALU.is_ge, fill=0.0, base=0, pattern=[[1, P]],
                channel_multiplier=-1)
            sel(out=negm[:, :], in_=negm[:, :], compare_op=ALU.is_ge, fill=0.0, base=0, pattern=[[1, P]],
                channel_multiplier=-1)
            sel(out=own8[:, :], in_=own8[:, :], compare_op=ALU.is_ge, fill=0.0, base=0, pattern=[[-DEC_SEQ, DEC_BATCH]],
                channel_multiplier=1)
            grid = [[-DEC_SEQ, DEC_BATCH], [0, DEC_SEQ]]
            s16 = same16[:, :].rearrange("p (a b) -> p a b", a=DEC_BATCH)
            link(sel(out=s16, in_=s16, compare_op=ALU.is_ge, fill=0.0, base=0, pattern=grid, channel_multiplier=1))
            link(sel(out=s16, in_=s16, compare_op=ALU.is_ge, fill=0.0, base=DEC_SEQ - 1,
                     pattern=[[DEC_SEQ, DEC_BATCH], [0, DEC_SEQ]], channel_multiplier=-1))
            s64 = same64[:, :].rearrange("p (a b) -> p a b", a=2)
            link(sel(out=s64, in_=s64, compare_op=ALU.is_ge, fill=0.0, base=0, pattern=[[-64, 2], [0, 64]],
                     channel_multiplier=1))
            link(sel(out=s64, in_=s64, compare_op=ALU.is_ge, fill=0.0, base=63, pattern=[[64, 2], [0, 64]],
                     channel_multiplier=-1))
            sel(out=own8[:, :], in_=own8[:, :], compare_op=ALU.is_ge, fill=0.0, base=DEC_SEQ - 1,
                pattern=[[DEC_SEQ, DEC_BATCH]], channel_multiplier=-1)
            G.tensor_copy(lmask[:, 0, :], ident[:, :])
            for l in range(1, LEVELS):
                m = 1 << l
                v = lmask[:, l, :].rearrange("p (a b) -> p a b", b=m)
                u = uptri[:, :].rearrange("p (a b) -> p a b", b=m)
                ins = sel(out=v, in_=u, compare_op=ALU.is_ge, fill=0.0, base=0, pattern=[[-m, P // m], [0, m]],
                          channel_multiplier=1)
            link(ins)
            link(G.tensor_copy(up16[:, :], lmask[:, 4, :]))
            for l in range(LEVELS):
                up = lmask[:, l + 1, :] if l < LEVELS - 1 else uptri[:, :]
                link(G.tensor_tensor(lmask[:, l, :], up, lmask[:, l, :], ALU.subtract))
            link(G.tensor_tensor(newi[:, 0:P], same16[:, :], up16[:, :], ALU.subtract))
            for q in range(1, 8):
                link(G.tensor_tensor(newi[:, 0:16], newi[:, 0:16], newi[:, 16 * q:16 * q + 16], ALU.add))
            link(G.tensor_copy(newm[0:64, 96:112], newi[0:64, 0:16]))
            link(G.tensor_copy(newm[64:P, 112:128], newi[64:P, 0:16]))
            G.tensor_scalar(newi[:, :], newm[:, :], -1.0, 1.0, ALU.mult, ALU.add).then_inc(s["consts"], 1)

            for i in range(6, B_OUT[0][1] + 1):
                cut_lo(i)

            def row_sources(i):
                if i >= 2:
                    filled(pool, ("brow", i - 2))
                G.tensor_tensor(scr[i % 2][:, :, :], spread(tri(i)[:, :], 1, [P, HEADS, P]),
                                spread(gdec[:, i, :], 2, [P, HEADS, P]), ALU.mult).then_inc(s["rhs_ready"], 1)
                G.tensor_tensor(scr[2 + i % 2][:, :, :], spread(ident[:, :], 1, [P, HEADS, P]),
                                spread(beta[:, i, :], 2, [P, HEADS, P]), ALU.mult).then_inc(s["rhs_ready"], 1)

            pool.wait_ge(s["gates"], 1)
            passed(pool, ("av", NI - 1))
            row_sources(0)
            row_sources(1)
            for i in range(NT):
                pool.wait_ge(s["dt_ready"], i + 1)
                if i >= 2:
                    pool.wait_ge(s["lt_ready"], i - 1)
                G.tensor_tensor(scr[8 + i % 2][:, :, :], scr[4 + i % 2][:, :, :],
                                spread(tri(i)[:, :], 1, [P, HEADS, P]), ALU.mult).then_inc(s["dtu_ready"], 1)
                if i + 2 < NT:
                    row_sources(i + 2)
                evacuated(pool, ("brow", i))
                link(G.tensor_tensor(XT[:, i, :, :], LT[:, i, :, :], spread(lmask[:, 0, :], 1, [P, HEADS, P]), ALU.mult))
                G.tensor_tensor(XT[:, i, :, :], spread(ident[:, :], 1, [P, HEADS, P]), XT[:, i, :, :], ALU.subtract)\
                    .then_inc(s["xt0_ready"], 1)
            for n, (l, i) in enumerate(LM_ORDER):
                if n >= 2:
                    filled(pool, ("Y",) + LM_ORDER[n - 2])
                G.tensor_tensor(scr[4 + n % 2][:, :, :], LT[:, i, :, :], spread(lmask[:, l, :], 1, [P, HEADS, P]),
                                ALU.mult).then_inc(s["lm_ready"], 1)
            evacuated(pool, ("vn", PT))
            for h in range(HEADS):
                if h >= 2:
                    filled(pool, ("dSs", h - 2, 1))
                G.tensor_tensor(vmask[h % 2][:, :, :], spread(scr[8 + PT % 2][:, h, :], 1, [P, DEC_BATCH, P]),
                                spread(own8[:, :], 2, [P, DEC_BATCH, P]), ALU.mult).then_inc(s["vm_ready"], 1)
            for n, f in enumerate(GN):
                if n == 0:
                    filled(pool, ("o", PT))
                pool.wait_ge(s["yhi_ready"], n + 1)
                G.tensor_tensor(mxlo[:, f, :], mixed(f), mxhi[:, f, :].bitcast(F32), ALU.subtract)\
                    .then_inc(s["ylo_ready"], 1)
            for i in range(B_OUT[0][1] + 1, NB):
                cut_lo(i)

        @block.scalar
        def _(act_e):
            V = nc.scalar.activation
            e = act_e
            chain = [0]

            def link(ins):
                chain[0] += 1
                ins.then_inc(s["act_chain"], 1)
                e.wait_ge(s["act_chain"], chain[0])

            def cut_hi(i):
                e.wait_ge(w_loaded[i % 2], 16 * (i // 2 + 1))
                if i >= 2:
                    passed(e, i - 2)
                V(wv(whi, i), wv(wraw, i), ACT.Copy).then_inc(s["w_hi_ready"], 1)

            def rstd(col, n=1, width=D_MODEL):
                link(V(stat[:, 1, col:col + n], stat[:, 0, col:col + n], ACT.Ln, bias=epsc[:, :], scale=1.0 / width))
                V(stat[:, 2, col:col + n], stat[:, 1, col:col + n], ACT.Exp, scale=-0.5).then_inc(s["rstd_ready"], 1)

            def hi_part(kind, n, dst):
                for g in range(2):
                    b = filled(e, (kind, n, g))
                    V(dst[:, 4 * g:4 * g + 4], quad(b), ACT.Copy).then_inc(s["h_hi_ready"], 1)

            LN_EXP = "natural_log_exp_and_others"
            e.preload_act_table_set(LN_EXP)
            e.wait_ge(s["eps_ready"], 1)

            def square1(n):
                e.wait_ge(s[f"x_loaded{n % XIN}"], 16 * (n // XIN + 1))
                link(V(junk[:, :], xin[n % XIN][:, :], ACT.Square, accum_out=stat[:, 0, n:n + 1]))
                rstd(n)

            def hi1(n):
                hi_part("norm1", n, dest1(n, mhi, hhi))

            square1(0)
            square1(1)
            hi1(0)
            cut_hi(0)
            hi1(1)
            square1(2)
            cut_hi(1)
            square1(3)
            hi1(2)
            square1(4)
            cut_hi(2)
            for t in range(2):
                b = filled(e, ("mk", 0, t))
                for h in range(HEADS):
                    ins = V(junk_mk[:, h, :], bank[b][:, h * P:(h + 1) * P], ACT.Square,
                            accum_out=stat[:, 0, 17 + 4 * t + h:18 + 4 * t + h])
                link(ins)
                rstd(17 + 4 * t, HEADS, DK)
            hi1(3)
            cut_hi(3)
            square1(5)
            hi1(4)
            square1(6)
            e.wait_ge(s["small_loaded"], 16 * SMALL_LOADS)
            V(w8hi[:, :, :], w8raw[:, :, :], ACT.Copy).then_inc(s["w8_ready"], 1)
            cut_hi(4)
            for t in range(2):
                b = filled(e, ("mv", 0, t))
                V(memv[:, t, :], bank[b][:, :], ACT.Copy).then_inc(bank_free[b], 1)
            hi1(5)
            hi1(6)
            cut_hi(5)
            for t in range(2):
                b = filled(e, ("memkT", t))
                V(memkT[:, :, t * P:(t + 1) * P], quad(b), ACT.Copy).then_inc(bank_free[b], 1)

            def gate(ct):
                e.wait_ge(s["conv_done"], ct + 3)
                V(cb[ct % 2][:, PAD:PAD + TOK], qkvz[:, ct, :], ACT.Sigmoid).then_inc(s["sig_ready"], 1)

            def to_conv(ct, keys):
                t = cb[ct % 2]
                A0, B0 = filled(e, keys[0]), None
                V(t[:, PAD:PAD + HALF], bank[A0][:, 0:HALF], ACT.Copy).then_inc(bank_free[A0], 1)
                B0 = filled(e, keys[1])
                V(t[:, PAD + HALF:PAD + SEQ], bank[B0][:, 0:SEQ - HALF], ACT.Copy)
                V(conv_s(t)[:, :, PAD:], bank[B0][:, SEQ - HALF:HALF].rearrange("p (b t) -> p b t", b=DEC_BATCH),
                  ACT.Copy).then_inc(bank_free[B0], 1)

            def l2(c):
                for h in range(2):
                    b = filled(e, ("l2", c, h))
                    if c >= 2 and h == 0:
                        e.wait_ge(s["l2_done"], c - 1)
                    ins = V(rA[c % 2][:, h * HALF:(h + 1) * HALF], bank[b][:, 0:HALF], ACT.Ln, bias=epsc[:, :])
                    ins.then_inc(bank_free[b], 1)
                evacuated(e, ("l2", c, 1))
                V(rA[c % 2][:, :], rA[c % 2][:, :], ACT.Exp, scale=-0.5).then_inc(s["rinv_ready"], 1)

            scale = SB_DH ** -0.5

            def sb_in(n):
                kind, x, i = SB_ITEMS[n]
                if kind == "s":
                    for b2 in range(2):
                        bt = 2 * x + b2
                        for hp in range(2):
                            if hp == 0 and b2 == 0 and x > 0:
                                filled(e, ("z", n - 1, 1))
                            b = filled(e, ("kc", bt, hp))
                            V(kTs[b2][:, hp, :], bank[b][:, :], ACT.Copy).then_inc(bank_free[b], 1)
                w = (i + 1) * P if kind == "p" else 640
                if n >= 2:
                    filled(e, ("AT", n - 2, at_banks(n - 2) - 1))
                for g, (c0, c1) in enumerate(((640 - w, 640),) if kind == "p" else ((0, 512), (512, 640))):
                    b = filled(e, ("z", n, g))
                    z = bank[b][:, 0:c1 - c0]
                    V(att_a[n % 2][:, c0:c1], z, ACT.Sigmoid, scale=scale)
                    V(att_m[n % 2][:, c0:c1], z, ACT.Sigmoid, scale=-scale).then_inc(bank_free[b], 1)

            def sb_turned(n):
                if n >= 2:
                    passed(e, ("av", n - 2))
                nb = SB_ITEMS[n][2] + 1 if SB_ITEMS[n][0] == "p" else 5
                for g in range(at_banks(n)):
                    b = filled(e, ("AT", n, g))
                    w = min(4, nb - 4 * g) * P
                    V(att_t[n % 2][:, 512 * g:512 * g + w], bank[b][:, 0:w], ACT.Copy).then_inc(bank_free[b], 1)

            def to_sbuf(dst, keys):
                for h in range(2):
                    b = filled(e, keys[h])
                    V(dst[:, h * HALF:(h + 1) * HALF], bank[b][:, 0:HALF], ACT.Copy).then_inc(bank_free[b], 1)

            for c in range(2):
                to_sbuf(cq[:, c, :], [(("cq", 0), c, h) for h in range(2)])
            cut_hi(B_CK[1])
            cut_hi(B_SB)
            for t in range(NT):
                b = filled(e, ("ck", 0, t))
                V(ckv[:, t, :], bank[b][:, :], ACT.Copy).then_inc(bank_free[b], 1)
            cut_hi(B_SC)
            for c in range(2):
                to_sbuf(yb[:, c, :], [("sB", c, h) for h in range(2)])
            for hp in range(2):
                for g, (c0, w) in enumerate(((0, SEQ), (SEQ, P))):
                    b = filled(e, ("kT", hp, g))
                    V(kT[:, hp, c0:c0 + w], bank[b][:, 0:w], ACT.Copy).then_inc(bank_free[b], 1)

            def to_yc(hp):
                b = filled(e, ("oc", hp))
                V(yc[:, hp, 0:SEQ], bank[b][:, :], ACT.Copy).then_inc(bank_free[b], 1)

            for n, (name, i, c) in enumerate(WOVEN):
                if c == 0:
                    cut_hi(i + 1)
                keys = [(name, c, h) for h in range(2)]
                ct = n - 4
                if name == "sC":
                    e.wait_ge(s["out_mk"], 16)
                    to_sbuf(scC[:, c, :], keys)
                elif name != "sx":
                    if ct < 2:
                        e.wait_ge(s["conv_done"], ct + 1)
                    else:
                        e.wait_ge(s["silu_done"], ct - 1)
                    to_conv(ct, keys)
                if n >= 1:
                    sb_turned(n - 1)
                if n == 9:
                    e.wait_ge(s["conv_done"], 2)
                    to_yc(0)
                sb_in(n)
                if ct >= 1:
                    gate(ct - 1)
            for j in range(4):
                if j == 0:
                    cut_hi(B_Z[1])
                if j == 2:
                    cut_hi(B_OUT[0][0])
                to_sbuf(qkvz[:, 12 + j, :], [(("z", j // 2), j % 2, h) for h in range(2)])
                if j == 0:
                    sb_turned(N_P - 1)
                    gate(11)
                elif j == 1:
                    to_yc(1)
                    e.preload_act_table_set(LN_EXP)
                else:
                    l2(2 * j - 4)
                    l2(2 * j - 3)
                if j == 2:
                    evacuated(e, ("gates", 2))
                    e.wait_ge(s["gates_act"], 1)
                    V(gtmp[:, 0], gba[:, :, 0:4], ACT.Exp, scale=-1.0)
                    link(V(gtmp[:, 1], gtmp[:, 3], ACT.Abs))
                    link(V(gtmp[:, 1], gtmp[:, 1], ACT.Exp, scale=-1.0))
                    V(gtmp[:, 1], gtmp[:, 1], ACT.Ln, bias=ones[:, 0:1])
                    V(nA[:, :], nA[:, :], ACT.Exp).then_inc(s["gates_act"], 1)
            for c in range(4, 8):
                l2(c)
            cut_hi(B_OUT[0][1])
            for j in range(4):
                V(qkvz[:, 12 + j, :], qkvz[:, 12 + j, :], ACT.Silu)

            e.wait_ge(s["l2_done"], 8)
            sb_in(N_P)
            for n in range(N_P, NI):
                if n + 1 < NI:
                    sb_in(n + 1)
                sb_turned(n)
            b = filled(e, ("oc", 2))
            for h2 in range(2):
                r = slice(64 * h2, 64 * h2 + 64)
                for hp in range(2):
                    src = bank[b][r, 256 * hp:256 * hp + 256].rearrange("p (b q t) -> p b q t", b=DEC_BATCH, q=2)[:, :, h2, :]
                    ins = V(yc[r, hp, SEQ:TOK].rearrange("p (b t) -> p b t", b=DEC_BATCH), src, ACT.Copy)
            ins.then_inc(bank_free[b], 1)

            e.preload_act_table_set(LN_EXP)
            for i in range(NT):
                e.wait_ge(s["dif_ready"], 2 * i + 1)
                V(kdec[:, i, :], gcs[:, i, 2, :], ACT.Exp)
                V(bege[:, i, :], gcs[:, i, 0, :], ACT.Exp).then_inc(s["small_exp"], 1)
                e.wait_ge(s["dif_ready"], 2 * i + 2)
                V(scr[4 + i % 2][:, :, :], scr[4 + i % 2][:, :, :], ACT.Exp).then_inc(s["dt_ready"], 1)
                if i >= 2:
                    e.wait_ge(s["lt_ready"], i - 1)
                b = filled(e, ("grow", i))
                V(scr[6 + i % 2][:, :, :], quad(b), ACT.Exp).then_inc(bank_free[b], 1)

            def to_x(l, i):
                b = filled(e, ("X", l, i))
                V(XY[:, i, :, :], quad(b), ACT.Copy).then_inc(bank_free[b], 1)

            for i in range(NT):
                to_x(0, i)
            for l in range(1, LEVELS):
                for i in TILES_AT[l]:
                    b = filled(e, ("Y", l, i))
                    V(XY[:, i, :, :], quad(b), ACT.Copy).then_inc(bank_free[b], 1)
                if l < LEVELS - 1:
                    for i in TILES_AT[l + 1]:
                        to_x(l, i)
            def w_part(i):
                b = filled(e, ("wT", i))
                V((smp_w if i == PT else scr[6 + i % 2])[:, :, :], quad(b), ACT.Copy, scale=-1.0).then_inc(bank_free[b], 1)

            def vn_part(i):
                b = filled(e, ("vn", i))
                V(scr[8 + i % 2][:, :, :], quad(b), ACT.Copy).then_inc(bank_free[b], 1)

            def o_part(i):
                b = filled(e, ("o", i))
                V(qkvz[:, 0:HEADS, i * P:(i + 1) * P], quad(b), ACT.Copy).then_inc(bank_free[b], 1)

            def group_rms(n):
                if n >= 2:
                    e.wait_ge(s["y_ready"], n - 1)
                for h in range(2):
                    b = filled(e, ("gn", n, h))
                    V(rG[n % 2][:, h * HALF:(h + 1) * HALF], bank[b][:, 0:HALF], ACT.Ln, bias=epsc[:, :],
                      scale=1.0 / (DK if GN[n] < 4 else SB_DH)).then_inc(bank_free[b], 1)
                evacuated(e, ("gn", n, 1))
                V(rG[n % 2][:, :], rG[n % 2][:, :], ACT.Exp, scale=-0.5).then_inc(s["rf_ready"], 1)

            def y_hi(n):
                e.wait_ge(s["y_ready"], n + 1)
                V(mxhi[:, GN[n], :], mixed(GN[n]), ACT.Copy).then_inc(s["yhi_ready"], 1)

            w_part(PT)
            w_part(0)
            for i in range(PT):
                vn_part(i)
                if i + 1 < PT:
                    w_part(i + 1)
                o_part(i)
                group_rms(i)
            b = filled(e, ("ws", 0))
            V(smp_ws[:, :, :], quad(b), ACT.Copy).then_inc(bank_free[b], 1)
            y_hi(0)
            vn_part(PT)
            b = filled(e, ("qs", 0))
            V(smp_w[:, :, :], quad(b), ACT.Copy).then_inc(bank_free[b], 1)
            y_hi(1)
            for n in range(4, 8):
                if n < 6:
                    y_hi(n - 2)
                group_rms(n)
                if n >= 5:
                    y_hi(n - 1)
            y_hi(7)

            def square_rows(n, base, name, junk):
                for half in range(2):
                    evacuated(e, (name, half, n))
                link(V(junk[:, :], xres[:, n, :], ACT.Square, accum_out=stat[:, 0, base + n:base + n + 1]))
                rstd(base + n)

            def norm_hi(kind, n):
                hi_part(kind, n, hhi[:, :, n * P:(n + 1) * P])

            cut_hi(20)
            cut_hi(21)
            for n in range(NT):
                square_rows(n, 7, "out", junk2)
                if n >= 1:
                    norm_hi("norm2", n - 1)
            norm_hi("norm2", PT)
            cut_hi(22)
            cut_hi(23)
            for n in range(2):
                for c in range(2):
                    for h in range(2):
                        b = filled(e, (("mq", n), c, h))
                        V(qm[:, 2 * n + c, h * HALF:(h + 1) * HALF], bank[b][:, 0:HALF], ACT.Copy)\
                            .then_inc(bank_free[b], 1)
            for h in range(HEADS):
                if h >= 2:
                    e.wait_ge(s["qm_ready"], h - 1)
                for g in range(2):
                    b = filled(e, ("mqn", h, g))
                    V(rM[h % 2][:, g * HALF:(g + 1) * HALF], bank[b][:, 0:HALF], ACT.Ln, bias=epsc[:, :], scale=1.0 / DK)\
                        .then_inc(bank_free[b], 1)
                evacuated(e, ("mqn", h, 1))
                V(rM[h % 2][:, :], rM[h % 2][:, :], ACT.Exp, scale=-0.5).then_inc(s["qr_ready"], 1)
            cut_hi(24)
            cut_hi(25)

            mscale = DK ** -0.5

            def soft(i):
                e.wait_ge(s["max_ready"], i + 1)
                if i >= 2:
                    filled(e, ("pT", i - 2, 1))
                for h in range(HEADS):
                    b = filled(e, ("ms", i, h // 2)) if h % 2 == 0 else b
                    ins = V(probs[i % 2][:, h, :], bank[b][:, (h % 2) * N_MEM:(h % 2 + 1) * N_MEM], ACT.Exp,
                            bias=mstat[:, 1, i, h:h + 1], scale=mscale, accum_out=mstat[:, 2, i, h:h + 1])
                    if h % 2:
                        ins.then_inc(bank_free[b], 1)

            def prob_turned(i):
                if i >= 2:
                    filled(e, ("om", i - 2))
                for g in range(2):
                    b = filled(e, ("pT", i, g))
                    V(probT[i % 2][:, 2 * g:2 * g + 2, :, :].rearrange("p h n t -> p (h n t)"), bank[b][:, :], ACT.Copy)\
                        .then_inc(bank_free[b], 1)

            def om_part(i):
                b = filled(e, ("om", i))
                V(omhi[:, :, i * P:(i + 1) * P], quad(b), ACT.Copy).then_inc(s["om_hi"], 1)

            def sample_keys(bt):
                if bt >= 2:
                    passed(e, ("sT", bt - 2))
                b = filled(e, ("km", bt, 0))
                V(kmT[bt % 2][:, :, 0:P], quad(b), ACT.Copy).then_inc(bank_free[b], 1)

            soft(0)
            for i in range(PT):
                if i + 1 < PT:
                    soft(i + 1)
                sample_keys(2 * i)
                prob_turned(i)
                sample_keys(2 * i + 1)
                if i >= 1:
                    om_part(i - 1)
            om_part(PT - 1)
            b = filled(e, ("sT", 0))
            V(stsb[:, 0, :, :], quad(b), ACT.Copy).then_inc(bank_free[b], 1)
            soft(PT)
            square_rows(0, 12, "mo", junk3)
            prob_turned(PT)
            square_rows(1, 12, "mo", junk3)
            om_part(PT)
            norm_hi("norm3", 0)
            norm_hi("norm3", 1)
            square_rows(2, 12, "mo", junk3)
            square_rows(3, 12, "mo", junk3)
            norm_hi("norm3", 2)
            square_rows(4, 12, "mo", junk3)
            cut_hi(26)
            norm_hi("norm3", 3)
            norm_hi("norm3", 4)
            cut_hi(27)

            for j in range(FT // 2):
                for c in range(2):
                    ct = 2 * j + c
                    if ct >= 2:
                        e.wait_ge(s["ffn_conv"], ct - 1)
                    to_conv(ct, [(("gate", j), c, h) for h in range(2)])
                cut_hi(28 + 2 * j)
                for c in range(2):
                    ct = 2 * j + c
                    e.wait_ge(s["ffn_conv"], ct + 1)
                    V(act[:, ct, :], act[:, ct, :], ACT.Silu).then_inc(s["ffn_silu"], 1)
                cut_hi(29 + 2 * j)
            nxt = B_DN[0][0] + 2
            for n in range(2 * FT):
                half, k = divmod(n, FT)
                if n >= KD:
                    passed(e, ("dn",) + divmod(n - KD, FT))
                else:
                    filled(e, (("up", FT // 2 - 1), 1, 1))
                evacuated(e, (("up", k // 2), k % 2, 0))
                evacuated(e, (("up", k // 2), k % 2, 1))
                V(hhi[:, n % KD, :], act[:, k, :], ACT.Copy).then_inc(s["ahi_ready"], 1)
                if n % 4 == 3 and n >= KD and nxt < NB:
                    cut_hi(nxt)
                    nxt += 1
            while nxt < NB:
                cut_hi(nxt)
                nxt += 1

        @block.vector
        def _(dve):
            V = nc.vector
            chain = [0]

            def link(ins):
                chain[0] += 1
                ins.then_inc(s["dve_chain"], 1)
                dve.wait_ge(s["dve_chain"], chain[0])

            for t in cb:
                V.memset(t[:, 0:PAD], 0.0)
            def lo_part(kind, n, hi, lo):
                for g in range(2):
                    lo_part.count += 1
                    dve.wait_ge(s["h_hi_ready"], lo_part.count)
                    b, _ = use[(kind, n, g)]
                    V.tensor_tensor(lo[:, 4 * g:4 * g + 4], quad(b), hi[:, 4 * g:4 * g + 4].bitcast(F32), ALU.subtract)\
                        .then_inc(bank_free[b], 1)
            lo_part.count = 0
            def scaled1(n):
                dve.wait_ge(s["gmin_loaded" if n < 2 else "gmix_loaded"], 16)
                dve.wait_ge(s["rstd_ready"], n + 1 if n < 5 else n + 3)
                if n >= 2:
                    filled(dve, ("norm1", n - 2, 1))
                V.scalar_tensor_tensor(out=xn[n % 2][:, :], in0=xin[n % XIN][:, :], scalar=stat[:, 2, n:n + 1],
                                       in1=(gmin if n < 2 else gmix)[:, :], op0=ALU.mult, op1=ALU.mult)\
                    .then_inc(s["xn_ready"], 1)

            def lo1(n):
                lo_part("norm1", n, dest1(n, mhi, hhi), dest1(n, mlo, hlo))

            scaled1(0)
            scaled1(1)
            lo1(0)
            scaled1(2)
            lo1(1)
            scaled1(3)
            lo1(2)
            scaled1(4)
            dve.wait_ge(s["small_loaded"], 16 * SMALL_LOADS)
            for t in range(2):
                dve.wait_ge(s["rstd_ready"], 6 + t)
                b = filled(dve, ("mk", 0, t))
                for h in range(HEADS):
                    ins = V.scalar_tensor_tensor(out=mkout[:, t, h * P:(h + 1) * P], in0=bank[b][:, h * P:(h + 1) * P],
                                                 scalar=stat[:, 2, 17 + 4 * t + h:18 + 4 * t + h], in1=gmk[:, :],
                                                 op0=ALU.mult, op1=ALU.mult)
                ins.then_inc(bank_free[b], 1)
            lo1(3)
            scaled1(5)
            lo1(4)
            scaled1(6)
            lo1(5)
            lo1(6)
            b = filled(dve, ("cache", 0))
            V.tensor_copy(flat(cacheT), bank[b][:, 0:288])
            V.tensor_copy(flat(cacheS), bank[b][:, 288:320]).then_inc(bank_free[b], 1)
            for h in range(2):
                b = filled(dve, ("gates", h))
                V.tensor_copy(gT[:, h * HALF:(h + 1) * HALF], bank[b][0:8, 0:HALF]).then_inc(bank_free[b], 1)
            filled(dve, ("mv", 0, 1))
            link(V.memset(qbl[:, :, :, :], 0.0))
            for t in att_m:
                V.memset(t[:, 640:641], 1.0)
            for c in range(2):
                for h in range(2):
                    evacuated(dve, (("cq", 0), c, h))
            for h2 in range(2):
                r = slice(64 * h2, 64 * h2 + 64)
                ins = V.tensor_copy(qbl[r, :, :, 16 * h2:16 * h2 + 16],
                                    cq[r, :, SEQ:TOK].rearrange("p a (b t) -> p a b t", b=DEC_BATCH))
            ins.then_inc(s["q_blocks"], 1)
            b = filled(dve, ("gates", 2))
            V.tensor_copy(flat(gba), bank[b][:, 0:8 * NT]).then_inc(bank_free[b], 1)

            def conv(t, out, w, taps, state, npads):
                first = PAD + 1 - taps
                ts, os = conv_s(t), out[:, SEQ:TOK].rearrange("p (b t) -> p b t", b=DEC_BATCH)
                keep_n = taps - 1
                V.tensor_copy(state[:, 0:keep_n], t[:, PAD + SEQ - keep_n:PAD + SEQ])
                V.tensor_copy(state[:, keep_n:].rearrange("p (b t) -> p b t", b=DEC_BATCH),
                              ts[:, :, PAD + DEC_SEQ - keep_n:])
                for k in range(taps):
                    a, bb = t[:, first + k:first + k + SEQ], ts[:, :, first + k:first + k + DEC_SEQ]
                    if k == 0:
                        V.tensor_scalar(out[:, 0:SEQ], a, w[:, 0:1], None, ALU.mult)
                        ins = V.tensor_scalar(os, bb, w[:, 0:1], None, ALU.mult)
                    else:
                        V.scalar_tensor_tensor(out=out[:, 0:SEQ], in0=a, scalar=w[:, k:k + 1], in1=out[:, 0:SEQ],
                                               op0=ALU.mult, op1=ALU.add)
                        ins = V.scalar_tensor_tensor(out=os, in0=bb, scalar=w[:, k:k + 1], in1=os,
                                                     op0=ALU.mult, op1=ALU.add)
                    if k < taps - 1:
                        link(ins)
                return ins

            def pads(t, cache, n):
                link(V.tensor_copy(conv_s(t)[:, :, PAD - n:PAD], cache.rearrange("p (b t) -> p b t", b=DEC_BATCH)))

            def gdn_conv(ct):
                t = cb[ct % 2]
                if ct >= 2:
                    dve.wait_ge(s["silu_done"], ct - 1)
                pads(t, cacheT[:, ct, :], 3)
                for h in range(2):
                    evacuated(dve, (("qkv", ct // 2), ct % 2, h))
                conv(t, qkvz[:, ct, :], gcw[:, ct, :], 4, cst[:, ct, :], 3).then_inc(s["conv_done"], 1)

            def silu(ct):
                dve.wait_ge(s["sig_ready"], ct + 1)
                V.tensor_tensor(qkvz[:, ct, :], qkvz[:, ct, :], cb[ct % 2][:, PAD:PAD + TOK], ALU.mult)\
                    .then_inc(s["silu_done"], 1)

            def square(c):
                if c < 2:
                    passed(dve, ("av", N_P - 1))
                    dve.wait_ge(s["silu_done"], c + 1)
                if c >= 2:
                    filled(dve, ("l2", c - 2, 1))
                V.tensor_tensor(sqA[c % 2][:, :], qkvz[:, c, :], qkvz[:, c, :], ALU.mult).then_inc(s["sq_ready"], 1)

            def unit(c):
                dve.wait_ge(s["rinv_ready"], c + 1)
                V.scalar_tensor_tensor(out=qkvz[:, c, :], in0=qkvz[:, c, :], scalar=DK ** -0.5 if c < 4 else 1.0,
                                       in1=rA[c % 2][:, :], op0=ALU.mult, op1=ALU.mult).then_inc(s["l2_done"], 1)

            def short_conv(c):
                keys = [("sx", c, h) for h in range(2)]
                t = cb[c]
                pads(t, cacheS[:, c, :], 2)
                for h in range(2):
                    evacuated(dve, ("sC", c, h))
                    evacuated(dve, ("sB", c, h))
                b = filled(dve, keys[0])
                V.tensor_tensor(t[:, PAD:PAD + HALF], bank[b][:, 0:HALF], scC[:, c, 0:HALF], ALU.mult)\
                    .then_inc(bank_free[b], 1)
                b = filled(dve, keys[1])
                V.tensor_tensor(t[:, PAD + HALF:PAD + SEQ], bank[b][:, 0:SEQ - HALF], scC[:, c, HALF:SEQ], ALU.mult)
                V.tensor_tensor(conv_s(t)[:, :, PAD:], bank[b][:, SEQ - HALF:HALF].rearrange("p (b t) -> p b t", b=DEC_BATCH),
                                scC[:, c, SEQ:TOK].rearrange("p (b t) -> p b t", b=DEC_BATCH), ALU.mult)\
                    .then_inc(bank_free[b], 1)
                evacuated(dve, keys[0])
                evacuated(dve, keys[1])
                link(conv(t, scC[:, c, :], scw[:, c, :], 3, scst[:, c, :], 2))
                V.tensor_tensor(yb[:, c, :], yb[:, c, :], scC[:, c, :], ALU.mult).then_inc(s["conv_done"], 1)
            def weights(n):
                kind, x, i = SB_ITEMS[n]
                w = (i + 1) * P if kind == "p" else 640
                for g in range(1 if kind == "p" else 2):
                    evacuated(dve, ("z", n, g))
                a, m = att_a[n % 2], att_m[n % 2]
                if kind == "s":
                    c = 96 - 32 * x
                    V.tensor_tensor(a[:, 512:640], a[:, 512:640], newm[:, c:c + P], ALU.mult)
                    link(V.tensor_tensor(m[:, 512:640], m[:, 512:640], newi[:, c:c + P], ALU.max))
                mr = m[:, 640 - w:640][:, ::-1]
                link(V.tensor_tensor_scan(mr, mr, ones[:, 0:1].to_broadcast([P, w]), 1.0, ALU.mult, ALU.mult))
                V.tensor_tensor(a[:, 640 - w:640], a[:, 640 - w:640], m[:, 641 - w:641], ALU.mult)\
                    .then_inc(s["A_ready"], 1)

            def strow_part():
                for g in range(3):
                    b = filled(dve, ("strow", g))
                    V.tensor_copy(strow[:, g * 512:(g + 1) * 512], bank[b][0:27, :]).then_inc(bank_free[b], 1)
                b = filled(dve, ("strow", 3))
                V.tensor_copy(scsrow[:, :], bank[b][0:18, 0:SC_DIM]).then_inc(bank_free[b], 1)

            def beta_decay():
                evacuated(dve, ("gates", 2))
                V.tensor_tensor(gtmp[:, 3], gba[:, :, 4:8], spread(dtb[:, :], 1, [P, NT, HEADS]), ALU.add)\
                    .then_inc(s["gates_act"], 1)
                dve.wait_ge(s["gates_act"], 2)
                link(V.tensor_scalar(gtmp[:, 0], gtmp[:, 0], 1.0, None, ALU.add))
                V.reciprocal(beta[:, :, :], gtmp[:, 0])
                link(V.tensor_scalar(gtmp[:, 2], gtmp[:, 3], 0.0, None, ALU.max))
                link(V.tensor_tensor(gtmp[:, 2], gtmp[:, 2], gtmp[:, 1], ALU.add))
                V.scalar_tensor_tensor(out=gdec[:, :, :], in0=gtmp[:, 2], scalar=-1.0,
                                       in1=spread(nA[:, :], 1, [P, NT, HEADS]), op0=ALU.mult, op1=ALU.mult)\
                    .then_inc(s["gates"], 1)

            for n, (name, i, c) in enumerate(WOVEN):
                ct = n - 4
                if name == "sx":
                    short_conv(c)
                elif ct >= 0:
                    gdn_conv(ct)
                weights(n)
                if ct >= 1:
                    silu(ct - 1)
            silu(11)
            square(0)
            square(1)
            for c in range(8):
                unit(c)
                if c + 2 < 8:
                    square(c + 2)
                if c == 1:
                    beta_decay()
                if c == 3:
                    strow_part()
            dve.wait_ge(s["l2_done"], 8)
            for t in att_m:
                ins = V.memset(t[:, 640:641], 1.0)
            link(ins)
            for n in range(N_P, NI):
                weights(n)

            passed(dve, ("av", NI - 1))
            for i in range(NT):
                tt = slice(i * P, (i + 1) * P)
                b = filled(dve, ("gcol", i))
                V.tensor_copy(gcs[:, i, 0:2, :].rearrange("p a h -> p (a h)"), bank[b][:, 0:8]).then_inc(bank_free[b], 1)
                evacuated(dve, ("gcol", i))
                V.tensor_tensor(gcs[:, i, 2, :], gcs[:, i, 1, :], gcs[:, i, 0, :], ALU.subtract).then_inc(s["dif_ready"], 1)
                b = filled(dve, ("grow", i))
                if i >= 2:
                    dve.wait_ge(s["dtu_ready"], i - 1)
                for h in range(HEADS):
                    ins = V.tensor_scalar(scr[4 + i % 2][:, h, :], bank[b][:, h * P:(h + 1) * P], gcs[:, i, 0, h:h + 1], 0.0,
                                          ALU.subtract, ALU.min)
                ins.then_inc(s["dif_ready"], 1)
                dve.wait_ge(s["small_exp"], i + 1)
                V.tensor_tensor(bege[:, i, :], bege[:, i, :], beta[:, i, :], ALU.mult)
                dve.wait_ge(s["dtu_ready"], i + 1)
                d = scr[8 + i % 2][:, :, :]
                b = filled(dve, ("qk", i))
                V.tensor_tensor(qkD[:, i, :, :], quad(b), d, ALU.mult).then_inc(bank_free[b], 1)
                b = filled(dve, ("kk", i))
                V.tensor_tensor(LT[:, i, :, :], quad(b), d, ALU.mult).then_inc(bank_free[b], 1)
                evacuated(dve, ("kk", i))
                b = filled(dve, ("brow", i))
                V.tensor_tensor(LT[:, i, :, :], LT[:, i, :, :], quad(b), ALU.mult).then_inc(bank_free[b], 1)
                evacuated(dve, ("grow", i))
                er = scr[6 + i % 2]
                if i < PT:
                    V.tensor_copy(etot[:, i, :], er[:, :, P - 1])
                else:
                    V.tensor_copy(etotS[:, :, :], er[:, :, :].rearrange("p h (b t) -> p h b t", b=DEC_BATCH)[:, :, :, DEC_SEQ - 1])
                V.tensor_tensor(qkvz[:, 0:HEADS, tt], qkvz[:, 0:HEADS, tt], er[:, :, :], ALU.mult).then_inc(s["lt_ready"], 1)
            def vk_part(i):
                b = filled(dve, ("Vt", i))
                slots = (smp_v, smp_kb, smp_kd) if i == PT else (scr[i % 2], scr[2 + i % 2], scr[4 + i % 2])
                if 2 <= i < PT:
                    filled(dve, ("dS", i - 2))
                V.tensor_tensor(slots[0][:, :, :], quad(b), spread(beta[:, i, :], 2, [P, HEADS, P]), ALU.mult)\
                    .then_inc(bank_free[b], 1)
                b = filled(dve, ("Kt", i))
                V.tensor_tensor(slots[1][:, :, :], quad(b), spread(bege[:, i, :], 2, [P, HEADS, P]), ALU.mult)\
                    .then_inc(s["kd_ready"], 1)
                V.tensor_tensor(slots[2][:, :, :], quad(b), spread(kdec[:, i, :], 2, [P, HEADS, P]), ALU.mult)\
                    .then_inc(bank_free[b], 1)

            for l in range(1, LEVELS):
                if l == LEVELS - 1:
                    vk_part(PT)
                    vk_part(0)
                for i in TILES_AT[l]:
                    b = filled(dve, ("dX", l, i))
                    V.tensor_tensor(XT[:, i, :, :], XT[:, i, :, :], quad(b), ALU.subtract).then_inc(bank_free[b], 1)

            def group_square(n):
                if n >= 2:
                    filled(dve, ("gn", n - 2, 1))
                V.tensor_tensor(sqG[n % 2][:, :], mixed(GN[n]), mixed(GN[n]), ALU.mult).then_inc(s["sqf_ready"], 1)

            def y_part(n):
                f = GN[n]
                dve.wait_ge(s["rf_ready"], n + 1)
                ins = V.scalar_tensor_tensor(out=mixed(f), in0=mixed(f), scalar=gout[:, 0:1] if f < 4 else gout[:, f:f + 1],
                                             in1=rG[n % 2][:, :], op0=ALU.mult, op1=ALU.mult)
                if f < 4:
                    link(ins)
                    ins = V.tensor_tensor(mixed(f), mixed(f), qkvz[:, 12 + f, :], ALU.mult)
                ins.then_inc(s["y_ready"], 1)

            for g in range(3):
                evacuated(dve, ("oc", g))
            group_square(0)
            group_square(1)
            vk_part(1)
            for i in range(PT):
                b = filled(dve, ("dS", i))
                if i == 0:
                    V.tensor_copy(stP[0][:, :, :], quad(b)).then_inc(bank_free[b], 1)
                else:
                    for h in range(HEADS):
                        ins = V.scalar_tensor_tensor(out=stP[i % 2][:, h, :], in0=stP[(i - 1) % 2][:, h, :], scalar=etot[:, i, h:h + 1],
                                                     in1=bank[b][:, h * P:(h + 1) * P], op0=ALU.mult, op1=ALU.add)
                    ins.then_inc(bank_free[b], 1)
                evacuated(dve, ("dS", i))
                if i + 2 < PT:
                    vk_part(i + 2)
                if i >= 1:
                    y_part(i - 1)
                    if i < 3:
                        group_square(i + 1)
            y_part(3)
            b = filled(dve, ("o", PT))
            evacuated(dve, ("qs", 0))
            V.tensor_tensor(qkvz[:, 0:HEADS, SEQ:TOK], quad(b), smp_w[:, :, :], ALU.add).then_inc(bank_free[b], 1)
            for i in range(NT):
                evacuated(dve, ("o", i))
            group_square(4)
            for h in range(HEADS):
                if h < 3:
                    group_square(5 + h)
                for g in range(2):
                    b = filled(dve, ("dSs", h, g))
                    for j in range(4):
                        bt = 4 * g + j
                        ins = V.scalar_tensor_tensor(out=stS[:, bt, h, :], in0=stS[:, bt, h, :], scalar=etotS[:, h, bt:bt + 1],
                                                     in1=bank[b][:, j * P:(j + 1) * P], op0=ALU.mult, op1=ALU.add)
                    ins.then_inc(bank_free[b], 1)
                y_part(4 + h)

            def add_res(name, half, t):
                b = filled(dve, (name, half, t))
                c = slice(512 * half, 512 * half + 512)
                V.tensor_tensor(xres[:, t, c], xres[:, t, c], bank[b][:, :], ALU.add).then_inc(bank_free[b], 1)

            def scaled_rows(kind, n, base, g, xn):
                evacuated(dve, ({"norm2": "out", "norm3": "mo"}[kind], 1, n))
                dve.wait_ge(s["rstd_ready"], {"norm2": 10, "norm3": 15}[kind] + n)
                if n >= 2:
                    filled(dve, (kind, n - 2, 1))
                V.scalar_tensor_tensor(out=xn[n % 2][:, :], in0=xres[:, n, :], scalar=stat[:, 2, base + n:base + n + 1],
                                       in1=g[:, :], op0=ALU.mult, op1=ALU.mult).then_inc(s["xn_ready"], 1)

            def norm_lo(kind, n):
                c = slice(n * P, (n + 1) * P)
                lo_part(kind, n, hhi[:, :, c], hlo[:, :, c])

            dve.wait_ge(s["xres_loaded"], 32)
            for n in range(NT):
                add_res("out", 0, n)
            dve.wait_ge(s["gm_loaded"], 16)
            for n in range(NT):
                add_res("out", 1, n)
                scaled_rows("norm2", n, 7, gmem, xn2)
                if n >= 1:
                    norm_lo("norm2", n - 1)
            norm_lo("norm2", PT)

            def q_square(h):
                for g in range(2):
                    evacuated(dve, (("mq", h // 2), h % 2, g))
                if h >= 2:
                    filled(dve, ("mqn", h - 2, 1))
                V.tensor_tensor(sqM[h % 2][:, :], qm[:, h, :], qm[:, h, :], ALU.mult).then_inc(s["qsq_ready"], 1)
            q_square(0)
            q_square(1)
            for h in range(HEADS):
                dve.wait_ge(s["qr_ready"], h + 1)
                V.scalar_tensor_tensor(out=qm[:, h, :], in0=qm[:, h, :], scalar=gmq[:, :], in1=rM[h % 2][:, :],
                                       op0=ALU.mult, op1=ALU.mult).then_inc(s["qm_ready"], 1)
                if h + 2 < HEADS:
                    q_square(h + 2)

            mscale = DK ** -0.5

            def soft_max(i):
                for g in range(2):
                    b = filled(dve, ("ms", i, g))
                    ins = V.tensor_reduce(mstat[:, 0, i, 2 * g:2 * g + 2],
                                          bank[b][:, :].rearrange("p (h n) -> p h n", h=2), AX.X, ALU.max)
                link(ins)
                V.tensor_scalar(mstat[:, 1, i, :], mstat[:, 0, i, :], -mscale, None, ALU.mult).then_inc(s["max_ready"], 1)

            def soft_norm(i):
                for g in range(2):
                    evacuated(dve, ("ms", i, g))
                link(V.reciprocal(mstat[:, 3, i, :], mstat[:, 2, i, :]))
                for h in range(HEADS):
                    ins = V.tensor_scalar(probs[i % 2][:, h, :], probs[i % 2][:, h, :], mstat[:, 3, i, h:h + 1], None, ALU.mult)
                ins.then_inc(s["prob_ready"], 1)

            def om_part(i):
                dve.wait_ge(s["om_hi"], i + 1)
                b, _ = use[("om", i)]
                c = slice(i * P, (i + 1) * P)
                V.tensor_tensor(omlo[:, :, c], quad(b), omhi[:, :, c].bitcast(F32), ALU.subtract).then_inc(bank_free[b], 1)

            def sample_keys(bt):
                if bt >= 2:
                    passed(dve, ("sT", bt - 2))
                b = filled(dve, ("km", bt, 1))
                V.tensor_copy(kmT[bt % 2][:, :, P:N_MEM], quad(b)).then_inc(bank_free[b], 1)

            soft_max(0)
            soft_norm(0)
            for i in range(PT):
                if i + 1 < PT:
                    soft_max(i + 1)
                sample_keys(2 * i)
                if i + 1 < PT:
                    soft_norm(i + 1)
                sample_keys(2 * i + 1)
                if i >= 1:
                    om_part(i - 1)
            om_part(PT - 1)
            b = filled(dve, ("sT", 1))
            V.tensor_copy(stsb[:, 1, :, :], quad(b)).then_inc(bank_free[b], 1)
            soft_max(PT)
            soft_norm(PT)

            def add_mem(n):
                add_res("mo", 0, n)
                add_res("mo", 1, n)

            dve.wait_ge(s["gm_loaded"], 32)
            add_mem(0)
            scaled_rows("norm3", 0, 12, gffn, xn3)
            add_mem(1)
            scaled_rows("norm3", 1, 12, gffn, xn3)
            add_mem(2)
            om_part(PT)
            norm_lo("norm3", 0)
            norm_lo("norm3", 1)
            scaled_rows("norm3", 2, 12, gffn, xn3)
            add_mem(3)
            scaled_rows("norm3", 3, 12, gffn, xn3)
            norm_lo("norm3", 2)
            add_mem(4)
            scaled_rows("norm3", 4, 12, gffn, xn3)
            for t in cb:
                ins = V.memset(t[:, 0:PAD], 0.0)
            link(ins)
            norm_lo("norm3", 3)
            norm_lo("norm3", 4)
            dve.wait_ge(s["f_loaded"], 64)
            b = filled(dve, ("cacheF", 0))
            V.tensor_copy(flat(cacheF), bank[b][:, 0:16 * FT]).then_inc(bank_free[b], 1)
            evacuated(dve, ("cacheF", 0))
            for j in range(FT // 2):
                for c in range(2):
                    ct = 2 * j + c
                    t = cb[ct % 2]
                    pads(t, cacheF[:, ct, :], 2)
                    for h in range(2):
                        evacuated(dve, (("gate", j), c, h))
                    conv(t, act[:, ct, :], fcw[:, ct, :], 3, fcst[:, ct, :], 2).then_inc(s["ffn_conv"], 1)
                for c in range(2):
                    ct = 2 * j + c
                    dve.wait_ge(s["ffn_silu"], ct + 1)
                    for h in range(2):
                        b = filled(dve, (("up", j), c, h))
                        hs = slice(h * HALF, (h + 1) * HALF)
                        V.tensor_tensor(act[:, ct, hs], act[:, ct, hs], bank[b][:, 0:HALF], ALU.mult).then_inc(bank_free[b], 1)

            def act_lo(n):
                half, k = divmod(n, FT)
                dve.wait_ge(s["ahi_ready"], n + 1)
                V.tensor_tensor(hlo[:, n % KD, :], act[:, k, :], hhi[:, n % KD, :].bitcast(F32), ALU.subtract)\
                    .then_inc(s["alo_ready"], 1)
            for n in range(FT + 4):
                act_lo(n)
            for n in range(NT):
                add_res("dn", 0, n)
            for g in range(6):
                b = filled(dve, ("frow", g))
                w = min(4, FT - 4 * g) * P
                V.tensor_copy(fsrow[:, 512 * g:512 * g + w], bank[b][0:18, 0:w]).then_inc(bank_free[b], 1)
            for n in range(FT + 4, 2 * FT):
                act_lo(n)
            for n in range(NT):
                add_res("dn", 1, n)


_INS = ["x_prompt", "x_sample", "mem_prompt", "state_gdn", "cache_gdn_conv", "cache_sc_conv", "cache_sb_k", "cache_sb_v",
        "cache_mem_k", "cache_mem_v", "cache_ffn_conv", "norm_mix_g", "w_in", "gdn_conv_w", "gdn_A_log", "gdn_dt_bias",
        "gdn_norm_g", "sc_conv_w", "sc_norm_g", "sb_norm_g", "w_mix_out", "norm_mem_g", "mem_in_norm_g", "w_mq", "w_mk",
        "w_mv", "mq_norm_g", "mk_norm_g", "w_mo", "norm_ffn_g", "w_gate", "w_up", "ffn_conv_w", "w_down"]
_SHAPES = {"x_prompt": (512, 1024), "x_sample": (128, 1024), "mem_prompt": (256, 1024), "state_gdn": (8, 4, 128, 128),
           "cache_gdn_conv": (8, 3, 1536), "cache_sc_conv": (8, 2, 256), "cache_sb_k": (8, 512, 256),
           "cache_sb_v": (8, 512, 256), "cache_mem_k": (8, 256, 512), "cache_mem_v": (8, 256, 512),
           "cache_ffn_conv": (8, 2, 2816)}
_OUTS = [("y_prompt", (512, 1024), (1, 512, 1024)), ("y_sample", (128, 1024), (8, 16, 1024)),
         ("p_gdn_state", (4, 128, 128), (1, 1, 4, 128, 128)), ("p_gdn_conv", (3, 1536), (1, 1, 3, 1536)),
         ("p_sc_conv", (2, 256), (1, 1, 2, 256)), ("p_sb_k", (512, 256), (1, 1, 512, 4, 64)),
         ("p_sb_v", (512, 256), (1, 1, 512, 4, 64)), ("p_mem_k", (256, 512), (1, 1, 256, 4, 128)),
         ("p_mem_v", (256, 512), (1, 1, 256, 4, 128)), ("p_ffn_conv", (2, 2816), (1, 1, 2, 2816)),
         ("s_gdn_state", (8, 4, 128, 128), (1, 8, 4, 128, 128)), ("s_gdn_conv", (24, 1536), (1, 8, 3, 1536)),
         ("s_sc_conv", (16, 256), (1, 8, 2, 256)), ("s_sb_k", (128, 256), (1, 8, 16, 4, 64)),
         ("s_sb_v", (128, 256), (1, 8, 16, 4, 64)), ("s_ffn_conv", (16, 2816), (1, 8, 2, 2816))]


def kernel(**inputs):
    import numpy as _np
    import concourse.bacc as _bacc
    from concourse.bass_utils import run_bass_kernel_spmd as _run

    nc = _bacc.Bacc("TRN2", target_bir_lowering=False, num_devices=1)
    arrays, A, O = {}, {}, {}
    for name in _INS:
        a = _np.ascontiguousarray(inputs[name])
        a = a.reshape(_SHAPES.get(name, a.shape[1:]))
        arrays[f"in_{name}"] = a
        A[name] = nc.dram_tensor(f"in_{name}", a.shape, F32, kind="ExternalInput").ap()
    for name, shape, _ in _OUTS:
        O[name] = nc.dram_tensor(f"out_{name}", shape, F32, kind="ExternalOutput").ap()
    hybrid_step(nc, A, O)
    r = _run(nc, [arrays], core_ids=[0])
    return tuple(r.results[0][f"out_{name}"].reshape(shape) for name, _, shape in _OUTS)
```
